# Optimizing a Trainium2 kernel written in Bass

```python
import jax, jax.numpy as jnp
from jax import lax
import numpy as np

D_MODEL = 1024
BATCH = 1
SEQ = 1024
DEPTH = 1

ATTN_HEADS = 8
HEAD_DIM = 64
KV_GROUPS = 2
HEADS_PER_GROUP = ATTN_HEADS // KV_GROUPS
ATTN_DIM = ATTN_HEADS * HEAD_DIM
KV_DIM = KV_GROUPS * HEAD_DIM
N_NSA_BRANCHES = 3
CMP_BLOCK = 32
CMP_STRIDE = 16
CMP_HIDDEN = 2 * HEAD_DIM
SLC_BLOCK = 64
N_SELECT = 16
WINDOW = 512
Q_BLOCK = 64
FORCE_BONUS = 1000.0
RWKV_HEADS = 8
RWKV_HEAD_DIM = 64
RWKV_DIM = RWKV_HEADS * RWKV_HEAD_DIM
W_LORA = 64
A_LORA = 64
G_LORA = 128
RWKV_MIX_DIM = 3 * RWKV_DIM + W_LORA + A_LORA + G_LORA
N_BRANCHES = 2
D_FF = 4 * D_MODEL
NSA_DIM = ATTN_DIM + 6 * KV_DIM + N_NSA_BRANCHES * ATTN_HEADS
PROJ_DIM = NSA_DIM + RWKV_MIX_DIM + N_BRANCHES * D_MODEL
RMS_EPS = 1e-6
GN_EPS = 64e-5
NEG_INF = -1e30

kernel_name = "nsa_rwkv7_gated_hybrid"

def rms_norm(x, gain):
    xf = x.astype(jnp.float32)
    y = xf * lax.rsqrt(jnp.mean(xf * xf, axis=-1, keepdims=True) + RMS_EPS)
    return (y * gain.astype(jnp.float32)).astype(x.dtype)

def masked_softmax(s, mask):
    s = jnp.where(mask, s.astype(jnp.float32), NEG_INF)
    return jax.nn.softmax(s, axis=-1) * mask

def compress_blocks(kv, pos, w1, w2):
    S = kv.shape[2]
    n_cmp = (S - CMP_BLOCK) // CMP_STRIDE + 1
    idx = (jnp.arange(n_cmp) * CMP_STRIDE)[:, None] + jnp.arange(CMP_BLOCK)[None, :]
    blocks = kv[:, :, idx] + pos
    flat = blocks.reshape(blocks.shape[:3] + (CMP_BLOCK * HEAD_DIM,))
    return jax.nn.gelu(flat @ w1) @ w2

def nsa_attention(q, kc, vc, ks, vs, kw, vw, gates, q_gain, k_gain, cmp_pos, cmp_w1, cmp_w2):
    B, S, _ = q.shape
    dt = q.dtype
    scale = HEAD_DIM ** -0.5
    qh = rms_norm(q.reshape(B, S, KV_GROUPS, HEADS_PER_GROUP, HEAD_DIM), q_gain)
    qh = qh.transpose(0, 2, 3, 1, 4)
    heads = lambda t: t.reshape(B, S, KV_GROUPS, HEAD_DIM).transpose(0, 2, 1, 3)
    k_cmp = rms_norm(compress_blocks(heads(kc), cmp_pos[0], cmp_w1[0], cmp_w2[0]), k_gain[0])
    v_cmp = compress_blocks(heads(vc), cmp_pos[1], cmp_w1[1], cmp_w2[1])
    k_slc = rms_norm(heads(ks), k_gain[1])
    v_slc = heads(vs)
    k_win = rms_norm(heads(kw), k_gain[2])
    v_win = heads(vw)

    n_cmp = k_cmp.shape[2]
    n_slc = S // SLC_BLOCK
    k_sel = min(N_SELECT, n_slc)
    cmp_start = jnp.arange(n_cmp) * CMP_STRIDE
    cmp_end = cmp_start + CMP_BLOCK - 1
    slc_start = jnp.arange(n_slc) * SLC_BLOCK
    overlap = ((cmp_start[:, None] <= slc_start[None, :] + SLC_BLOCK - 1)
               & (cmp_end[:, None] >= slc_start[None, :])).astype(jnp.float32)
    k_slc_b = k_slc.reshape(B, KV_GROUPS, n_slc, SLC_BLOCK, HEAD_DIM)
    v_slc_b = v_slc.reshape(B, KV_GROUPS, n_slc, SLC_BLOCK, HEAD_DIM)
    pad = ((0, 0), (0, 0), (WINDOW, 0), (0, 0))
    k_win_p = jnp.pad(k_win, pad)
    v_win_p = jnp.pad(v_win, pad)
    b_ix = jnp.arange(B)[:, None, None, None]
    g_ix = jnp.arange(KV_GROUPS)[None, :, None, None]
    blk_ids = jnp.arange(n_slc)

    def block(qb):
        t0 = qb * Q_BLOCK
        tpos = t0 + jnp.arange(Q_BLOCK)
        qblk = lax.dynamic_slice_in_dim(qh, t0, Q_BLOCK, axis=3)
        cmask = cmp_end[None, :] <= tpos[:, None]
        p_c = masked_softmax(jnp.einsum('bghtd,bgnd->bghtn', qblk, k_cmp) * scale, cmask)
        o_c = jnp.einsum('bghtn,bgnd->bghtd', p_c.astype(dt), v_cmp)
        imp = jnp.einsum('bghtn,nj->bgtj', p_c, overlap)
        cur = tpos // SLC_BLOCK
        forced = ((blk_ids[None, :] == 0) | (blk_ids[None, :] == cur[:, None])
                  | (blk_ids[None, :] == cur[:, None] - 1))
        causal_blk = slc_start[None, :] <= tpos[:, None]
        imp = jnp.where(causal_blk, imp + jnp.where(forced, FORCE_BONUS, 0.0), -1.0)
        _, idx = lax.top_k(imp, k_sel)
        kg = k_slc_b[b_ix, g_ix, idx]
        vg = v_slc_b[b_ix, g_ix, idx]
        tok = idx[..., None] * SLC_BLOCK + jnp.arange(SLC_BLOCK)
        smask = (tok <= tpos[None, None, :, None, None]).reshape(B, KV_GROUPS, 1, Q_BLOCK, k_sel * SLC_BLOCK)
        s_s = jnp.einsum('bghtd,bgtkpd->bghtkp', qblk, kg) * scale
        p_s = masked_softmax(s_s.reshape(B, KV_GROUPS, HEADS_PER_GROUP, Q_BLOCK, k_sel * SLC_BLOCK), smask)
        p_s = p_s.reshape(B, KV_GROUPS, HEADS_PER_GROUP, Q_BLOCK, k_sel, SLC_BLOCK).astype(dt)
        o_s = jnp.einsum('bghtkp,bgtkpd->bghtd', p_s, vg)
        kwin = lax.dynamic_slice_in_dim(k_win_p, t0, Q_BLOCK + WINDOW, axis=2)
        vwin = lax.dynamic_slice_in_dim(v_win_p, t0, Q_BLOCK + WINDOW, axis=2)
        kpos = t0 - WINDOW + jnp.arange(Q_BLOCK + WINDOW)
        diff = tpos[:, None] - kpos[None, :]
        wmask = (kpos[None, :] >= 0) & (diff >= 0) & (diff < WINDOW)
        p_w = masked_softmax(jnp.einsum('bghtd,bgsd->bghts', qblk, kwin) * scale, wmask)
        o_w = jnp.einsum('bghts,bgsd->bghtd', p_w.astype(dt), vwin)
        return jnp.stack([o_c, o_s, o_w], axis=-2)

    out = lax.map(block, jnp.arange(S // Q_BLOCK))
    out = out.transpose(1, 0, 4, 2, 3, 5, 6).reshape(B, S, ATTN_HEADS, N_NSA_BRANCHES, HEAD_DIM)
    g = jax.nn.sigmoid(gates.reshape(B, S, ATTN_HEADS, N_NSA_BRANCHES))
    return jnp.einsum('bshcd,bshc->bshd', out, g).reshape(B, S, ATTN_DIM)

def rwkv7_time_mix(p, mu, w0, w_lora_up, a0, a_lora_up, g_lora_up, k_k, k_a, r_k, ln_w, ln_b):
    B, S, _ = p.shape
    f32 = jnp.float32
    dt = p.dtype
    shifted = jnp.pad(p, ((0, 0), (1, 0), (0, 0)))[:, :-1]
    p = p + (shifted - p) * mu
    splits = np.cumsum((RWKV_DIM, RWKV_DIM, RWKV_DIM, W_LORA, A_LORA)).tolist()
    r, k, v, wl, al, gl = jnp.split(p, splits, axis=-1)
    w = -jax.nn.softplus(-(w0 + jnp.tanh(wl) @ w_lora_up)) - 0.5
    decay = jnp.exp(-jnp.exp(w.astype(f32)))
    a = jax.nn.sigmoid(a0 + al @ a_lora_up)
    g = jax.nn.sigmoid(gl) @ g_lora_up
    hd = lambda t: t.reshape(B, S, RWKV_HEADS, RWKV_HEAD_DIM).astype(f32)
    kk = hd(k * k_k)
    kk = kk * lax.rsqrt(jnp.maximum(jnp.sum(kk * kk, axis=-1, keepdims=True), 1e-24))
    k = k * (1.0 + (a - 1.0) * k_a)
    rh, wh, kh, vh, ah = hd(r), hd(decay), hd(k), hd(v), hd(a)

    def step(state, inp):
        r_t, w_t, k_t, v_t, kk_t, a_t = inp
        sa = jnp.einsum('bhvk,bhk->bhv', state, -kk_t)
        state = (state * w_t[:, :, None, :] + sa[..., None] * (kk_t * a_t)[:, :, None, :]
                 + v_t[..., None] * k_t[:, :, None, :])
        return state, jnp.einsum('bhvk,bhk->bhv', state, r_t)

    tm = lambda t: jnp.moveaxis(t, 1, 0)
    state0 = jnp.zeros((B, RWKV_HEADS, RWKV_HEAD_DIM, RWKV_HEAD_DIM), f32)
    _, y = lax.scan(step, state0, (tm(rh), tm(wh), tm(kh), tm(vh), tm(kk), tm(ah)))
    y = jnp.moveaxis(y, 0, 1)
    mean = jnp.mean(y, axis=-1, keepdims=True)
    var = jnp.mean(jnp.square(y - mean), axis=-1, keepdims=True)
    y = ((y - mean) * lax.rsqrt(var + GN_EPS)).reshape(B, S, RWKV_DIM) * ln_w + ln_b
    bonus = jnp.sum(rh * kh * r_k, axis=-1, keepdims=True) * vh
    y = (y + bonus.reshape(B, S, RWKV_DIM)) * g
    return y.astype(dt)

def setup_inputs(seed: int = 0) -> dict:
    key = jax.random.key(seed)
    ks = jax.random.split(key, 32)
    f32 = jnp.float32
    nrm = lambda k, shape, s: jax.random.normal(k, shape, f32) * s
    L = DEPTH
    ramp = jnp.arange(RWKV_DIM, dtype=f32) / (RWKV_DIM - 1)
    return {
        "x": nrm(ks[0], (BATCH, SEQ, D_MODEL), 1.0),
        "mix_norm": 1.0 + nrm(ks[1], (L, D_MODEL), 0.02),
        "w_in": nrm(ks[2], (L, D_MODEL, PROJ_DIM), D_MODEL ** -0.5),
        "q_gain": 1.0 + nrm(ks[3], (L, HEAD_DIM), 0.02),
        "k_gain": 1.0 + nrm(ks[4], (L, N_NSA_BRANCHES, HEAD_DIM), 0.02),
        "cmp_pos": nrm(ks[5], (L, 2, CMP_BLOCK, HEAD_DIM), 0.1),
        "cmp_w1": nrm(ks[6], (L, 2, CMP_BLOCK * HEAD_DIM, CMP_HIDDEN), (CMP_BLOCK * HEAD_DIM) ** -0.5),
        "cmp_w2": nrm(ks[7], (L, 2, CMP_HIDDEN, HEAD_DIM), CMP_HIDDEN ** -0.5),
        "w_attn_branch": nrm(ks[8], (L, ATTN_DIM, D_MODEL), ATTN_DIM ** -0.5),
        "tok_mix": jax.random.uniform(ks[9], (L, RWKV_MIX_DIM), f32),
        "w0": -6.0 + 5.0 * ramp ** 0.9 + nrm(ks[10], (L, RWKV_DIM), 0.1),
        "w_lora_up": nrm(ks[11], (L, W_LORA, RWKV_DIM), 0.5 * W_LORA ** -0.5),
        "a0": nrm(ks[12], (L, RWKV_DIM), 0.1),
        "a_lora_up": nrm(ks[13], (L, A_LORA, RWKV_DIM), A_LORA ** -0.5),
        "g_lora_up": nrm(ks[14], (L, G_LORA, RWKV_DIM), G_LORA ** -0.5),
        "k_k": 0.85 + nrm(ks[15], (L, RWKV_DIM), 0.02),
        "k_a": 1.0 + nrm(ks[16], (L, RWKV_DIM), 0.02),
        "r_k": nrm(ks[17], (L, RWKV_HEADS, RWKV_HEAD_DIM), 0.1),
        "ln_x_w": 1.0 + nrm(ks[18], (L, RWKV_DIM), 0.02),
        "ln_x_b": nrm(ks[19], (L, RWKV_DIM), 0.02),
        "w_rwkv_branch": nrm(ks[20], (L, RWKV_DIM, D_MODEL), RWKV_DIM ** -0.5),
        "w_out": nrm(ks[21], (L, D_MODEL, D_MODEL), D_MODEL ** -0.5),
        "ffn_norm": 1.0 + nrm(ks[22], (L, D_MODEL), 0.02),
        "w_ffn_up": nrm(ks[23], (L, D_MODEL, D_FF), D_MODEL ** -0.5),
        "w_ffn_down": nrm(ks[24], (L, D_FF, D_MODEL), D_FF ** -0.5),
    }

def reference(x, mix_norm, w_in, q_gain, k_gain, cmp_pos, cmp_w1, cmp_w2, w_attn_branch,
              tok_mix, w0, w_lora_up, a0, a_lora_up, g_lora_up, k_k, k_a, r_k, ln_x_w, ln_x_b,
              w_rwkv_branch, w_out, ffn_norm, w_ffn_up, w_ffn_down):
    nsa_splits = np.cumsum((ATTN_DIM,) + (KV_DIM,) * 6).tolist()
    for l in range(DEPTH):
        u = rms_norm(x, mix_norm[l])
        proj = u @ w_in[l]
        nsa_p, rwkv_p, gate_p = jnp.split(proj, [NSA_DIM, NSA_DIM + RWKV_MIX_DIM], axis=-1)
        q, kc, vc, ks_, vs_, kw, vw, nsa_g = jnp.split(nsa_p, nsa_splits, axis=-1)
        y_a = nsa_attention(q, kc, vc, ks_, vs_, kw, vw, nsa_g, q_gain[l], k_gain[l],
                            cmp_pos[l], cmp_w1[l], cmp_w2[l])
        y_b = rwkv7_time_mix(rwkv_p, tok_mix[l], w0[l], w_lora_up[l], a0[l], a_lora_up[l],
                             g_lora_up[l], k_k[l], k_a[l], r_k[l], ln_x_w[l], ln_x_b[l])
        g_a, g_b = jnp.split(gate_p, N_BRANCHES, axis=-1)
        merged = (jax.nn.sigmoid(g_a) * (y_a @ w_attn_branch[l])
                  + jax.nn.sigmoid(g_b) * (y_b @ w_rwkv_branch[l]))
        x = x + merged @ w_out[l]
        h = rms_norm(x, ffn_norm[l])
        x = x + jnp.square(jax.nn.relu(h @ w_ffn_up[l])) @ w_ffn_down[l]
    return x


_drawn_inputs = setup_inputs


def setup_inputs(seed=0):
    import zlib

    import numpy as np

    out = dict(_drawn_inputs(seed))
    spreads = {}
    factors = {'mix_norm': 4.429,
     'q_gain': 59.876,
     'k_gain': 64.0,
     'cmp_pos': 31.704,
     'w_lora_up': 17.775,
     'a0': 4.823,
     'k_k': 64.0,
     'k_a': 8.0,
     'ln_x_w': 64.0,
     'ln_x_b': 64.0,
     'ffn_norm': 25.672,
     'cmp_w1': 3.254,
     'cmp_w2': 2.743}
    for name, (base, spread) in spreads.items():
        noise = np.random.default_rng([zlib.crc32(name.encode()), seed]).standard_normal(out[name].shape)
        drawn = base * np.exp(spread * noise) if base else spread * noise
        out[name] = __import__('jax').numpy.asarray(drawn.astype(out[name].dtype))
    for name, factor in factors.items():
        out[name] = (out[name] * factor).astype(out[name].dtype)
    return out
```

```python
import numpy as np
import concourse.bass as bass
from concourse import mybir
from contextlib import ExitStack, contextmanager

F32 = mybir.dt.float32
BF16 = mybir.dt.bfloat16
ALU = mybir.AluOpType
ACT = mybir.ActivationFunctionType
AX = mybir.AxisListType

P = 128
T = 1024
D = 1024
KC = D // P
HALF = 512
NH = 8
HD = 64
PAIRS = NH // 2
NQT = T // P
WIN_TILES = 512 // P
NCMP = (T - 32) // 16 + 1
CMP_HID = 128
DFF = 4096
NSA_TILES = 8
RW_TILES = 14
C = 64
NCH = T // C
NSA_COLS = 1304
TOKC = 280
RMS_EPS = 1e-6
GN_EPS = 64e-5
DECAY_SCALE = float(np.exp(np.float64(-0.5)))
NEG = -1e30

MIXN, FFNN, QG, KG, MU, W0, A0, KK, KA, RKP, LNW, LNB, NPAR = 0, 8, 16, 17, 20, 34, 38, 42, 50, 58, 66, 70, 74
_c = {}
_n = 0
for _name, _w in (("ident", 128), ("ones", 128), ("blockones", 128), ("diagneg", 128), ("winneg", 128),
                  ("cmask", 8 * 63), ("flag", 1), ("u_d", 64), ("u_32", 64), ("u_64", 64), ("u_lt", 64),
                  ("u_le", 64), ("l_d", 64), ("l_32", 64), ("l_64", 64), ("ident64", 64), ("scan", 512),
                  ("eps", 1), ("gneps", 1)):
    _c[_name] = (_n, _w)
    _n += _w
NCST = _n


def constants():
    out = np.zeros((P, NCST), np.float32)

    def put(name, a):
        o, w = _c[name]
        out[:, o:o + w] = np.asarray(a).reshape(-1, w)

    p = np.arange(P)[:, None]
    f = np.arange(P)[None, :]
    put("ident", p == f)
    put("ones", np.ones((P, P)))
    put("blockones", p // HD == f // HD)
    put("diagneg", np.where(f > p, NEG, 0.0))
    put("winneg", np.where(f <= p, NEG, 0.0))
    n = np.arange(NCMP)[None, None, :]
    q = np.arange(NQT)[None, :, None] * P + np.arange(P)[:, None, None]
    put("cmask", np.where(16 * n + 31 <= q, 0.0, NEG))
    put("flag", p >= 31)
    s = p % C
    t = np.arange(C)[None, :]
    b16 = s // 16 == t // 16
    b32 = s // 32 == t // 32
    put("u_d", (s < t) & b16)
    put("u_32", (s < t) & ~b16 & b32)
    put("u_64", (s < t) & ~b32)
    put("u_lt", s < t)
    put("u_le", s <= t)
    put("l_d", (s > t) & b16)
    put("l_32", (s > t) & ~b16 & b32)
    put("l_64", (s > t) & ~b32)
    put("ident64", s == t)
    put("scan", np.broadcast_to(np.arange(512) % C != 0, (P, 512)))
    put("eps", np.full((P, 1), RMS_EPS))
    put("gneps", np.full((P, 1), GN_EPS))
    return out


@contextmanager
def cleared_semaphores(nc, prefix):
    made = {}

    def sem(name):
        if name not in made:
            made[name] = nc.alloc_semaphore(prefix + name)
        return made[name]

    yield sem
    nc.clear_and_free_semaphores(list(made.values()))
    nc.all_engine_barrier()


class Arena:

    def __init__(self, tensor):
        self.t = tensor

    def at(self, off, *shape):
        n = int(np.prod(shape))
        ap = self.t[:, off:off + n]
        if len(shape) == 1:
            return ap
        names = "abcd"[:len(shape)]
        kw = {x: s for x, s in zip(names, shape)}
        return ap.rearrange("p (" + " ".join(names) + ") -> p " + " ".join(names), **kw)


O_CST = 0
O_PAR = O_CST + NCST
O_SMALL = O_PAR + NPAR
O_RSTD = O_SMALL + 160
O_NSA = O_RSTD + 1024
O_VT = O_NSA + 8 * 1024
O_WR = O_VT + 8 * TOKC
O_U = O_WR + 2 * 1024
O_X = O_U + 8 * 1024
ARENA = 52900


def par(A, i, n=1):
    return A.at(O_PAR + i, n)


def cst(A, name):
    o, w = _c[name]
    return A.at(O_CST + o, w)


def load_and_norm(nc, A, PS, x_in, cst_in, par_in):
    X = A.at(O_X, 8, 1024)
    SQ = A.at(O_X + 8 * 1024, 2, 1024)
    U = A.at(O_U, 8, 1024)
    RSTD = A.at(O_RSTD, 1024)
    with (nc.semaphore("n_const") as const_in, nc.semaphore("n_x0") as x0, nc.semaphore("n_x1") as x1,
          nc.semaphore("n_sq") as squared,
          nc.semaphore("n_sum") as summed, nc.semaphore("n_rms") as rms, nc.semaphore("n_rs") as rs,
          nc.Block() as block):
        @block.sync
        def _(sp):
            sp.dma_start(A.at(O_CST, NCST), cst_in).then_inc(const_in, 16)
            sp.dma_start(A.at(O_PAR, NPAR), par_in).then_inc(const_in, 16)
            for c in range(KC):
                if c >= 2:
                    sp.wait_ge((x0, x1)[c % 2], 16 * (c // 2))
                sp.dma_start(X[:, c, :], x_in[c * P:(c + 1) * P, :]).then_inc((x0, x1)[c % 2], 16)

        @block.scalar
        def _(act):
            for c in range(KC):
                act.wait_ge((x0, x1)[c % 2], 16 * (c // 2 + 1))
                if c >= 2:
                    act.wait_ge(summed, c - 1)
                act.activation(SQ[:, c % 2, :], X[:, c, :], ACT.Square).then_inc(squared, 1)
            act.wait_ge(summed, KC)
            act.activation(RSTD, PS[:, 0:2, :], ACT.Sqrt, scale=1.0 / D, bias=cst(A, "eps")).then_inc(rms, 1)

        @block.tensor
        def _(pe):
            pe.wait_ge(const_in, 32)
            for c in range(KC):
                pe.wait_ge(squared, c + 1)
                for h in range(2):
                    last = pe.matmul(PS[:, h, :], cst(A, "ones"), SQ[:, c % 2, h * HALF:(h + 1) * HALF],
                                     start=c == 0, stop=c == KC - 1)
                last.then_inc(summed, 1)

        @block.vector
        def _(dve):
            dve.wait_ge(rms, 1)
            dve.reciprocal(RSTD, RSTD).then_inc(rs, 1)
            dve.wait_ge(rs, 1)
            for c in range(KC):
                dve.scalar_tensor_tensor(U[:, c, :], X[:, c, :], par(A, MIXN + c), RSTD, ALU.mult, ALU.mult)


def project(nc, A, PS, w_in, n_tiles, OUT, rhs, tag):
    W = A.at(O_WR, 2, KC, P)
    n_pairs = n_tiles // 2
    with ExitStack() as ctx:
        sem = lambda n: ctx.enter_context(nc.semaphore(f"{tag}_{n}"))
        loaded = [sem("loaded0"), sem("loaded1")]
        product = [sem("product0"), sem("product1")]
        out_low = [sem("outlow0"), sem("outlow1")]
        out_high = [sem("outhigh0"), sem("outhigh1")]
        block = ctx.enter_context(nc.Block())

        @block.sync
        def _(sp):
            for s in range(2):
                sp.dma_start(W[:, s], w_in[s].rearrange("p (c n) -> p c n", c=KC)).then_inc(loaded[s], 16)
            with sp.Fori(0, n_pairs - 1) as i:
                for s in range(2):
                    sp.wait_ge(product[s], 2 * i + 2)
                    sp.dma_start(W[:, s], w_in[2 * i + 2 + s].rearrange("p (c n) -> p c n", c=KC)).then_inc(loaded[s], 16)

        @block.tensor
        def _(pe):
            with pe.Fori(0, n_pairs) as i:
                for s in range(2):
                    pe.wait_ge(loaded[s], 16 * i + 16)
                    for h in range(2):
                        pe.wait_ge((out_low, out_high)[h][s], i)
                        for c in range(KC):
                            last = pe.matmul(PS[:, 2 * s + h, :], W[:, s, c, :],
                                             rhs[:, c, h * HALF:(h + 1) * HALF],
                                             start=c == 0, stop=c == KC - 1)
                        last.then_inc(product[s], 1)

        @block.scalar
        def _(act):
            with act.Fori(0, n_pairs) as i:
                for s in range(2):
                    act.wait_ge(product[s], 2 * i + 1)
                    act.activation(OUT[:, 2 * i + s, 0:HALF], PS[:, 2 * s, :], ACT.Copy).then_inc(out_low[s], 1)

        @block.vector
        def _(dve):
            with dve.Fori(0, n_pairs) as i:
                for s in range(2):
                    dve.wait_ge(product[s], 2 * i + 2)
                    dve.tensor_copy(OUT[:, 2 * i + s, HALF:T], PS[:, 2 * s + 1, :]).then_inc(out_high[s], 1)


def project_tokens(nc, A, PS, w_in, VT, U):
    W = A.at(O_X, KC, TOKC)
    with (nc.semaphore("t_loaded") as loaded, nc.semaphore("t_product") as product,
          nc.semaphore("t_out") as out, nc.semaphore("t_tanh") as tanh, nc.Block() as block):
        @block.sync
        def _(sp):
            sp.dma_start(W, w_in.rearrange("p (c n) -> p c n", c=KC)).then_inc(loaded, 16)

        @block.tensor
        def _(pe):
            pe.wait_ge(loaded, 16)
            for t in range(NQT):
                for c in range(KC):
                    last = pe.matmul(PS[:, t, 0:TOKC], U[:, c, t * P:(t + 1) * P], W[:, c, :],
                                     start=c == 0, stop=c == KC - 1)
                last.then_inc(product, 1)

        @block.vector
        def _(dve):
            for t in range(NQT):
                dve.wait_ge(product, t + 1)
                dve.tensor_copy(VT[:, t, :], PS[:, t, 0:TOKC]).then_inc(out, 1)
            dve.wait_ge(tanh, 1)
            dve.tensor_scalar(VT[:, :, 256:TOKC], VT[:, :, 256:TOKC], 0.5, 0.5, ALU.mult, ALU.add)

        @block.scalar
        def _(act):
            act.wait_ge(out, NQT)
            act.activation(VT[:, :, 256:TOKC], VT[:, :, 256:TOKC], ACT.Tanh, scale=0.5).then_inc(tanh, 1)


def norm_heads(nc, A, PS, NSA, KPAD):
    SQ = A.at(O_X, 2, HALF)
    R = A.at(O_X + 2 * HALF, 2, HALF)
    GAINS = A.at(O_SMALL, 3)
    units = [(i, h) for i in range(6) for h in range(2)]
    with (nc.semaphore("h_sq") as squared, nc.semaphore("h_sum") as summed, nc.semaphore("h_root") as root,
          nc.semaphore("h_inv") as inverse, nc.semaphore("h_done") as done, nc.semaphore("h_zero") as zero,
          nc.Block() as block):
        @block.gpsimd
        def _(pool):
            for b in range(2):
                pool.memset(KPAD[64:128, 2 * b, :], 0.0)
                pool.memset(KPAD[0:64, 2 * b + 1, :], 0.0)

        @block.scalar
        def _(act):
            def root_of(n):
                act.wait_ge(summed, n + 1)
                if n >= 2:
                    act.wait_ge(done, n - 1)
                act.activation(R[:, n % 2, :], PS[:, n % 2, :], ACT.Sqrt, scale=1.0 / HD,
                               bias=cst(A, "eps")).then_inc(root, 1)

            for n, (i, h) in enumerate(units):
                if n >= 2:
                    act.wait_ge(summed, n - 1)
                act.activation(SQ[:, n % 2, :], NSA[:, i, h * HALF:(h + 1) * HALF], ACT.Square).then_inc(squared, 1)
                if n >= 1:
                    root_of(n - 1)
            root_of(len(units) - 1)

        @block.tensor
        def _(pe):
            for n in range(len(units)):
                pe.wait_ge(squared, n + 1)
                if n >= 2:
                    pe.wait_ge(root, n - 1)
                pe.matmul(PS[:, n % 2, :], cst(A, "blockones"), SQ[:, n % 2, :],
                          start=True, stop=True).then_inc(summed, 1)

        @block.vector
        def _(dve):
            dve.tensor_scalar(GAINS[:, 0:1], par(A, QG), 0.125, None, ALU.mult).then_inc(zero, 1)
            dve.wait_ge(zero, 1)
            for n, (i, h) in enumerate(units):
                cols = slice(h * HALF, (h + 1) * HALF)
                dve.wait_ge(root, n + 1)
                dve.reciprocal(R[:, n % 2, :], R[:, n % 2, :]).then_inc(inverse, 1)
                dve.wait_ge(inverse, n + 1)
                if i < PAIRS:
                    dve.scalar_tensor_tensor(NSA[:, i, cols], NSA[:, i, cols], GAINS[:, 0:1], R[:, n % 2, :],
                                             ALU.mult, ALU.mult).then_inc(done, 1)
                else:
                    b = i - PAIRS
                    for g in range(2):
                        rows = slice(64 * g, 64 * g + 64)
                        last = dve.scalar_tensor_tensor(KPAD[rows, 2 * b + g, cols], NSA[rows, i, cols],
                                                        par(A, KG + 1 + b)[rows], R[rows, n % 2, :],
                                                        ALU.mult, ALU.mult)
                    last.then_inc(done, 1)


def compress(nc, A, PS, NSA, KPC, VC, w1_in, w2_in, pos_in):
    W1 = A.at(O_X, 2, 32, CMP_HID)
    KV = A.at(O_X + 8192, 2, 2, 1024)
    POS = A.at(O_X + 12288, 2, 32)
    W2 = A.at(O_X + 12288 + 64, 2, HD)
    H = A.at(O_X + 12288 + 192, 4, CMP_HID)
    Q = A.at(O_X + 12288 + 704, 4, CMP_HID)
    HT = A.at(O_X + 12288 + 1216, 4, NCMP)
    SQ = A.at(O_X + 12288 + 1216 + 252, NCMP)
    KR = A.at(O_X + 12288 + 1216 + 252 + 63, NCMP)
    with ExitStack() as ctx:
        sem = lambda n: ctx.enter_context(nc.semaphore("c_" + n))
        loaded, posed, hidden, copied, squared, inner, tanh, gelu, turned, turned_out, out2, k_sq, k_sum, k_root, step = (
            sem(x) for x in ("loaded", "posed", "hidden", "copied", "squared", "inner", "tanh", "gelu", "turned",
                             "turnedout", "out2", "ksq", "ksum", "kroot", "step"))
        loaded2 = sem("loaded2")
        block = ctx.enter_context(nc.Block())

        @block.sync
        def _(sp):
            for half in range(2):
                sp.dma_start(POS[64 * half:64 * half + 64], pos_in).then_inc(loaded2, 16)
            sp.dma_start(W2, w2_in).then_inc(loaded2, 16)
            for half in range(2):
                sp.dma_start(W1[64 * half:64 * half + 64], w1_in).then_inc(loaded, 16)

        @block.vector
        def _(dve):
            dve.wait_ge(loaded2, 48)
            for v in range(2):
                src = NSA[:, 6 + v, :].rearrange("p (n s) -> p n s", s=16)
                for b in range(2):
                    dve.tensor_tensor(KV[:, v, b, :].rearrange("p (n s) -> p n s", s=16), src,
                                      POS[:, v, 16 * b:16 * b + 16].unsqueeze(1).to_broadcast([P, 64, 16]),
                                      ALU.add).then_inc(posed, 1)
            dve.wait_ge(hidden, 4)
            dve.tensor_copy(H[0:NCMP], PS[0:NCMP, 0:4, 0:CMP_HID]).then_inc(copied, 1)
            dve.wait_ge(squared, 1)
            dve.tensor_scalar(Q[0:NCMP], Q[0:NCMP], 0.044715, 1.0, ALU.mult, ALU.add).then_inc(step, 1)
            dve.wait_ge(step, 1)
            dve.tensor_tensor(Q[0:NCMP], Q[0:NCMP], H[0:NCMP], ALU.mult).then_inc(inner, 1)
            dve.wait_ge(tanh, 1)
            dve.scalar_tensor_tensor(H[0:NCMP], Q[0:NCMP], 1.0, H[0:NCMP], ALU.add, ALU.mult).then_inc(gelu, 1)
            dve.wait_ge(turned, 1)
            dve.tensor_scalar(HT, PS[:, 4, 0:4 * NCMP].rearrange("p (a n) -> p a n", a=4), 0.5, None,
                              ALU.mult).then_inc(turned_out, 1)
            dve.wait_ge(out2, 1)
            dve.tensor_copy(VC[0:NCMP], PS[0:NCMP, 6, 0:2 * HD].rearrange("p (g d) -> p g d", g=2))
            dve.memset(KPC, 0.0).then_inc(step, 1)
            dve.wait_ge(k_root, 1)
            dve.reciprocal(KR, KR).then_inc(step, 1)
            dve.wait_ge(step, 3)
            for g in range(2):
                rows = slice(64 * g, 64 * g + 64)
                dve.scalar_tensor_tensor(KPC[rows, g, :], PS[rows, 5, 0:NCMP], par(A, KG)[rows], KR[rows, :],
                                         ALU.mult, ALU.mult)

        @block.tensor
        def _(pe):
            pe.wait_ge(loaded, 32)
            for v in range(2):
                pe.wait_ge(posed, 2 * v + 2)
                for g in range(2):
                    rows = slice(64 * g, 64 * g + 64)
                    for p in range(32):
                        kv = KV[rows, v, p // 16, :].rearrange("p (n s) -> p n s", s=16)
                        last = pe.matmul(PS[0:NCMP, 2 * v + g, 0:CMP_HID],
                                         kv[:, p // 16:p // 16 + NCMP, p % 16], W1[rows, v, p, :],
                                         start=p == 0, stop=p == 31)
                    last.then_inc(hidden, 1)
            pe.wait_ge(gelu, 1)
            for a in range(4):
                last = pe.transpose(PS[:, 4, a * NCMP:(a + 1) * NCMP], H[0:NCMP, a, :], cst(A, "ident")[0:NCMP, 0:NCMP])
            last.then_inc(turned, 1)
            pe.wait_ge(turned_out, 1)
            for g in range(2):
                pe.matmul(PS[64 * g:64 * g + 64, 5, 0:NCMP], W2[:, 0, :], HT[:, g, :], start=True, stop=True)
            for g in range(2):
                last = pe.matmul(PS[0:NCMP, 6, g * HD:(g + 1) * HD], HT[:, 2 + g, :], W2[:, 1, :], start=True, stop=True)
            last.then_inc(out2, 1)
            pe.wait_ge(k_sq, 1)
            pe.matmul(PS[:, 7, 0:NCMP], cst(A, "blockones"), SQ, start=True, stop=True).then_inc(k_sum, 1)

        @block.scalar
        def _(act):
            act.wait_ge(copied, 1)
            act.activation(Q[0:NCMP], H[0:NCMP], ACT.Square).then_inc(squared, 1)
            act.wait_ge(inner, 1)
            act.activation(Q[0:NCMP], Q[0:NCMP], ACT.Tanh, scale=float(np.sqrt(2.0 / np.pi))).then_inc(tanh, 1)
            act.wait_ge(out2, 1)
            act.activation(SQ, PS[:, 5, 0:NCMP], ACT.Square).then_inc(k_sq, 1)
            act.wait_ge(k_sum, 1)
            act.activation(KR, PS[:, 7, 0:NCMP], ACT.Sqrt, scale=1.0 / HD, bias=cst(A, "eps")).then_inc(k_root, 1)


def attention(nc, A, PS, NSA, KPAD, KPC, VT, VC):
    PT = A.at(O_X + 6144, 2, 14, PAIRS, P)
    PB = A.at(O_X + 6144 + 14336, 2, 1728)
    QB = A.at(O_X + 6144 + 14336 + 3456, P)
    at = O_X + 6144 + 14336 + 3456 + P
    IDENTB = A.at(at, 64).bitcast(BF16)
    DIAGB = A.at(at + 64, 64).bitcast(BF16)
    WINB = A.at(at + 128, 64).bitcast(BF16)
    NM = A.at(at + 192, 2, 3)
    L = A.at(at + 198, 2, 3)
    RL = A.at(at + 204, 2, 3)
    SC = A.at(at + 210, 2, 3)
    CMP, SLC, WIN = 0, 1, 2
    S_slc = PS[:, 0:2, :].rearrange("p a n -> p (a n)")
    S_win = PS[:, 2:4, :].rearrange("p a n -> p (a n)")
    CMP_AT = 640
    T_BANK, O_BANK = 4, 7

    def window(qt):
        return max(0, qt - WIN_TILES), qt + 1

    def blocks(qt):
        lo, hi = window(qt)
        return ([("slc", k, k * P) for k in range(qt + 1)]
                + [("win", k, 1024 + (k - lo) * P) for k in range(lo, hi)] + [("cmp", 0, 1664)])

    def chunks(qt):
        b = list(enumerate(blocks(qt)))
        n = qt + 1
        out = [b[k:min(k + 4, n)] for k in range(0, n, 4)]
        return out + [b[k:k + 4] for k in range(n, len(b), 4)]

    def evacuated_by(qt):
        return [k % 2 for k in range(len(chunks(qt)))]

    n_chunks = [len(chunks(qt)) for qt in range(NQT)]
    per_engine = [[evacuated_by(qt).count(e) for qt in range(NQT)] for e in range(2)]

    def unit(qt, j, g):
        return 8 * qt + 2 * j + g

    def chunk_count(qt, j, g, k):
        return 8 * sum(n_chunks[:qt]) + (2 * j + g) * n_chunks[qt] + k + 1

    def out_count(e, qt, j, g, k):
        return (8 * sum(per_engine[e][:qt]) + (2 * j + g) * per_engine[e][qt]
                + evacuated_by(qt)[:k + 1].count(e))

    def in_order(eng, front, back, after):
        front(0, 0, 0)
        for qt in range(NQT):
            def pair(j):
                front(qt, j, 1)
                back(qt, j, 0)
                front(qt, j + 1, 0)
                back(qt, j, 1)
            if qt == 0:
                for j in range(PAIRS - 1):
                    pair(j)
            else:
                with eng.Fori(0, PAIRS - 1) as j:
                    pair(j)
            front(qt, PAIRS - 1, 1)
            back(qt, PAIRS - 1, 0)
            if qt + 1 < NQT:
                front(qt + 1, 0, 0)
            back(qt, PAIRS - 1, 1)
            after(qt)

    with ExitStack() as ctx:
        sem = lambda n: ctx.enter_context(nc.semaphore("a_" + n))
        masks = sem("masks")
        q_copied = sem("qcopied")
        scored_slc = sem("scoredslc")
        scored_win = sem("scoredwin")
        maxed = sem("maxed")
        exp_slc = sem("expslc")
        exp_win = sem("expwin")
        inverse = sem("inverse")
        factor = sem("factor")
        scaled = sem("scaled")
        turned = sem("turned")
        out_by = [sem("outact"), sem("outdve")]
        summed = sem("summed")
        begun = [sem("begunpe"), sem("begunpool")]
        stored = sem("stored")
        block = ctx.enter_context(nc.Block())

        @block.gpsimd
        def _(pool):
            for dst, name in ((IDENTB, "ident"), (DIAGB, "diagneg"), (WINB, "winneg")):
                last = pool.tensor_copy(dst, cst(A, name))
            last.then_inc(masks, 1)

            def front(qt, j, g):
                if g == 0:
                    if not (isinstance(j, int) and unit(qt, j, g) == 0):
                        pool.wait_ge(scored_win, unit(qt, j, g))
                    pool.tensor_copy(QB, NSA[:, j, qt * P:(qt + 1) * P]).then_inc(q_copied, 1)

            def back(qt, j, g):
                lo, hi = window(qt)
                pool.wait_ge(factor, unit(qt, j, g) + 1)
                pool.sem_inc(begun[1], 1)
                for at_, n, c in ((0, (qt + 1) * P, SLC), (1024, (hi - lo) * P, WIN), (1664, NCMP, CMP)):
                    pool.tensor_scalar(PB[:, g, at_:at_ + n], PB[:, g, at_:at_ + n], SC[:, g, c:c + 1], None,
                                       ALU.mult).then_inc(scaled, 1)

            in_order(pool, front, back, lambda qt: None)

        @block.tensor
        def _(pe):
            pe.wait_ge(masks, 1)

            def front(qt, j, g):
                u = unit(qt, j, g)
                first = isinstance(u, int) and u == 0
                lo, hi = window(qt)
                pe.wait_ge(q_copied, 4 * qt + j + 1)
                if not first:
                    pe.wait_ge(exp_slc, u)
                n = (qt + 1) * P
                for b in range(0, n, HALF):
                    w = min(HALF, n - b)
                    diag = b + w == n
                    pe.matmul(S_slc[:, b:b + w], QB, KPAD[:, g, b:b + w], start=True, stop=not diag)
                last = pe.matmul(S_slc[:, n - P:n], IDENTB, DIAGB, start=False, stop=True)
                last.then_inc(scored_slc, 1)
                if not first:
                    pe.wait_ge(exp_win, u)
                n = (hi - lo) * P
                for b in range(0, n, HALF):
                    w = min(HALF, n - b)
                    old = b == 0 and qt >= WIN_TILES
                    diag = b + w == n
                    pe.matmul(S_win[:, b:b + w], QB, KPAD[:, 2 + g, lo * P + b:lo * P + b + w], start=True,
                              stop=not (old or diag))
                    if old:
                        pe.matmul(S_win[:, 0:P], IDENTB, WINB, start=False, stop=not diag)
                    if diag:
                        pe.matmul(S_win[:, n - P:n], IDENTB, DIAGB, start=False, stop=True)
                pe.matmul(S_win[:, CMP_AT:CMP_AT + NCMP], QB, KPC[:, g, :], start=True, stop=False)
                last = pe.matmul(S_win[:, CMP_AT:CMP_AT + NCMP], cst(A, "ident"),
                                 cst(A, "cmask")[:, qt * NCMP:(qt + 1) * NCMP], start=False, stop=True)
                last.then_inc(scored_win, 1)

            def back(qt, j, g):
                u = unit(qt, j, g)
                for k, chunk in enumerate(chunks(qt)):
                    kinds = {kind for _, (kind, _, _) in chunk}
                    pe.wait_ge(scaled, 3 * u + (3 if "cmp" in kinds else 2 if "win" in kinds else 1))
                    if k >= 3:
                        e = evacuated_by(qt)[k - 3]
                        pe.wait_ge(out_by[e], out_count(e, qt, j, g, k - 3))
                    else:
                        before = max(x for x in range(n_chunks[qt]) if x % 3 == k % 3)
                        e = evacuated_by(qt)[before]
                        v = out_count(e, qt, j, g, before) - per_engine[e][qt]
                        if not (isinstance(v, int) and u == 0):
                            pe.wait_ge(out_by[e], v)
                    pe.sem_inc(begun[0], 1)
                    for x, (_, (kind, _, col)) in enumerate(chunk):
                        if kind == "cmp":
                            last = pe.transpose(PS[0:NCMP, T_BANK + k % 3, x * P:(x + 1) * P],
                                                PB[:, g, col:col + NCMP], cst(A, "ident"))
                        else:
                            last = pe.transpose(PS[:, T_BANK + k % 3, x * P:(x + 1) * P],
                                                PB[:, g, col:col + P], cst(A, "ident"))
                    last.then_inc(turned, 1)

            def after(qt):
                for e in range(2):
                    pe.wait_ge(out_by[e], out_count(e, qt, PAIRS - 1, 1, n_chunks[qt] - 1))
                if qt >= 1:
                    pe.wait_ge(stored, qt)
                for g in range(2):
                    todo = blocks(qt)
                    for x, (kind, k, _) in enumerate(todo):
                        rows = NCMP if kind == "cmp" else P
                        v = (VC[0:NCMP, g, :] if kind == "cmp" else
                             VT[:, k, (kind == "win") * P + g * HD:(kind == "win") * P + (g + 1) * HD])
                        last = pe.matmul(PS[g * HD:(g + 1) * HD, O_BANK, :], v,
                                         PT[0:rows, g, x, :, :].rearrange("p a n -> p (a n)"),
                                         start=x == 0, stop=x == len(todo) - 1)
                last.then_inc(summed, 1)

            in_order(pe, front, back, after)

        def copy_out(eng, e, copy, qt, j, g):
            for k, chunk in enumerate(chunks(qt)):
                if evacuated_by(qt)[k] != e:
                    continue
                eng.wait_ge(turned, chunk_count(qt, j, g, k))
                if qt >= 1:
                    eng.wait_ge(summed, qt)
                x0 = chunk[0][0]
                whole = [c for c in chunk if c[1][0] != "cmp"]
                if whole:
                    last = copy(PT[:, g, x0:x0 + len(whole), j, :],
                                PS[:, T_BANK + k % 3, 0:len(whole) * P].rearrange("p (a n) -> p a n", n=P))
                if len(whole) < len(chunk):
                    x = len(whole)
                    last = copy(PT[0:NCMP, g, x0 + x, j, :], PS[0:NCMP, T_BANK + k % 3, x * P:(x + 1) * P])
                last.then_inc(out_by[e], 1)

        @block.vector
        def _(dve):
            def front(qt, j, g):
                u = unit(qt, j, g)
                lo, hi = window(qt)
                dve.wait_ge(scored_slc, u + 1)
                dve.tensor_reduce(NM[:, g, SLC:SLC + 1], S_slc[:, 0:(qt + 1) * P], axis=AX.X, op=ALU.max,
                                  negate=True).then_inc(maxed, 1)
                dve.wait_ge(scored_win, u + 1)
                dve.tensor_reduce(NM[:, g, WIN:WIN + 1], S_win[:, 0:(hi - lo) * P], axis=AX.X, op=ALU.max,
                                  negate=True).then_inc(maxed, 1)
                dve.tensor_reduce(NM[:, g, CMP:CMP + 1], S_win[:, CMP_AT:CMP_AT + NCMP], axis=AX.X, op=ALU.max,
                                  negate=True).then_inc(maxed, 1)

            def back(qt, j, g):
                u = unit(qt, j, g)
                dve.wait_ge(exp_win, u + 1)
                dve.reciprocal(RL[:, g, :], L[:, g, :]).then_inc(inverse, 1)
                dve.wait_ge(inverse, u + 1 + min(qt, 1) * 0)
                if qt == 0:
                    dve.tensor_tensor(RL[:, g, CMP:CMP + 1], RL[:, g, CMP:CMP + 1], cst(A, "flag"),
                                      ALU.mult).then_inc(masks, 1)
                    dve.wait_ge(masks, u + 2)
                gate = VT[:, qt, 256:TOKC].rearrange("p (g j c) -> p g j c", g=2, c=3)[:, g, j, :]
                dve.tensor_tensor(SC[:, g, :], RL[:, g, :], gate, ALU.mult).then_inc(factor, 1)
                copy_out(dve, 1, lambda o, i: dve.tensor_copy(o, i), qt, j, g)

            in_order(dve, front, back, lambda qt: None)

        @block.scalar
        def _(act):
            def front(qt, j, g):
                u = unit(qt, j, g)
                lo, hi = window(qt)
                if not (isinstance(u, int) and u < 2):
                    if isinstance(u, int) or qt > 0:
                        act.wait_ge(turned, free_count(qt, j, g))
                act.wait_ge(maxed, 3 * u + 1)
                act.activation(PB[:, g, 0:(qt + 1) * P], S_slc[:, 0:(qt + 1) * P], ACT.Exp,
                               bias=NM[:, g, SLC:SLC + 1], accum_out=L[:, g, SLC:SLC + 1]).then_inc(exp_slc, 1)
                act.wait_ge(maxed, 3 * u + 3)
                act.activation(PB[:, g, 1024:1024 + (hi - lo) * P], S_win[:, 0:(hi - lo) * P], ACT.Exp,
                               bias=NM[:, g, WIN:WIN + 1], accum_out=L[:, g, WIN:WIN + 1])
                act.activation(PB[:, g, 1664:1664 + NCMP], S_win[:, CMP_AT:CMP_AT + NCMP], ACT.Exp,
                               bias=NM[:, g, CMP:CMP + 1], accum_out=L[:, g, CMP:CMP + 1]).then_inc(exp_win, 1)

            def free_count(qt, j, g):
                if isinstance(j, int):
                    u = unit(qt, j, g) - 2
                    q0, r = divmod(u, 8)
                    return chunk_count(q0, r // 2, r % 2, n_chunks[q0] - 1)
                return chunk_count(qt, j - 1, g, n_chunks[qt] - 1)

            def back(qt, j, g):
                copy_out(act, 0, lambda o, i: act.activation(o, i, ACT.Copy), qt, j, g)

            def after(qt):
                act.wait_ge(summed, qt + 1)
                act.activation(NSA[:, 0:PAIRS, qt * P:(qt + 1) * P],
                               PS[:, O_BANK, :].rearrange("p (a n) -> p a n", n=P), ACT.Copy).then_inc(stored, 1)

            in_order(act, front, back, after)


def mix_and_lora(nc, A, PS, RJ, DEC, AA, KN, lora_in):
    DIFF = A.at(O_NSA + 4 * 1024, 2, 1024)
    SQ = A.at(O_NSA + 6 * 1024, 2, HALF)
    R = A.at(O_NSA + 7 * 1024, 2, HALF)
    LORA = A.at(O_VT, HALF)
    HALFB = A.at(O_SMALL, 8)
    order = [12, 13] + list(range(4, 8)) + list(range(0, 4)) + list(range(8, 12))
    with ExitStack() as ctx:
        sem = lambda n: ctx.enter_context(nc.semaphore("m_" + n))
        loaded, diff, mixed, tanh_in, product, tanh_out, affine = (
            sem(x) for x in ("loaded", "diff", "mixed", "tanhin", "product", "tanhout", "affine"))
        squared, summed, clamped, root, inverse, keyed, half_bias = (
            sem(x) for x in ("squared", "summed", "clamped", "root", "inverse", "keyed", "halfbias"))
        block = ctx.enter_context(nc.Block())
        units = [(j, h) for j in range(PAIRS) for h in range(2)]

        @block.sync
        def _(sp):
            sp.dma_start(LORA, lora_in).then_inc(loaded, 16)

        @block.vector
        def _(dve):
            dve.tensor_scalar(HALFB, par(A, W0, 8), 0.5, None, ALU.mult).then_inc(half_bias, 1)

            def mix(n):
                i, b = order[n], n % 2
                if n >= 2:
                    dve.wait_ge(mixed, n - 1)
                dve.tensor_tensor(DIFF[:, b, 1:T], RJ[:, i, 0:T - 1], RJ[:, i, 1:T], ALU.subtract)
                dve.tensor_scalar(DIFF[:, b, 0:1], RJ[:, i, 0:1], -1.0, None, ALU.mult).then_inc(diff, 1)
                dve.wait_ge(diff, n + 1)
                dve.scalar_tensor_tensor(RJ[:, i, :], DIFF[:, b, :], par(A, MU + i), RJ[:, i, :],
                                         ALU.mult, ALU.add).then_inc(mixed, 1)

            for n in range(6):
                mix(n)
            for n, (j, h) in enumerate(units):
                cols = slice(h * HALF, (h + 1) * HALF)
                dve.wait_ge(mixed, 3 + j)
                dve.wait_ge(summed, n + 1)
                dve.tensor_scalar(R[:, n % 2, :], PS[:, n % 2, :], 1e-24, None, ALU.max).then_inc(clamped, 1)
                dve.wait_ge(root, n + 1)
                dve.reciprocal(R[:, n % 2, :], R[:, n % 2, :]).then_inc(inverse, 1)
                dve.wait_ge(inverse, n + 1)
                dve.scalar_tensor_tensor(KN[:, j, cols], RJ[:, 4 + j, cols], par(A, KK + 2 * j), R[:, n % 2, :],
                                         ALU.mult, ALU.mult).then_inc(keyed, 1)
            for n in range(6, RW_TILES):
                mix(n)
            dve.wait_ge(tanh_in, 2)
            dve.tensor_scalar(RJ[:, 13, :], RJ[:, 13, :], 0.5, 0.5, ALU.mult, ALU.add)
            for n, (j, h) in enumerate(units):
                cols = slice(h * HALF, (h + 1) * HALF)
                dve.wait_ge(tanh_out, 2 * n + 2)
                dve.tensor_scalar(DEC[:, j, cols], DEC[:, j, cols], -0.5 * DECAY_SCALE, -0.5 * DECAY_SCALE,
                                  ALU.mult, ALU.add)
                dve.tensor_scalar(AA[:, j, cols], AA[:, j, cols], 0.5, 0.5, ALU.mult, ALU.add)

        @block.scalar
        def _(act):
            for n, (j, h) in enumerate(units):
                act.wait_ge(mixed, 3 + j)
                if n >= 2:
                    act.wait_ge(summed, n - 1)
                act.activation(SQ[:, n % 2, :], RJ[:, 4 + j, h * HALF:(h + 1) * HALF], ACT.Square,
                               scale=par(A, KK + 2 * j)).then_inc(squared, 1)
                act.wait_ge(clamped, n + 1)
                act.activation(R[:, n % 2, :], R[:, n % 2, :], ACT.Sqrt).then_inc(root, 1)
            act.wait_ge(mixed, 2)
            act.activation(RJ[0:64, 12, :], RJ[0:64, 12, :], ACT.Tanh).then_inc(tanh_in, 1)
            act.activation(RJ[:, 13, :], RJ[:, 13, :], ACT.Tanh, scale=0.5).then_inc(tanh_in, 1)
            act.wait_ge(half_bias, 1)
            for n, (j, h) in enumerate(units):
                cols = slice(h * HALF, (h + 1) * HALF)
                for x, dst in enumerate((DEC, AA)):
                    act.wait_ge(product, 2 * n + x + 1)
                    act.activation(dst[:, j, cols], PS[:, 2 + 2 * x + n % 2, :], ACT.Tanh, scale=0.5,
                                   bias=HALFB[:, 4 * x + j:4 * x + j + 1]).then_inc(tanh_out, 1)

        @block.tensor
        def _(pe):
            for n in range(len(units)):
                pe.wait_ge(squared, n + 1)
                if n >= 2:
                    pe.wait_ge(clamped, n - 1)
                pe.matmul(PS[:, n % 2, :], cst(A, "blockones"), SQ[:, n % 2, :], start=True, stop=True).then_inc(summed, 1)
            pe.wait_ge(loaded, 16)
            pe.wait_ge(tanh_in, 1)
            for n, (j, h) in enumerate(units):
                for x in range(2):
                    if n >= 2:
                        pe.wait_ge(tanh_out, 2 * n + x - 3)
                    rows = slice(64 * x, 64 * x + 64)
                    pe.matmul(PS[:, 2 + 2 * x + n % 2, :], LORA[rows, j * P:(j + 1) * P],
                              RJ[rows, 12, h * HALF:(h + 1) * HALF], start=True, stop=True).then_inc(product, 1)


def rwkv_chunks(nc, A, PS, RJ, DEC, AA, KN):
    R8, K8, V8, D8, A8, KN8 = (x.rearrange("p a (b n) -> p (a b) n", b=2)
                               for x in (RJ[:, 0:4, :], RJ[:, 4:8, :], RJ[:, 8:12, :], DEC, AA, KN))
    base = [O_NSA + 4 * 1024 + 512 * x for x in range(8)] + [O_VT + 512 * x for x in range(4)]
    base += list(range(O_X + 20 * 1024, ARENA - 511, 512))
    names = iter(base)

    def temp():
        return A.at(next(names), 8, C)

    def flat(x):
        return x.rearrange("p a b -> p (a b)")

    AR = A.at(O_X + 12 * 1024, 2, 8, C)
    AMV = A.at(O_X + 18 * 1024, 8, 2, C)
    GH = A.at(O_X + 19 * 1024, 8, 2, C)
    LW, E0, E1, E2, KM, Bf, Kf, Kc = (temp() for _ in range(8))
    Bc = LW
    Vt, Bt, Kt = (temp() for _ in range(3))
    V_IN = temp()
    MT, RB, RK = (temp() for _ in range(3))
    N1, L1, L32, L64 = (temp() for _ in range(4))
    L2, N2, L4, N4, L8 = (temp() for _ in range(5))
    Z, TT, X = (temp() for _ in range(3))
    DG = E0

    def bc(ap):
        return ap.unsqueeze(1).to_broadcast([P, 8, C])

    def bank(b):
        return PS[:, b, :].rearrange("p (a n) -> p a n", n=C)

    def wide(b):
        return PS[:, b:b + 2, :].rearrange("p b (a x n) -> p (b a) x n", x=2, n=C)

    def split(b):
        return PS[:, b:b + 2, 0:4 * C].rearrange("p s (m n) -> p s m n", n=C)

    def duo(b):
        return PS[:, b:b + 2, :].rearrange("p s (m x n) -> p s m x n", x=2, n=C)

    def halves(x):
        return x.rearrange("p (m s) n -> p s m n", s=2)

    def bc3(ap):
        return ap.unsqueeze(1).unsqueeze(1).to_broadcast([P, 2, 4, C])

    def dual(b, m):
        return PS[:, b, m * P:(m + 1) * P]

    units = [(m, h, c) for m in range(4) for h in range(2) for c in range(2)]
    rows = lambda x: slice(64 * x, 64 * x + 64)
    W_LAST = E1[:, :, C - 1:C].to_broadcast([P, 8, C])

    with ExitStack() as ctx:
        sem = ctx.enter_context(cleared_semaphores(nc, "r_"))
        block = ctx.enter_context(nc.Block())

        @block.gpsimd
        def _(pool):
            with pool.Fori(0, 8) as it:
                pool.wait_ge(sem("t_v"), it)
                pool.tensor_copy(flat(V_IN), V8[:, it, :]).then_inc(sem("v_in"), 1)

        @block.scalar
        def _(act):
            with act.Fori(0, 8) as it:
                def wait(n):
                    act.wait_ge(sem(n), it + 1)

                def copy(dst, src, done):
                    act.activation(dst, src, ACT.Copy).then_inc(sem(done), 1)

                wait("lw")
                act.activation(E2, LW, ACT.Exp, scale=-1.0).then_inc(sem("e2"), 1)
                act.activation(E1, LW, ACT.Exp).then_inc(sem("e1"), 1)
                wait("lwx")
                act.activation(E0, E0, ACT.Exp).then_inc(sem("e0"), 1)
                wait("t_v")
                copy(flat(Vt), PS[:, 6, :], "v_out")
                wait("t_b")
                copy(flat(Bt), PS[:, 7, :], "b_out")
                wait("t_k")
                copy(flat(Kt), PS[:, 2, :], "k_out")
                wait("t_a")
                copy(AMV[:, :, 0, :], bank(3), "a_out")
                for src, dst, b in (("l2", L2, 6), ("l4", L4, 6), ("l8", L8, 6), ("t4", TT, 7), ("t5", TT, 7)):
                    wait("p_" + src)
                    copy(dst, bank(b), src)
                wait("p_mv")
                copy(AMV[:, :, 1, :], bank(5), "mv")
                wait("p_gh")
                copy(GH, wide(0), "gh")
                wait("p_y0")
                copy(halves(K8[:, it, :].rearrange("p (a b) -> p a b", b=C)), split(4), "y0")
                wait("p_q")
                copy(halves(A8[:, it, :].rearrange("p (a b) -> p a b", b=C)), split(0), "qq")

        @block.vector
        def _(dve):
            with dve.Fori(0, 8) as it:
                def wait(n):
                    dve.wait_ge(sem(n), it + 1)

                def mul(dst, a, b, done):
                    dve.tensor_tensor(dst, a, b, ALU.mult).then_inc(sem(done), 1)

                def add(dst, a, b, done):
                    dve.tensor_tensor(dst, a, b, ALU.add).then_inc(sem(done), 1)

                def eight(x):
                    return x[:, it, :].rearrange("p (a b) -> p a b", b=C)

                dve.tensor_tensor_scan(flat(LW), cst(A, "scan"), D8[:, it, :], 0.0, ALU.mult,
                                       ALU.add).then_inc(sem("lw"), 1)
                wait("lw")
                dve.tensor_tensor(flat(E0), flat(LW), D8[:, it, :], ALU.subtract).then_inc(sem("lwx"), 1)
                dve.tensor_scalar(flat(KM), A8[:, it, :], -1.0, A.at(O_PAR + KA, 8)[:, bass.ds(it, 1)],
                                  ALU.add, ALU.mult).then_inc(sem("kmt"), 1)
                wait("kmt")
                dve.scalar_tensor_tensor(flat(KM), flat(KM), 1.0, K8[:, it, :], ALU.add,
                                         ALU.mult).then_inc(sem("km"), 1)
                wait("e2")
                dve.tensor_tensor(Bf, eight(KN8), eight(A8), ALU.mult).then_inc(sem("bonus"), 1)
                wait("km")
                mul(Kf, KM, E2, "kh")
                dve.wait_ge(sem("bonus"), 2 * it + 1)
                mul(Bf, Bf, E2, "bh")
                wait("e1")
                mul(AR[:, 1], eight(R8), E1, "rh")
                wait("e0")
                dve.scalar_tensor_tensor(AR[:, 0], eight(KN8), -1.0, E0, ALU.mult,
                                         ALU.mult).then_inc(sem("ah"), 1)
                wait("kh")
                wait("bh")
                dve.scalar_tensor_tensor(flat(E2), R8[:, it, :], A.at(O_PAR + RKP, 8)[:, bass.ds(it, 1)], flat(KM),
                                         ALU.mult, ALU.mult).then_inc(sem("rk_in"), 1)
                mul(Bc, Bf, W_LAST, "bc")
                mul(Kc, Kf, W_LAST, "kc")
                wait("ah")
                mul(DG, bc(cst(A, "ident64")), W_LAST, "dg")
                wait("p_nrb")
                dve.tensor_tensor(halves(N1), duo(0)[:, :, :, 0, :], bc3(cst(A, "u_d")), ALU.mult)
                mul(halves(RB), duo(0)[:, :, :, 1, :], bc3(cst(A, "u_le")), "nrb_out")
                wait("p_l")
                for dst, name in ((L1, "l_d"), (L32, "l_32")):
                    dve.tensor_tensor(halves(dst), split(2), bc3(cst(A, name)), ALU.mult)
                mul(halves(L64), split(2), bc3(cst(A, "l_64")), "l_out")
                wait("nrb_out")
                add(Z, N1, bc(cst(A, "ident64")), "z1")
                wait("p_mrk")
                dve.tensor_tensor(halves(MT), duo(4)[:, :, :, 0, :], bc3(cst(A, "u_lt")), ALU.mult)
                mul(halves(RK), duo(4)[:, :, :, 1, :], bc3(cst(A, "u_le")), "mrk_out")
                wait("bonus_sum")
                wait("v_in")
                dve.tensor_tensor(V8[:, it, :], PS[:, 4, :], V8[:, it, :], ALU.mult).then_inc(sem("bonus"), 1)

                def power(name, dst):
                    wait("p_" + name)
                    dve.tensor_copy(dst, bank(0)).then_inc(sem(name), 1)

                def to_z(name):
                    wait("p_" + name)
                    add(Z, Z, bank(1), name)

                power("n2", N2)
                to_z("z2")
                power("n4", N4)
                to_z("z3")
                to_z("z4")
                power("x", X)
                to_z("z5")
                power("x2", X)
                to_z("z6")
                wait("p_r2")
                add(halves(eight(R8)), halves(AR[:, 1]), split(2), "r2")
                wait("p_p")
                add(halves(eight(D8)), halves(DG), split(6), "pp")

        @block.tensor
        def _(pe):
            with pe.Fori(0, 8) as it:
                def wait(n):
                    pe.wait_ge(sem(n), it + 1)

                def before(n):
                    pe.wait_ge(sem(n), it)

                def started():
                    pe.sem_inc(sem("begun"), 1)

                def token(out_bank, lhs, rhs, done):
                    started()
                    for m, h, c in units:
                        last = pe.matmul(bank(out_bank)[rows(c), 2 * m + h, :], lhs[rows(c), 2 * m + h, :],
                                         rhs[rows(c), 2 * m + h, :], start=True, stop=True)
                    last.then_inc(sem(done), 1)

                def turn(out_bank, src, done):
                    for m in range(4):
                        last = pe.transpose(dual(out_bank, m), src[:, 2 * m:2 * m + 2, :], cst(A, "ident"))
                    last.then_inc(sem(done), 1)

                wait("ah")
                wait("bh")
                wait("rh")
                before("qq")
                started()
                for m, h, c in units:
                    last = pe.matmul(duo(0)[rows(c), h, m, :, :], Bf[rows(h), 2 * m + c, :],
                                     AR[rows(h), :, 2 * m + c, :], start=True, stop=True)
                last.then_inc(sem("p_nrb"), 1)
                before("r2")
                started()
                for m, h, c in units:
                    last = pe.matmul(split(2)[rows(c), h, m, :], AR[rows(h), 0, 2 * m + c, :],
                                     Bf[rows(h), 2 * m + c, :], start=True, stop=True)
                last.then_inc(sem("p_l"), 1)
                wait("kh")
                before("y0")
                started()
                for m, h, c in units:
                    last = pe.matmul(duo(4)[rows(c), h, m, :, :], Kf[rows(h), 2 * m + c, :],
                                     AR[rows(h), :, 2 * m + c, :], start=True, stop=True)
                last.then_inc(sem("p_mrk"), 1)
                wait("v_in")
                before("pp")
                for m in range(4):
                    last = pe.transpose(dual(6, m), V_IN[:, 2 * m:2 * m + 2, :], cst(A, "ident"))
                last.then_inc(sem("t_v"), 1)
                wait("bc")
                turn(7, Bc, "t_b")
                wait("kc")
                wait("l_out")
                turn(2, Kc, "t_k")
                for m in range(4):
                    last = pe.transpose(dual(3, m), AR[:, 0, 2 * m:2 * m + 2, :], cst(A, "ident"))
                last.then_inc(sem("t_a"), 1)
                wait("mrk_out")
                wait("rk_in")
                pe.matmul(PS[:, 4, :], cst(A, "blockones"), flat(E2), start=True, stop=True).then_inc(sem("bonus_sum"), 1)
                wait("nrb_out")
                wait("v_out")
                token(6, N1, L1, "p_l2")
                token(0, L1, N1, "p_n2")
                wait("z1")
                wait("l2")
                token(1, L2, Z, "p_z2")
                wait("n2")
                token(6, N2, L2, "p_l4")
                token(0, L2, N2, "p_n4")
                wait("v_out")
                token(5, MT, Vt, "p_mv")
                wait("l4")
                wait("z2")
                token(1, L4, Z, "p_z3")
                wait("n4")
                token(6, N4, L4, "p_l8")
                wait("l8")
                wait("z3")
                token(1, L8, Z, "p_z4")
                wait("z4")
                token(0, L32, Z, "p_x")
                wait("b_out")
                started()
                for m, h, c in units:
                    last = pe.matmul(bank(7)[rows(c), 2 * m + h, :], Z[rows(c), 2 * m + h, :],
                                     cst(A, "ident64")[rows(c), :], start=True, stop=True)
                last.then_inc(sem("p_t4"), 1)
                wait("x")
                wait("t4")
                token(1, TT, X, "p_z5")
                wait("z5")
                token(0, L64, Z, "p_x2")
                started()
                for m, h, c in units:
                    last = pe.matmul(bank(7)[rows(c), 2 * m + h, :], Z[rows(c), 2 * m + h, :],
                                     cst(A, "ident64")[rows(c), :], start=True, stop=True)
                last.then_inc(sem("p_t5"), 1)
                wait("x2")
                wait("t5")
                token(1, TT, X, "p_z6")
                wait("z6")
                wait("mv")
                wait("a_out")
                started()
                for m, h, c in units:
                    last = pe.matmul(wide(0)[rows(c), 2 * m + h, :, :], Z[rows(c), 2 * m + h, :],
                                     AMV[rows(c), 2 * m + h, :, :], start=True, stop=True)
                last.then_inc(sem("p_gh"), 1)
                wait("k_out")
                wait("gh")
                started()
                for m, h, c in units:
                    last = pe.matmul(split(2)[rows(h), c, m, :], GH[rows(c), 2 * m + h, 0, :],
                                     RB[rows(c), 2 * m + h, :], start=True, stop=True)
                last.then_inc(sem("p_r2"), 1)
                pe.wait_ge(sem("bonus"), 2 * it + 2)
                started()
                for m, h, c in units:
                    pe.matmul(split(4)[rows(h), c, m, :], GH[rows(c), 2 * m + h, 1, :],
                              RB[rows(c), 2 * m + h, :], start=True, stop=False)
                    last = pe.matmul(split(4)[rows(h), c, m, :], Vt[rows(c), 2 * m + h, :],
                                     RK[rows(c), 2 * m + h, :], start=False, stop=True)
                last.then_inc(sem("p_y0"), 1)
                started()
                for m, h, c in units:
                    last = pe.matmul(split(6)[rows(h), c, m, :], GH[rows(c), 2 * m + h, 0, :],
                                     Bt[rows(c), 2 * m + h, :], start=True, stop=True)
                last.then_inc(sem("p_p"), 1)
                started()
                for m, h, c in units:
                    pe.matmul(split(0)[rows(h), c, m, :], Bt[rows(c), 2 * m + h, :],
                              GH[rows(c), 2 * m + h, 1, :], start=True, stop=False)
                    last = pe.matmul(split(0)[rows(h), c, m, :], Kt[rows(c), 2 * m + h, :],
                                     Vt[rows(c), 2 * m + h, :], start=False, stop=True)
                last.then_inc(sem("p_q"), 1)


def rwkv_scan(nc, A, PS, RJ, DEC, AA):
    S = A.at(O_NSA + 4 * 1024, 2, PAIRS, C)
    chunk = lambda x, n: x[:, 0:PAIRS, n * C:(n + 1) * C]
    with (nc.semaphore("s_moved") as moved, nc.semaphore("s_state") as state, nc.semaphore("s_read") as read,
          nc.semaphore("s_y") as y_done, nc.Block() as block):
        @block.tensor
        def _(pe):
            for n in range(NCH):
                pe.wait_ge(state, n + 1)
                P_, R_ = chunk(DEC, n), chunk(RJ, n)
                if n < NCH - 1:
                    for j in range(PAIRS):
                        for h in range(2):
                            r = slice(64 * h, 64 * h + 64)
                            last = pe.matmul(PS[r, n % 2, j * C:(j + 1) * C], P_[r, j, :], S[r, n % 2, j, :],
                                             start=True, stop=True)
                    last.then_inc(moved, 1)
                if n >= 2:
                    pe.wait_ge(y_done, n - 1)
                for j in range(PAIRS):
                    for h in range(2):
                        r = slice(64 * h, 64 * h + 64)
                        last = pe.matmul(PS[r, 2 + n % 2, j * C:(j + 1) * C], S[r, n % 2, j, :], R_[r, j, :],
                                         start=True, stop=True)
                last.then_inc(read, 1)

        @block.vector
        def _(dve):
            dve.memset(S[:, 0], 0.0).then_inc(state, 1)

            def out(n):
                dve.wait_ge(read, n + 1)
                y0 = chunk(RJ[:, 4:8, :], n)
                dve.tensor_tensor(y0, y0, PS[:, 2 + n % 2, 0:PAIRS * C].rearrange("p (a b) -> p a b", b=C),
                                  ALU.add).then_inc(y_done, 1)

            for n in range(NCH):
                if n < NCH - 1:
                    dve.wait_ge(moved, n + 1)
                    if n >= 1:
                        dve.wait_ge(read, n)
                    dve.tensor_tensor(S[:, (n + 1) % 2], PS[:, n % 2, 0:PAIRS * C].rearrange("p (a b) -> p a b", b=C),
                                      chunk(AA, n), ALU.add).then_inc(state, 1)
                out(n)


def rwkv_out(nc, A, PS, RJ, g_in):
    GUP = A.at(O_VT, HALF)
    W = A.at(O_U, 8, HALF)
    with ExitStack() as ctx:
        sem = lambda n: ctx.enter_context(nc.semaphore("g_" + n))
        loaded, mean, centred, squared, var, root, inverse, gate, out, step = (
            sem(x) for x in ("loaded", "mean", "centred", "squared", "var", "root", "inverse", "gate", "out", "step"))
        block = ctx.enter_context(nc.Block())
        units = [(j, slice(h * HALF, (h + 1) * HALF)) for j in range(PAIRS) for h in range(2)]

        @block.sync
        def _(sp):
            sp.dma_start(GUP, g_in).then_inc(loaded, 16)

        @block.tensor
        def _(pe):
            pe.wait_ge(loaded, 16)
            for n in range(len(units) + 1):
                if n < len(units):
                    j, cols = units[n]
                    if n >= 2:
                        pe.wait_ge(centred, n - 1)
                    pe.matmul(PS[:, n % 2, :], cst(A, "blockones"), RJ[:, 4 + j, cols], start=True, stop=True).then_inc(mean, 1)
                if n >= 1:
                    k = n - 1
                    j, cols = units[k]
                    pe.wait_ge(squared, k + 1)
                    if k >= 2:
                        pe.wait_ge(root, k - 1)
                        pe.wait_ge(out, k - 1)
                    pe.matmul(PS[:, 2 + k % 2, :], cst(A, "blockones"), W[:, k % 2, :], start=True, stop=True).then_inc(var, 1)
                    pe.matmul(PS[:, 4 + k % 2, :], GUP[:, j * P:(j + 1) * P], RJ[:, 13, cols], start=True,
                              stop=True).then_inc(gate, 1)

        @block.scalar
        def _(act):
            for n, (j, cols) in enumerate(units):
                act.wait_ge(centred, n + 1)
                if n >= 2:
                    act.wait_ge(var, n - 1)
                act.activation(W[:, n % 2, :], RJ[:, 4 + j, cols], ACT.Square).then_inc(squared, 1)
                act.wait_ge(var, n + 1)
                if n >= 2:
                    act.wait_ge(out, n - 1)
                act.activation(W[:, 2 + n % 2, :], PS[:, 2 + n % 2, :], ACT.Sqrt, scale=1.0 / HD,
                               bias=cst(A, "gneps")).then_inc(root, 1)

        @block.vector
        def _(dve):
            def centre(n):
                j, cols = units[n]
                dve.wait_ge(mean, n + 1)
                dve.scalar_tensor_tensor(RJ[:, 4 + j, cols], PS[:, n % 2, :], -1.0 / HD, RJ[:, 4 + j, cols],
                                         ALU.mult, ALU.add).then_inc(centred, 1)

            centre(0)
            for n, (j, cols) in enumerate(units):
                if n + 1 < len(units):
                    centre(n + 1)
                dve.wait_ge(root, n + 1)
                R = W[:, 2 + n % 2, :]
                Y = RJ[:, 4 + j, cols]
                dve.reciprocal(R, R).then_inc(inverse, 1)
                dve.wait_ge(inverse, n + 1)
                dve.scalar_tensor_tensor(Y, Y, par(A, LNW + j), R, ALU.mult, ALU.mult).then_inc(step, 1)
                dve.wait_ge(step, 2 * n + 1)
                dve.scalar_tensor_tensor(Y, Y, par(A, LNB + j), RJ[:, 8 + j, cols], ALU.add, ALU.add).then_inc(step, 1)
                dve.wait_ge(step, 2 * n + 2)
                dve.wait_ge(gate, n + 1)
                dve.tensor_tensor(Y, Y, PS[:, 4 + n % 2, :], ALU.mult).then_inc(out, 1)


def reload_norm(nc, A, PS, x_in, X, U):
    RSTD = A.at(O_RSTD, 1024)
    with (nc.semaphore("l_x") as loaded, nc.Block() as block):
        @block.sync
        def _(sp):
            sp.dma_start(X, x_in.rearrange("(c p) t -> p c t", p=P)).then_inc(loaded, 16)

        @block.vector
        def _(dve):
            dve.wait_ge(loaded, 16)
            for c in range(KC):
                dve.scalar_tensor_tensor(U[:, c, :], X[:, c, :], par(A, MIXN + c), RSTD, ALU.mult, ALU.mult)


def merge(nc, A, PS, w_in, U, YA, YB, M):
    KS = (KC, PAIRS, KC, PAIRS)
    AT = (0, 8, 12, 20)
    W = A.at(O_NSA + 4 * 1024, 2, 24, P)
    G = A.at(O_NSA + 4 * 1024 + 2 * 24 * P, 4, HALF)
    SRC = (U, YA, U, YB)
    with ExitStack() as ctx:
        sem = lambda n: ctx.enter_context(nc.semaphore("e_" + n))
        loaded = [sem("loaded0"), sem("loaded1")]
        product = [sem("product0"), sem("product1")]
        tanh = [sem("tanh0"), sem("tanh1")]
        part = [sem("part0"), sem("part1")]
        merged = [sem("merged0"), sem("merged1")]
        block = ctx.enter_context(nc.Block())

        @block.sync
        def _(sp):
            for s in range(2):
                sp.dma_start(W[:, s], w_in[s].rearrange("p (c n) -> p c n", n=P)).then_inc(loaded[s], 16)
            with sp.Fori(0, KC // 2 - 1) as i:
                for s in range(2):
                    sp.wait_ge(product[1], 2 * i + s + 1)
                    sp.dma_start(W[:, s], w_in[2 * i + 2 + s].rearrange("p (c n) -> p c n", n=P)).then_inc(loaded[s], 16)

        @block.tensor
        def _(pe):
            with pe.Fori(0, KC // 2) as i:
                for s in range(2):
                    pe.wait_ge(loaded[s], 16 * i + 16)
                    for h in range(2):
                        pe.wait_ge(merged[h], 2 * i + s)
                        for x in range(4):
                            for c in range(KS[x]):
                                last = pe.matmul(PS[:, 4 * h + x, :], W[:, s, AT[x] + c, :],
                                                 SRC[x][:, c, h * HALF:(h + 1) * HALF],
                                                 start=c == 0, stop=c == KS[x] - 1)
                        last.then_inc(product[h], 1)

        @block.scalar
        def _(act):
            with act.Fori(0, KC) as n:
                for h in range(2):
                    act.wait_ge(product[h], n + 1)
                    for x in range(2):
                        act.activation(G[:, 2 * h + x, :], PS[:, 4 * h + 2 * x, :], ACT.Tanh,
                                       scale=0.5).then_inc(tanh[h], 1)

        @block.vector
        def _(dve):
            with dve.Fori(0, KC) as n:
                for h in range(2):
                    dve.wait_ge(tanh[h], 2 * n + 2)
                    for x in range(2):
                        dve.scalar_tensor_tensor(G[:, 2 * h + x, :], G[:, 2 * h + x, :], 1.0, PS[:, 4 * h + 2 * x + 1, :],
                                                 ALU.add, ALU.mult).then_inc(part[h], 1)
                    dve.wait_ge(part[h], 2 * n + 2)
                    dve.tensor_tensor(M[:, n, h * HALF:(h + 1) * HALF], G[:, 2 * h, :], G[:, 2 * h + 1, :],
                                      ALU.add).then_inc(merged[h], 1)


def project_out(nc, A, PS, w_in, M, X):
    W = A.at(O_NSA + 4 * 1024, 2, KC, P)
    with ExitStack() as ctx:
        sem = lambda n: ctx.enter_context(nc.semaphore("o_" + n))
        loaded = [sem("loaded0"), sem("loaded1")]
        product = [sem("product0"), sem("product1")]
        added = [sem("added0"), sem("added1")]
        block = ctx.enter_context(nc.Block())

        @block.sync
        def _(sp):
            for s in range(2):
                sp.dma_start(W[:, s], w_in[s].rearrange("p (c n) -> p c n", n=P)).then_inc(loaded[s], 16)
            with sp.Fori(0, KC // 2 - 1) as i:
                for s in range(2):
                    sp.wait_ge(product[s], 2 * i + 2)
                    sp.dma_start(W[:, s], w_in[2 * i + 2 + s].rearrange("p (c n) -> p c n", n=P)).then_inc(loaded[s], 16)

        @block.tensor
        def _(pe):
            with pe.Fori(0, KC // 2) as i:
                for s in range(2):
                    pe.wait_ge(loaded[s], 16 * i + 16)
                    for h in range(2):
                        pe.wait_ge(added[s], 2 * i)
                        for c in range(KC):
                            last = pe.matmul(PS[:, 2 * s + h, :], W[:, s, c, :], M[:, c, h * HALF:(h + 1) * HALF],
                                             start=c == 0, stop=c == KC - 1)
                        last.then_inc(product[s], 1)

        @block.vector
        def _(dve):
            with dve.Fori(0, KC // 2) as i:
                for s in range(2):
                    for h in range(2):
                        cols = slice(h * HALF, (h + 1) * HALF)
                        dve.wait_ge(product[s], 2 * i + h + 1)
                        dve.scalar_tensor_tensor(X[:, 2 * i + s, cols], PS[:, 2 * s + h, :], 0.5, X[:, 2 * i + s, cols],
                                                 ALU.mult, ALU.add).then_inc(added[s], 1)


def norm_again(nc, A, PS, X, H):
    SQ = A.at(O_NSA, 2, 1024)
    R = A.at(O_RSTD, 1024)
    with (nc.semaphore("f_sq") as squared, nc.semaphore("f_sum") as summed, nc.semaphore("f_rms") as rms,
          nc.semaphore("f_rs") as rs, nc.Block() as block):
        @block.scalar
        def _(act):
            for c in range(KC):
                if c >= 2:
                    act.wait_ge(summed, c - 1)
                act.activation(SQ[:, c % 2, :], X[:, c, :], ACT.Square).then_inc(squared, 1)
            act.wait_ge(summed, KC)
            act.activation(R, PS[:, 0:2, :], ACT.Sqrt, scale=1.0 / D, bias=cst(A, "eps")).then_inc(rms, 1)

        @block.tensor
        def _(pe):
            for c in range(KC):
                pe.wait_ge(squared, c + 1)
                for h in range(2):
                    last = pe.matmul(PS[:, h, :], cst(A, "ones"), SQ[:, c % 2, h * HALF:(h + 1) * HALF],
                                     start=c == 0, stop=c == KC - 1)
                last.then_inc(summed, 1)

        @block.vector
        def _(dve):
            dve.wait_ge(rms, 1)
            dve.reciprocal(R, R).then_inc(rs, 1)
            dve.wait_ge(rs, 1)
            for c in range(KC):
                dve.scalar_tensor_tensor(H[:, c, :], X[:, c, :], par(A, FFNN + c), R, ALU.mult, ALU.mult)


def mlp(nc, A, PS, w_in, H, X, out):
    GROUPS = DFF // 1024
    W = A.at(O_NSA, 2, KC, P)
    R = A.at(O_NSA + 2048, 4, HALF)
    F = A.at(O_X, KC, 1024)
    with ExitStack() as ctx:
        sem = lambda n: ctx.enter_context(nc.semaphore("p_" + n))
        loaded = [sem("loaded0"), sem("loaded1")]
        product = [sem("product0"), sem("product1")]
        relu = [sem("relu0"), sem("relu1")]
        inner = [sem("inner0"), sem("inner1")]
        added = [sem("added0"), sem("added1")]
        stored = sem("stored")
        begun = sem("begun")
        block = ctx.enter_context(nc.Block())

        @block.sync
        def _(sp):
            for s in range(2):
                sp.dma_start(W[:, s], w_in[s].rearrange("p (c n) -> p c n", n=P)).then_inc(loaded[s], 16)
            with sp.Fori(0, 8 * GROUPS - 1) as i:
                for s in range(2):
                    sp.wait_ge(product[s], 2 * i + 2)
                    sp.dma_start(W[:, s], w_in[2 * i + 2 + s].rearrange("p (c n) -> p c n", n=P)).then_inc(loaded[s], 16)
            for s in range(2):
                sp.wait_ge(added[s], 8 * GROUPS)
            sp.dma_start(out.rearrange("(c p) t -> p c t", p=P), X).then_inc(stored, 16)
            sp.wait_ge(stored, 16)

        @block.tensor
        def _(pe):
            def tile(s, src, n, free):
                pe.wait_ge(loaded[s], 16 * n + 16)
                for h in range(2):
                    for sem_, count in free(s, h):
                        pe.wait_ge(sem_, count)
                    for c in range(KC):
                        last = pe.matmul(PS[:, 2 * s + h, :], W[:, s, c, :], src[:, c, h * HALF:(h + 1) * HALF],
                                         start=c == 0, stop=c == KC - 1)
                    last.then_inc(product[s], 1)

            with pe.Fori(0, GROUPS) as g:
                with pe.Fori(0, 4) as i:
                    for s in range(2):
                        tile(s, H, 8 * g + i, lambda s, h: [(inner[s], 8 * g + 2 * i), (added[s], 8 * g)])
                for s in range(2):
                    pe.wait_ge(inner[s], 8 * g + 8)
                pe.sem_inc(begun, 1)
                with pe.Fori(0, 4) as i:
                    for s in range(2):
                        tile(s, F, 8 * g + 4 + i, lambda s, h: [(added[s], 8 * g + 2 * i)])

        @block.scalar
        def _(act):
            with act.Fori(0, GROUPS) as g:
                with act.Fori(0, 4) as i:
                    for s in range(2):
                        for h in range(2):
                            act.wait_ge(product[s], 16 * g + 2 * i + h + 1)
                            act.wait_ge(inner[s], 8 * g + 2 * i)
                            act.activation(R[:, 2 * s + h, :], PS[:, 2 * s + h, :], ACT.Relu).then_inc(relu[s], 1)

        @block.vector
        def _(dve):
            with dve.Fori(0, GROUPS) as g:
                with dve.Fori(0, 4) as i:
                    for s in range(2):
                        for h in range(2):
                            dve.wait_ge(relu[s], 8 * g + 2 * i + h + 1)
                            dve.tensor_tensor(F[:, 2 * i + s, h * HALF:(h + 1) * HALF], PS[:, 2 * s + h, :],
                                              R[:, 2 * s + h, :], ALU.mult).then_inc(inner[s], 1)
                with dve.Fori(0, 4) as i:
                    for s in range(2):
                        for h in range(2):
                            cols = slice(h * HALF, (h + 1) * HALF)
                            dve.wait_ge(product[s], 16 * g + 8 + 2 * i + h + 1)
                            dve.tensor_tensor(X[:, 2 * i + s, cols], PS[:, 2 * s + h, :], X[:, 2 * i + s, cols],
                                              ALU.add).then_inc(added[s], 1)


def layer(nc, x, cst_in, par_in, w_nsa, w_tok, w1, w2, pos, w_rw, lora, g_up, w_merge, w_out, w_mlp, out, debug=None, stage=None):
    with nc.sbuf_tensor("arena", [P, ARENA], F32) as arena, nc.psum_tensor("psum", [P, 8, HALF], F32) as psum:
        A = Arena(arena)
        PS = psum
        NSA = A.at(O_NSA, 8, 1024)
        VT = A.at(O_VT, 8, TOKC)
        U = A.at(O_U, 8, 1024)
        load_and_norm(nc, A, PS, x, cst_in, par_in)
        project(nc, A, PS, w_nsa, NSA_TILES, NSA, U, "nsa")
        project_tokens(nc, A, PS, w_tok, VT, U)
        KPC = A.at(ARENA - 300, 2, NCMP)
        VC = A.at(ARENA - 150, 2, HD)
        compress(nc, A, PS, NSA, KPC, VC, w1, w2, pos)
        KPAD = A.at(O_X + 2048, 4, 1024)
        norm_heads(nc, A, PS, NSA, KPAD)
        attention(nc, A, PS, NSA, KPAD, KPC, VT, VC)
        RJ = A.at(O_X, RW_TILES, 1024)
        KN = A.at(O_X + RW_TILES * 1024, PAIRS, 1024)
        DEC = A.at(O_U, PAIRS, 1024)
        AA = A.at(O_U + 4096, PAIRS, 1024)
        project(nc, A, PS, w_rw, RW_TILES, RJ, U, "rw")
        mix_and_lora(nc, A, PS, RJ, DEC, AA, KN, lora)
        if stage == "mix":
            debug(nc, A, dict(RJ=RJ, DEC=DEC, AA=AA, KN=KN))
            return
        rwkv_chunks(nc, A, PS, RJ, DEC, AA, KN)
        rwkv_scan(nc, A, PS, RJ, DEC, AA)
        rwkv_out(nc, A, PS, RJ, g_up)
        if not debug:
            X = A.at(O_X + 8 * 1024, 8, 1024)
            M = A.at(O_X + 16 * 1024, 8, 1024)
            reload_norm(nc, A, PS, x, X, U)
            merge(nc, A, PS, w_merge, U, NSA, RJ[:, 4:8, :], M)
            project_out(nc, A, PS, w_out, M, X)
            norm_again(nc, A, PS, X, U)
            mlp(nc, A, PS, w_mlp, U, X, out)
        if debug:
            debug(nc, A, dict(RJ=RJ, NSA=NSA, VT=VT, U=U, KPC=KPC, VC=VC, KPAD=KPAD))


def tiles(w):
    k, n = w.shape
    return np.ascontiguousarray(w.reshape(k // P, P, n // P, P).transpose(2, 1, 0, 3).reshape(n // P, P, -1))


def cols(v):
    return np.asarray(v).reshape(-1, P).T


def host_layout(x, mix_norm, w_in, q_gain, k_gain, cmp_pos, cmp_w1, cmp_w2, w_attn_branch, tok_mix, w0, w_lora_up,
                a0, a_lora_up, g_lora_up, k_k, k_a, r_k, ln_x_w, ln_x_b, w_rwkv_branch, w_out, ffn_norm,
                w_ffn_up, w_ffn_down):
    W = np.asarray(w_in)[0]
    q = [np.concatenate([W[:, HD * j:HD * j + HD], W[:, HD * (j + 4):HD * (j + 4) + HD]], 1) for j in range(PAIRS)]
    kc, vc, ks, vs, kw, vw = (W[:, 512 + P * i:640 + P * i] for i in range(6))
    gates = W[:, 1280:1304]
    ga, gb = W[:, -2 * D:-D], W[:, -D:]
    wa = np.asarray(w_attn_branch[0]).reshape(2, PAIRS, HD, D).transpose(1, 0, 2, 3).reshape(-1, D)
    two = lambda v: np.concatenate([v, v])
    twice = lambda v: np.repeat(cols(v), 2, axis=1)
    params = np.concatenate([
        cols(mix_norm[0]), cols(ffn_norm[0]), cols(two(q_gain[0])), *(cols(two(k_gain[0, i])) for i in range(3)),
        cols(tok_mix[0]), cols(w0[0]), cols(a0[0]), twice(k_k[0]), twice(k_a[0]), twice(r_k[0].reshape(-1)),
        cols(ln_x_w[0]), cols(ln_x_b[0])], 1)
    wtok = np.concatenate([vs, vw, gates], 1)
    c = np.ascontiguousarray
    return {
        "x": c(x[0].T), "cst": constants(), "par": c(params),
        "w_nsa": tiles(np.concatenate(q + [ks, kw, kc, vc], 1)),
        "w_tok": c(wtok.reshape(KC, P, TOKC).transpose(1, 0, 2).reshape(P, -1)),
        "w1": c(cmp_w1[0].reshape(2, 32, HD, CMP_HID).transpose(2, 0, 1, 3)),
        "w2": c(cmp_w2[0].transpose(1, 0, 2)),
        "pos": c(cmp_pos[0].transpose(2, 0, 1)),
        "w_rw": tiles(W[:, NSA_COLS:NSA_COLS + RW_TILES * P]),
        "lora": c(np.concatenate([w_lora_up[0], a_lora_up[0]], 0)), "g_up": c(g_lora_up[0]),
        "w_merge": np.concatenate([tiles(ga), tiles(wa), tiles(gb), tiles(w_rwkv_branch[0])], 2),
        "w_out": tiles(w_out[0]), "w_mlp": np.concatenate([x for g in range(4) for x in (
            tiles(w_ffn_up[0][:, 1024 * g:1024 * g + 1024]), tiles(w_ffn_down[0][1024 * g:1024 * g + 1024]))]),
    }


def kernel(**inputs):
    import concourse.bacc as bacc
    from concourse.bass_utils import run_bass_kernel_spmd

    nc = bacc.Bacc("TRN2", target_bir_lowering=False, num_devices=1)
    arrays = host_layout(**{k: np.asarray(v) for k, v in inputs.items()})
    args = [nc.dram_tensor(n, a.shape, mybir.dt.from_np(a.dtype), kind="ExternalInput").ap() for n, a in arrays.items()]
    out = nc.dram_tensor("out", (D, T), F32, kind="ExternalOutput").ap()
    layer(nc, *args, out)
    r = run_bass_kernel_spmd(nc, [arrays], core_ids=[0])
    return np.ascontiguousarray(r.results[0]["out"].T)[None]
```

```python
import numpy as np
import concourse.bass as bass
from concourse import mybir
from contextlib import ExitStack, contextmanager

F32 = mybir.dt.float32
BF16 = mybir.dt.bfloat16
F32R = mybir.dt.float32r
ALU = mybir.AluOpType
ACT = mybir.ActivationFunctionType
AX = mybir.AxisListType

P = 128
T = 1024
D = 1024
KC = D // P
HALF = 512
NH = 8
HD = 64
PAIRS = NH // 2
NQT = T // P
WIN_TILES = 512 // P
NCMP = (T - 32) // 16 + 1
CMP_HID = 128
DFF = 4096
NSA_TILES = 8
RW_TILES = 14
C = 64
NCH = T // C
NSA_COLS = 1304
TOKC = 280
RMS_EPS = 1e-6
GN_EPS = 64e-5
DECAY_SCALE = float(np.exp(np.float64(-0.5)))
NEG = -1e30

MIXN, FFNN, QG, KG, MU, W0, A0, KK, KA, RKP, LNW, LNB, NPAR = 0, 8, 16, 17, 20, 34, 38, 42, 50, 58, 66, 70, 74
_c = {}
_n = 0
for _name, _w in (("ident", 128), ("ones", 128), ("blockones", 128), ("diagneg", 128), ("winneg", 128),
                  ("cmask", 8 * 63), ("flag", 1), ("u_d", 64), ("u_32", 64), ("u_64", 64), ("u_lt", 64),
                  ("u_le", 64), ("l_d", 64), ("l_32", 64), ("l_64", 64), ("ident64", 64), ("scan", 512),
                  ("eps", 1), ("gneps", 1)):
    _c[_name] = (_n, _w)
    _n += _w
NCST = _n


def constants():
    out = np.zeros((P, NCST), np.float32)

    def put(name, a):
        o, w = _c[name]
        out[:, o:o + w] = np.asarray(a).reshape(-1, w)

    p = np.arange(P)[:, None]
    f = np.arange(P)[None, :]
    put("ident", p == f)
    put("ones", np.ones((P, P)))
    put("blockones", p // HD == f // HD)
    put("diagneg", np.where(f > p, NEG, 0.0))
    put("winneg", np.where(f <= p, NEG, 0.0))
    n = np.arange(NCMP)[None, None, :]
    q = np.arange(NQT)[None, :, None] * P + np.arange(P)[:, None, None]
    put("cmask", np.where(16 * n + 31 <= q, 0.0, NEG))
    put("flag", p >= 31)
    s = p % C
    t = np.arange(C)[None, :]
    b16 = s // 16 == t // 16
    b32 = s // 32 == t // 32
    put("u_d", (s < t) & b16)
    put("u_32", (s < t) & ~b16 & b32)
    put("u_64", (s < t) & ~b32)
    put("u_lt", s < t)
    put("u_le", s <= t)
    put("l_d", (s > t) & b16)
    put("l_32", (s > t) & ~b16 & b32)
    put("l_64", (s > t) & ~b32)
    put("ident64", s == t)
    put("scan", np.broadcast_to(np.arange(512) % C != 0, (P, 512)))
    put("eps", np.full((P, 1), RMS_EPS))
    put("gneps", np.full((P, 1), GN_EPS))
    return out


@contextmanager
def cleared_semaphores(nc, prefix):
    made = {}

    def sem(name):
        if name not in made:
            made[name] = nc.alloc_semaphore(prefix + name)
        return made[name]

    yield sem
    nc.clear_and_free_semaphores(list(made.values()))
    nc.all_engine_barrier()


class Arena:

    def __init__(self, tensor):
        self.t = tensor

    def at(self, off, *shape):
        n = int(np.prod(shape))
        ap = self.t[:, off:off + n]
        if len(shape) == 1:
            return ap
        names = "abcd"[:len(shape)]
        kw = {x: s for x, s in zip(names, shape)}
        return ap.rearrange("p (" + " ".join(names) + ") -> p " + " ".join(names), **kw)


O_CST = 0
O_PAR = O_CST + NCST
O_SMALL = O_PAR + NPAR
O_RSTD = O_SMALL + 160
BASE = O_RSTD + 1024
O_VT = 8 * 1024
WORK = 22528


def par(A, i, n=1):
    return A.at(O_PAR + i, n)


def cst(A, name):
    o, w = _c[name]
    return A.at(O_CST + o, w)


def hi_of(x):
    return x[:, 0]


def lo_of(x):
    return x[:, 1]


def load_weights(sp, raw, w_in, loaded, split, n_pairs):
    def load(n, s):
        sp.dma_start(raw[:, s], w_in[n].rearrange("p (c n) -> p c n", n=P)).then_inc(loaded[s], 16)

    for s in range(2):
        load(s, s)
    with sp.Fori(1, n_pairs) as i:
        for s in range(2):
            sp.wait_ge(split[s], i)
            load(2 * i + s, s)


def split_weights(pool, raw, W, loaded, rounded, split, product, begun, n_pairs):
    def pair(i):
        for s in range(2):
            pool.wait_ge(loaded[s], 16 * i + 16)
            if not isinstance(i, int):
                pool.wait_ge(product[s], 2 * i)
                pool.sem_inc(begun, 1)
            pool.tensor_copy(W[:, s, 0], raw[:, s]).then_inc(rounded[s], 1)
            pool.wait_ge(rounded[s], i + 1)
            if not isinstance(i, int):
                pool.sem_inc(begun, 1)
            pool.tensor_tensor(W[:, s, 1], raw[:, s], W[:, s, 0].bitcast(F32), ALU.subtract).then_inc(split[s], 1)

    pair(0)
    with pool.Fori(1, n_pairs) as i:
        pair(i)


def three_passes(pe, out, W, s, x, cols, chunks=KC):
    for c in range(chunks):
        pe.matmul(out, W[:, s, 0, c, :], hi_of(x)[:, c, cols], start=c == 0, stop=False)
        pe.matmul(out, W[:, s, 0, c, :], lo_of(x)[:, c, cols], start=False, stop=False)
        last = pe.matmul(out, W[:, s, 1, c, :], hi_of(x)[:, c, cols], start=False, stop=c == chunks - 1)
    return last


def slot_semaphores(sem):
    return [[sem(f"{n}{s}") for s in range(2)] for n in ("loaded", "rounded", "split", "product")] + [sem("poolbegun")]


HALVES = [slice(h * HALF, (h + 1) * HALF) for h in range(2)]


def load_and_norm(nc, A, PS, x_in, cst_in, par_in, X, SQ, U):
    RSTD = A.at(O_RSTD, 1024)
    with (nc.semaphore("n_const") as const_in, nc.semaphore("n_x0") as x0, nc.semaphore("n_x1") as x1,
          nc.semaphore("n_sq") as squared, nc.semaphore("n_scaled") as scaled, nc.semaphore("n_hi") as hi,
          nc.semaphore("n_sum") as summed, nc.semaphore("n_rms") as rms, nc.semaphore("n_rs") as rs,
          nc.Block() as block):
        @block.sync
        def _(sp):
            sp.dma_start(A.at(O_CST, NCST), cst_in).then_inc(const_in, 16)
            sp.dma_start(A.at(O_PAR, NPAR), par_in).then_inc(const_in, 16)
            for c in range(KC):
                if c >= 2:
                    sp.wait_ge((x0, x1)[c % 2], 16 * (c // 2))
                sp.dma_start(X[:, c, :], x_in[c * P:(c + 1) * P, :]).then_inc((x0, x1)[c % 2], 16)

        @block.scalar
        def _(act):
            for c in range(KC):
                act.wait_ge((x0, x1)[c % 2], 16 * (c // 2 + 1))
                if c >= 2:
                    act.wait_ge(summed, c - 1)
                act.activation(SQ[:, c % 2, :], X[:, c, :], ACT.Square).then_inc(squared, 1)
            act.wait_ge(summed, KC)
            act.activation(RSTD, PS[:, 0:2, :], ACT.Sqrt, scale=1.0 / D, bias=cst(A, "eps")).then_inc(rms, 1)
            for c in range(KC):
                act.wait_ge(scaled, c + 1)
                act.activation(hi_of(U)[:, c, :], X[:, c, :], ACT.Copy).then_inc(hi, 1)

        @block.tensor
        def _(pe):
            pe.wait_ge(const_in, 32)
            for c in range(KC):
                pe.wait_ge(squared, c + 1)
                for h in range(2):
                    last = pe.matmul(PS[:, h, :], cst(A, "ones"), SQ[:, c % 2, HALVES[h]],
                                     start=c == 0, stop=c == KC - 1)
                last.then_inc(summed, 1)

        @block.vector
        def _(dve):
            dve.wait_ge(rms, 1)
            dve.reciprocal(RSTD, RSTD).then_inc(rs, 1)
            dve.wait_ge(rs, 1)
            for c in range(KC + 1):
                if c < KC:
                    dve.scalar_tensor_tensor(X[:, c, :], X[:, c, :], par(A, MIXN + c), RSTD, ALU.mult,
                                             ALU.mult).then_inc(scaled, 1)
                if c >= 1:
                    dve.wait_ge(hi, c)
                    dve.tensor_tensor(lo_of(U)[:, c - 1, :], X[:, c - 1, :], hi_of(U)[:, c - 1, :].bitcast(F32),
                                      ALU.subtract)


def project(nc, A, PS, w_in, n_tiles, OUT, U, raw, W, tag, gates=None):
    n_pairs = n_tiles // 2
    with ExitStack() as ctx:
        sem = ctx.enter_context(cleared_semaphores(nc, tag + "_"))
        loaded, rounded, split, product, begun = slot_semaphores(sem)
        free = [[sem(f"free{s}{h}") for h in range(2)] for s in range(2)]
        staged = [sem("staged0"), sem("staged1")]
        kept = [sem("kept0"), sem("kept1")]
        block = ctx.enter_context(nc.Block())

        @block.sync
        def _(sp):
            if not gates:
                load_weights(sp, raw, w_in, loaded, split, n_pairs)
                return

            def store(n, i, s):
                sp.wait_ge(staged[s], 2 * i + 2)
                sp.dma_start(gates[n], OUT[:, s, :]).then_inc(kept[s], 16)

            for s in range(2):
                sp.dma_start(raw[:, s], w_in[s].rearrange("p (c n) -> p c n", n=P)).then_inc(loaded[s], 16)
            with sp.Fori(1, n_pairs) as i:
                for s in range(2):
                    sp.wait_ge(split[s], i)
                    sp.dma_start(raw[:, s], w_in[2 * i + s].rearrange("p (c n) -> p c n", n=P)).then_inc(loaded[s], 16)
                for s in range(2):
                    store(2 * i - 2 + s, i - 1, s)
            for s in range(2):
                store(2 * n_pairs - 2 + s, n_pairs - 1, s)
            for s in range(2):
                sp.wait_ge(kept[s], 16 * n_pairs)

        @block.gpsimd
        def _(pool):
            split_weights(pool, raw, W, loaded, rounded, split, product, begun, n_pairs)

        @block.tensor
        def _(pe):
            with pe.Fori(0, n_pairs) as i:
                for s in range(2):
                    pe.wait_ge(split[s], i + 1)
                    for h in range(2):
                        pe.wait_ge(free[s][h], i + 1)
                        three_passes(pe, PS[:, 2 * s + h, :], W, s, U, HALVES[h]).then_inc(product[s], 1)

        @block.scalar
        def _(act):
            if not gates:
                for s in range(2):
                    act.sem_inc(free[s][0], 1)
                with act.Fori(0, n_pairs) as i:
                    for s in range(2):
                        act.wait_ge(product[s], 2 * i + 1)
                        act.activation(OUT[:, 2 * i + s, HALVES[0]], PS[:, 2 * s, :], ACT.Copy).then_inc(free[s][0], 1)
                return
            for s in range(2):
                for h in range(2):
                    act.sem_inc(free[s][h], 1)

            def pair(i):
                for s in range(2):
                    for h in range(2):
                        act.wait_ge(product[s], 2 * i + h + 1)
                        if not isinstance(i, int):
                            act.wait_ge(kept[s], 16 * i)
                        act.activation(OUT[:, s, HALVES[h]], PS[:, 2 * s + h, :], ACT.Tanh, scale=0.5).then_inc(staged[s], 1)
                        act.wait_ge(staged[s], 2 * i + h + 1)
                        act.sem_inc(free[s][h], 1)

            pair(0)
            with act.Fori(1, n_pairs) as i:
                pair(i)

        @block.vector
        def _(dve):
            if gates:
                return
            for s in range(2):
                dve.sem_inc(free[s][1], 1)
            with dve.Fori(0, n_pairs) as i:
                for s in range(2):
                    dve.wait_ge(product[s], 2 * i + 2)
                    dve.tensor_copy(OUT[:, 2 * i + s, HALVES[1]], PS[:, 2 * s + 1, :]).then_inc(free[s][1], 1)


def project_tokens(nc, A, PS, w_in, VT, U, RAW, W):
    with (nc.semaphore("t_loaded") as loaded, nc.semaphore("t_product") as product,
          nc.semaphore("t_out") as out, nc.semaphore("t_tanh") as tanh, nc.semaphore("t_hi") as hi,
          nc.semaphore("t_lo") as lo, nc.Block() as block):
        @block.sync
        def _(sp):
            sp.dma_start(RAW, w_in.rearrange("p (c n) -> p c n", c=KC)).then_inc(loaded, 16)

        @block.tensor
        def _(pe):
            pe.wait_ge(lo, 1)
            for t in range(NQT):
                cols = slice(t * P, (t + 1) * P)
                for c in range(KC):
                    pe.matmul(PS[:, t, 0:TOKC], hi_of(U)[:, c, cols], W[:, 0, c, :], start=c == 0, stop=False)
                    pe.matmul(PS[:, t, 0:TOKC], hi_of(U)[:, c, cols], W[:, 1, c, :], start=False, stop=False)
                    last = pe.matmul(PS[:, t, 0:TOKC], lo_of(U)[:, c, cols], W[:, 0, c, :], start=False,
                                     stop=c == KC - 1)
                last.then_inc(product, 1)

        @block.vector
        def _(dve):
            dve.wait_ge(hi, 1)
            dve.tensor_tensor(W[:, 1], RAW, W[:, 0].bitcast(F32), ALU.subtract).then_inc(lo, 1)
            for t in range(NQT):
                dve.wait_ge(product, t + 1)
                dve.tensor_copy(VT[:, t, :], PS[:, t, 0:TOKC]).then_inc(out, 1)
            dve.wait_ge(tanh, 1)
            dve.tensor_scalar(VT[:, :, 256:TOKC], VT[:, :, 256:TOKC], 0.5, 0.5, ALU.mult, ALU.add)

        @block.scalar
        def _(act):
            act.wait_ge(loaded, 16)
            act.activation(W[:, 0], RAW, ACT.Copy).then_inc(hi, 1)
            act.wait_ge(out, NQT)
            act.activation(VT[:, :, 256:TOKC], VT[:, :, 256:TOKC], ACT.Tanh, scale=0.5).then_inc(tanh, 1)


def norm_heads(nc, A, WK, PS, NSA, KPAD):
    SQ = WK.at(4096, 2, HALF)
    R = WK.at(5120, 2, HALF)
    GAINS = A.at(O_SMALL, 3)
    units = [(i, h) for i in range(6) for h in range(2)]
    with (nc.semaphore("h_sq") as squared, nc.semaphore("h_sum") as summed, nc.semaphore("h_root") as root,
          nc.semaphore("h_inv") as inverse, nc.semaphore("h_done") as done, nc.semaphore("h_zero") as zero,
          nc.Block() as block):
        @block.gpsimd
        def _(pool):
            for b in range(2):
                pool.memset(KPAD[64:128, 2 * b, :], 0.0)
                pool.memset(KPAD[0:64, 2 * b + 1, :], 0.0)

        @block.scalar
        def _(act):
            def root_of(n):
                act.wait_ge(summed, n + 1)
                if n >= 2:
                    act.wait_ge(done, n - 1)
                act.activation(R[:, n % 2, :], PS[:, n % 2, :], ACT.Sqrt, scale=1.0 / HD,
                               bias=cst(A, "eps")).then_inc(root, 1)

            for n, (i, h) in enumerate(units):
                if n >= 2:
                    act.wait_ge(summed, n - 1)
                act.activation(SQ[:, n % 2, :], NSA[:, i, h * HALF:(h + 1) * HALF], ACT.Square).then_inc(squared, 1)
                if n >= 1:
                    root_of(n - 1)
            root_of(len(units) - 1)

        @block.tensor
        def _(pe):
            for n in range(len(units)):
                pe.wait_ge(squared, n + 1)
                if n >= 2:
                    pe.wait_ge(root, n - 1)
                pe.matmul(PS[:, n % 2, :], cst(A, "blockones"), SQ[:, n % 2, :],
                          start=True, stop=True).then_inc(summed, 1)

        @block.vector
        def _(dve):
            dve.tensor_scalar(GAINS[:, 0:1], par(A, QG), 0.125, None, ALU.mult).then_inc(zero, 1)
            dve.wait_ge(zero, 1)
            for n, (i, h) in enumerate(units):
                cols = slice(h * HALF, (h + 1) * HALF)
                dve.wait_ge(root, n + 1)
                dve.reciprocal(R[:, n % 2, :], R[:, n % 2, :]).then_inc(inverse, 1)
                dve.wait_ge(inverse, n + 1)
                if i < PAIRS:
                    dve.scalar_tensor_tensor(NSA[:, i, cols], NSA[:, i, cols], GAINS[:, 0:1], R[:, n % 2, :],
                                             ALU.mult, ALU.mult).then_inc(done, 1)
                else:
                    b = i - PAIRS
                    for g in range(2):
                        rows = slice(64 * g, 64 * g + 64)
                        last = dve.scalar_tensor_tensor(KPAD[rows, 2 * b + g, cols], NSA[rows, i, cols],
                                                        par(A, KG + 1 + b)[rows], R[rows, n % 2, :],
                                                        ALU.mult, ALU.mult)
                    last.then_inc(done, 1)


def compress(nc, A, WK, PS, NSA, KPC, VC, w1_in, w2_in, pos_in):
    W1 = WK.at(4096, 2, 32, CMP_HID)
    KV = WK.at(4096 + 8192, 2, 2, 1024)
    POS = WK.at(4096 + 12288, 2, 32)
    W2 = WK.at(4096 + 12288 + 64, 2, HD)
    H = WK.at(4096 + 12288 + 192, 4, CMP_HID)
    Q = WK.at(4096 + 12288 + 704, 4, CMP_HID)
    HT = WK.at(4096 + 12288 + 1216, 4, NCMP)
    SQ = WK.at(4096 + 12288 + 1216 + 252, NCMP)
    KR = WK.at(4096 + 12288 + 1216 + 252 + 63, NCMP)
    with ExitStack() as ctx:
        sem = lambda n: ctx.enter_context(nc.semaphore("c_" + n))
        loaded, posed, hidden, copied, squared, inner, tanh, gelu, turned, turned_out, out2, k_sq, k_sum, k_root, step = (
            sem(x) for x in ("loaded", "posed", "hidden", "copied", "squared", "inner", "tanh", "gelu", "turned",
                             "turnedout", "out2", "ksq", "ksum", "kroot", "step"))
        loaded2 = sem("loaded2")
        block = ctx.enter_context(nc.Block())

        @block.sync
        def _(sp):
            for half in range(2):
                sp.dma_start(POS[64 * half:64 * half + 64], pos_in).then_inc(loaded2, 16)
            sp.dma_start(W2, w2_in).then_inc(loaded2, 16)
            for half in range(2):
                sp.dma_start(W1[64 * half:64 * half + 64], w1_in).then_inc(loaded, 16)

        @block.vector
        def _(dve):
            dve.wait_ge(loaded2, 48)
            for v in range(2):
                src = NSA[:, 6 + v, :].rearrange("p (n s) -> p n s", s=16)
                for b in range(2):
                    dve.tensor_tensor(KV[:, v, b, :].rearrange("p (n s) -> p n s", s=16), src,
                                      POS[:, v, 16 * b:16 * b + 16].unsqueeze(1).to_broadcast([P, 64, 16]),
                                      ALU.add).then_inc(posed, 1)
            dve.wait_ge(hidden, 4)
            dve.tensor_copy(H[0:NCMP], PS[0:NCMP, 0:4, 0:CMP_HID]).then_inc(copied, 1)
            dve.wait_ge(squared, 1)
            dve.tensor_scalar(Q[0:NCMP], Q[0:NCMP], 0.044715, 1.0, ALU.mult, ALU.add).then_inc(step, 1)
            dve.wait_ge(step, 1)
            dve.tensor_tensor(Q[0:NCMP], Q[0:NCMP], H[0:NCMP], ALU.mult).then_inc(inner, 1)
            dve.wait_ge(tanh, 1)
            dve.scalar_tensor_tensor(H[0:NCMP], Q[0:NCMP], 1.0, H[0:NCMP], ALU.add, ALU.mult).then_inc(gelu, 1)
            dve.wait_ge(turned, 1)
            dve.tensor_scalar(HT, PS[:, 4, 0:4 * NCMP].rearrange("p (a n) -> p a n", a=4), 0.5, None,
                              ALU.mult).then_inc(turned_out, 1)
            dve.wait_ge(out2, 1)
            dve.tensor_copy(VC[0:NCMP], PS[0:NCMP, 6, 0:2 * HD].rearrange("p (g d) -> p g d", g=2))
            dve.memset(KPC, 0.0).then_inc(step, 1)
            dve.wait_ge(k_root, 1)
            dve.reciprocal(KR, KR).then_inc(step, 1)
            dve.wait_ge(step, 3)
            for g in range(2):
                rows = slice(64 * g, 64 * g + 64)
                dve.scalar_tensor_tensor(KPC[rows, g, :], PS[rows, 5, 0:NCMP], par(A, KG)[rows], KR[rows, :],
                                         ALU.mult, ALU.mult)

        @block.tensor
        def _(pe):
            pe.wait_ge(loaded, 32)
            for v in range(2):
                pe.wait_ge(posed, 2 * v + 2)
                for g in range(2):
                    rows = slice(64 * g, 64 * g + 64)
                    for p in range(32):
                        kv = KV[rows, v, p // 16, :].rearrange("p (n s) -> p n s", s=16)
                        last = pe.matmul(PS[0:NCMP, 2 * v + g, 0:CMP_HID],
                                         kv[:, p // 16:p // 16 + NCMP, p % 16], W1[rows, v, p, :],
                                         start=p == 0, stop=p == 31)
                    last.then_inc(hidden, 1)
            pe.wait_ge(gelu, 1)
            for a in range(4):
                last = pe.transpose(PS[:, 4, a * NCMP:(a + 1) * NCMP], H[0:NCMP, a, :], cst(A, "ident")[0:NCMP, 0:NCMP])
            last.then_inc(turned, 1)
            pe.wait_ge(turned_out, 1)
            for g in range(2):
                pe.matmul(PS[64 * g:64 * g + 64, 5, 0:NCMP], W2[:, 0, :], HT[:, g, :], start=True, stop=True)
            for g in range(2):
                last = pe.matmul(PS[0:NCMP, 6, g * HD:(g + 1) * HD], HT[:, 2 + g, :], W2[:, 1, :], start=True, stop=True)
            last.then_inc(out2, 1)
            pe.wait_ge(k_sq, 1)
            pe.matmul(PS[:, 7, 0:NCMP], cst(A, "blockones"), SQ, start=True, stop=True).then_inc(k_sum, 1)

        @block.scalar
        def _(act):
            act.wait_ge(copied, 1)
            act.activation(Q[0:NCMP], H[0:NCMP], ACT.Square).then_inc(squared, 1)
            act.wait_ge(inner, 1)
            act.activation(Q[0:NCMP], Q[0:NCMP], ACT.Tanh, scale=float(np.sqrt(2.0 / np.pi))).then_inc(tanh, 1)
            act.wait_ge(out2, 1)
            act.activation(SQ, PS[:, 5, 0:NCMP], ACT.Square).then_inc(k_sq, 1)
            act.wait_ge(k_sum, 1)
            act.activation(KR, PS[:, 7, 0:NCMP], ACT.Sqrt, scale=1.0 / HD, bias=cst(A, "eps")).then_inc(k_root, 1)


def attention(nc, A, WK, PS, NSA, KPAD, KPC, VT, VC):
    PT = WK.at(4096, 2, 14, PAIRS, P)
    PB = WK.at(18432, 2, 1728)
    QB = WK.at(21888, P)
    at = 22016
    IDENTB = WK.at(at, 64).bitcast(BF16)
    DIAGB = WK.at(at + 64, 64).bitcast(BF16)
    WINB = WK.at(at + 128, 64).bitcast(BF16)
    NM = WK.at(at + 192, 2, 3)
    L = WK.at(at + 198, 2, 3)
    RL = WK.at(at + 204, 2, 3)
    SC = WK.at(at + 210, 2, 3)
    CMP, SLC, WIN = 0, 1, 2
    S_slc = PS[:, 0:2, :].rearrange("p a n -> p (a n)")
    S_win = PS[:, 2:4, :].rearrange("p a n -> p (a n)")
    CMP_AT = 640
    T_BANK, O_BANK = 4, 7

    def window(qt):
        return max(0, qt - WIN_TILES), qt + 1

    def blocks(qt):
        lo, hi = window(qt)
        return ([("slc", k, k * P) for k in range(qt + 1)]
                + [("win", k, 1024 + (k - lo) * P) for k in range(lo, hi)] + [("cmp", 0, 1664)])

    def chunks(qt):
        b = list(enumerate(blocks(qt)))
        n = qt + 1
        out = [b[k:min(k + 4, n)] for k in range(0, n, 4)]
        return out + [b[k:k + 4] for k in range(n, len(b), 4)]

    def evacuated_by(qt):
        return [k % 2 for k in range(len(chunks(qt)))]

    n_chunks = [len(chunks(qt)) for qt in range(NQT)]
    per_engine = [[evacuated_by(qt).count(e) for qt in range(NQT)] for e in range(2)]

    def unit(qt, j, g):
        return 8 * qt + 2 * j + g

    def chunk_count(qt, j, g, k):
        return 8 * sum(n_chunks[:qt]) + (2 * j + g) * n_chunks[qt] + k + 1

    def out_count(e, qt, j, g, k):
        return (8 * sum(per_engine[e][:qt]) + (2 * j + g) * per_engine[e][qt]
                + evacuated_by(qt)[:k + 1].count(e))

    def in_order(eng, front, back, after):
        front(0, 0, 0)
        for qt in range(NQT):
            def pair(j):
                front(qt, j, 1)
                back(qt, j, 0)
                front(qt, j + 1, 0)
                back(qt, j, 1)
            if qt == 0:
                for j in range(PAIRS - 1):
                    pair(j)
            else:
                with eng.Fori(0, PAIRS - 1) as j:
                    pair(j)
            front(qt, PAIRS - 1, 1)
            back(qt, PAIRS - 1, 0)
            if qt + 1 < NQT:
                front(qt + 1, 0, 0)
            back(qt, PAIRS - 1, 1)
            after(qt)

    with ExitStack() as ctx:
        sem = ctx.enter_context(cleared_semaphores(nc, "a_"))
        masks = sem("masks")
        q_copied = sem("qcopied")
        scored_slc = sem("scoredslc")
        scored_win = sem("scoredwin")
        maxed = sem("maxed")
        exp_slc = sem("expslc")
        exp_win = sem("expwin")
        inverse = sem("inverse")
        factor = sem("factor")
        scaled = sem("scaled")
        turned = sem("turned")
        out_by = [sem("outact"), sem("outdve")]
        summed = sem("summed")
        begun = [sem("begun")]
        stored = sem("stored")
        block = ctx.enter_context(nc.Block())

        @block.gpsimd
        def _(pool):
            for dst, name in ((IDENTB, "ident"), (DIAGB, "diagneg"), (WINB, "winneg")):
                last = pool.tensor_copy(dst, cst(A, name))
            last.then_inc(masks, 1)

            def front(qt, j, g):
                if g == 0:
                    if not (isinstance(j, int) and unit(qt, j, g) == 0):
                        pool.wait_ge(scored_win, unit(qt, j, g))
                    pool.tensor_copy(QB, NSA[:, j, qt * P:(qt + 1) * P]).then_inc(q_copied, 1)

            in_order(pool, front, lambda qt, j, g: None, lambda qt: None)

        @block.tensor
        def _(pe):
            pe.wait_ge(masks, 1)

            def front(qt, j, g):
                u = unit(qt, j, g)
                first = isinstance(u, int) and u == 0
                lo, hi = window(qt)
                pe.wait_ge(q_copied, 4 * qt + j + 1)
                if not first:
                    pe.wait_ge(exp_slc, u)
                n = (qt + 1) * P
                for b in range(0, n, HALF):
                    w = min(HALF, n - b)
                    diag = b + w == n
                    pe.matmul(S_slc[:, b:b + w], QB, KPAD[:, g, b:b + w], start=True, stop=not diag)
                last = pe.matmul(S_slc[:, n - P:n], IDENTB, DIAGB, start=False, stop=True)
                last.then_inc(scored_slc, 1)
                if not first:
                    pe.wait_ge(exp_win, u)
                n = (hi - lo) * P
                for b in range(0, n, HALF):
                    w = min(HALF, n - b)
                    old = b == 0 and qt >= WIN_TILES
                    diag = b + w == n
                    pe.matmul(S_win[:, b:b + w], QB, KPAD[:, 2 + g, lo * P + b:lo * P + b + w], start=True,
                              stop=not (old or diag))
                    if old:
                        pe.matmul(S_win[:, 0:P], IDENTB, WINB, start=False, stop=not diag)
                    if diag:
                        pe.matmul(S_win[:, n - P:n], IDENTB, DIAGB, start=False, stop=True)
                pe.matmul(S_win[:, CMP_AT:CMP_AT + NCMP], QB, KPC[:, g, :], start=True, stop=False)
                last = pe.matmul(S_win[:, CMP_AT:CMP_AT + NCMP], cst(A, "ident"),
                                 cst(A, "cmask")[:, qt * NCMP:(qt + 1) * NCMP], start=False, stop=True)
                last.then_inc(scored_win, 1)

            def back(qt, j, g):
                u = unit(qt, j, g)
                for k, chunk in enumerate(chunks(qt)):
                    kinds = {kind for _, (kind, _, _) in chunk}
                    pe.wait_ge(scaled, 3 * u + (3 if "cmp" in kinds else 2 if "win" in kinds else 1))
                    if k >= 3:
                        e = evacuated_by(qt)[k - 3]
                        pe.wait_ge(out_by[e], out_count(e, qt, j, g, k - 3))
                    else:
                        before = max(x for x in range(n_chunks[qt]) if x % 3 == k % 3)
                        e = evacuated_by(qt)[before]
                        v = out_count(e, qt, j, g, before) - per_engine[e][qt]
                        if not (isinstance(v, int) and u == 0):
                            pe.wait_ge(out_by[e], v)
                    pe.sem_inc(begun[0], 1)
                    for x, (_, (kind, _, col)) in enumerate(chunk):
                        if kind == "cmp":
                            last = pe.transpose(PS[0:NCMP, T_BANK + k % 3, x * P:(x + 1) * P],
                                                PB[:, g, col:col + NCMP], cst(A, "ident"))
                        else:
                            last = pe.transpose(PS[:, T_BANK + k % 3, x * P:(x + 1) * P],
                                                PB[:, g, col:col + P], cst(A, "ident"))
                    last.then_inc(turned, 1)

            def after(qt):
                for e in range(2):
                    pe.wait_ge(out_by[e], out_count(e, qt, PAIRS - 1, 1, n_chunks[qt] - 1))
                if qt >= 1:
                    pe.wait_ge(stored, qt)
                for g in range(2):
                    todo = blocks(qt)
                    for x, (kind, k, _) in enumerate(todo):
                        rows = NCMP if kind == "cmp" else P
                        v = (VC[0:NCMP, g, :] if kind == "cmp" else
                             VT[:, k, (kind == "win") * P + g * HD:(kind == "win") * P + (g + 1) * HD])
                        last = pe.matmul(PS[g * HD:(g + 1) * HD, O_BANK, :], v,
                                         PT[0:rows, g, x, :, :].rearrange("p a n -> p (a n)"),
                                         start=x == 0, stop=x == len(todo) - 1)
                last.then_inc(summed, 1)

            in_order(pe, front, back, after)

        def copy_out(eng, e, copy, qt, j, g):
            for k, chunk in enumerate(chunks(qt)):
                if evacuated_by(qt)[k] != e:
                    continue
                eng.wait_ge(turned, chunk_count(qt, j, g, k))
                if qt >= 1:
                    eng.wait_ge(summed, qt)
                x0 = chunk[0][0]
                whole = [c for c in chunk if c[1][0] != "cmp"]
                if whole:
                    last = copy(PT[:, g, x0:x0 + len(whole), j, :],
                                PS[:, T_BANK + k % 3, 0:len(whole) * P].rearrange("p (a n) -> p a n", n=P))
                if len(whole) < len(chunk):
                    x = len(whole)
                    last = copy(PT[0:NCMP, g, x0 + x, j, :], PS[0:NCMP, T_BANK + k % 3, x * P:(x + 1) * P])
                last.then_inc(out_by[e], 1)

        @block.vector
        def _(dve):
            def front(qt, j, g):
                u = unit(qt, j, g)
                lo, hi = window(qt)
                dve.wait_ge(scored_slc, u + 1)
                dve.tensor_reduce(NM[:, g, SLC:SLC + 1], S_slc[:, 0:(qt + 1) * P], axis=AX.X, op=ALU.max,
                                  negate=True).then_inc(maxed, 1)
                dve.wait_ge(scored_win, u + 1)
                dve.tensor_reduce(NM[:, g, WIN:WIN + 1], S_win[:, 0:(hi - lo) * P], axis=AX.X, op=ALU.max,
                                  negate=True).then_inc(maxed, 1)
                dve.tensor_reduce(NM[:, g, CMP:CMP + 1], S_win[:, CMP_AT:CMP_AT + NCMP], axis=AX.X, op=ALU.max,
                                  negate=True).then_inc(maxed, 1)

            def back(qt, j, g):
                u = unit(qt, j, g)
                lo, hi = window(qt)
                dve.wait_ge(exp_win, u + 1)
                dve.reciprocal(RL[:, g, :], L[:, g, :]).then_inc(inverse, 1)
                dve.wait_ge(inverse, u + 1 + min(qt, 1) * 0)
                if qt == 0:
                    dve.tensor_tensor(RL[:, g, CMP:CMP + 1], RL[:, g, CMP:CMP + 1], cst(A, "flag"),
                                      ALU.mult).then_inc(masks, 1)
                    dve.wait_ge(masks, u + 2)
                gate = VT[:, qt, 256:TOKC].rearrange("p (g j c) -> p g j c", g=2, c=3)[:, g, j, :]
                dve.tensor_tensor(SC[:, g, :], RL[:, g, :], gate, ALU.mult).then_inc(factor, 1)
                dve.wait_ge(factor, u + 1)
                for at_, n, c in ((0, (qt + 1) * P, SLC), (1024, (hi - lo) * P, WIN), (1664, NCMP, CMP)):
                    dve.tensor_scalar(PB[:, g, at_:at_ + n], PB[:, g, at_:at_ + n], SC[:, g, c:c + 1], None,
                                      ALU.mult).then_inc(scaled, 1)
                copy_out(dve, 1, lambda o, i: dve.tensor_copy(o, i), qt, j, g)

            in_order(dve, front, back, lambda qt: None)

        @block.scalar
        def _(act):
            def front(qt, j, g):
                u = unit(qt, j, g)
                lo, hi = window(qt)
                if not (isinstance(u, int) and u < 2):
                    if isinstance(u, int) or qt > 0:
                        act.wait_ge(turned, free_count(qt, j, g))
                act.wait_ge(maxed, 3 * u + 1)
                act.activation(PB[:, g, 0:(qt + 1) * P], S_slc[:, 0:(qt + 1) * P], ACT.Exp,
                               bias=NM[:, g, SLC:SLC + 1], accum_out=L[:, g, SLC:SLC + 1]).then_inc(exp_slc, 1)
                act.wait_ge(maxed, 3 * u + 3)
                act.activation(PB[:, g, 1024:1024 + (hi - lo) * P], S_win[:, 0:(hi - lo) * P], ACT.Exp,
                               bias=NM[:, g, WIN:WIN + 1], accum_out=L[:, g, WIN:WIN + 1])
                act.activation(PB[:, g, 1664:1664 + NCMP], S_win[:, CMP_AT:CMP_AT + NCMP], ACT.Exp,
                               bias=NM[:, g, CMP:CMP + 1], accum_out=L[:, g, CMP:CMP + 1]).then_inc(exp_win, 1)

            def free_count(qt, j, g):
                if isinstance(j, int):
                    u = unit(qt, j, g) - 2
                    q0, r = divmod(u, 8)
                    return chunk_count(q0, r // 2, r % 2, n_chunks[q0] - 1)
                return chunk_count(qt, j - 1, g, n_chunks[qt] - 1)

            def back(qt, j, g):
                copy_out(act, 0, lambda o, i: act.activation(o, i, ACT.Copy), qt, j, g)

            def after(qt):
                act.wait_ge(summed, qt + 1)
                act.activation(NSA[:, 0:PAIRS, qt * P:(qt + 1) * P],
                               PS[:, O_BANK, :].rearrange("p (a n) -> p a n", n=P), ACT.Copy).then_inc(stored, 1)

            in_order(act, front, back, after)


def mix_and_lora(nc, A, NV, PS, RJ, DEC, AA, KN, lora_in):
    DIFF = NV.at(4 * 1024, 2, 1024)
    SQ = NV.at(6 * 1024, 2, HALF)
    R = NV.at(7 * 1024, 2, HALF)
    LORA = NV.at(O_VT, HALF)
    HALFB = A.at(O_SMALL, 8)
    order = [12, 13] + list(range(4, 8)) + list(range(0, 4)) + list(range(8, 12))
    with ExitStack() as ctx:
        sem = ctx.enter_context(cleared_semaphores(nc, "m_"))
        loaded, diff, mixed, tanh_in, product, tanh_out, affine = (
            sem(x) for x in ("loaded", "diff", "mixed", "tanhin", "product", "tanhout", "affine"))
        squared, summed, clamped, root, inverse, keyed, half_bias = (
            sem(x) for x in ("squared", "summed", "clamped", "root", "inverse", "keyed", "halfbias"))
        block = ctx.enter_context(nc.Block())
        units = [(j, h) for j in range(PAIRS) for h in range(2)]

        @block.sync
        def _(sp):
            sp.dma_start(LORA, lora_in).then_inc(loaded, 16)

        @block.vector
        def _(dve):
            dve.tensor_scalar(HALFB, par(A, W0, 8), 0.5, None, ALU.mult).then_inc(half_bias, 1)

            def mix(n):
                i, b = order[n], n % 2
                if n >= 2:
                    dve.wait_ge(mixed, n - 1)
                dve.tensor_tensor(DIFF[:, b, 1:T], RJ[:, i, 0:T - 1], RJ[:, i, 1:T], ALU.subtract)
                dve.tensor_scalar(DIFF[:, b, 0:1], RJ[:, i, 0:1], -1.0, None, ALU.mult).then_inc(diff, 1)
                dve.wait_ge(diff, n + 1)
                dve.scalar_tensor_tensor(RJ[:, i, :], DIFF[:, b, :], par(A, MU + i), RJ[:, i, :],
                                         ALU.mult, ALU.add).then_inc(mixed, 1)

            for n in range(6):
                mix(n)
            for n, (j, h) in enumerate(units):
                cols = slice(h * HALF, (h + 1) * HALF)
                dve.wait_ge(mixed, 3 + j)
                dve.wait_ge(summed, n + 1)
                dve.tensor_scalar(R[:, n % 2, :], PS[:, n % 2, :], 1e-24, None, ALU.max).then_inc(clamped, 1)
                dve.wait_ge(root, n + 1)
                dve.reciprocal(R[:, n % 2, :], R[:, n % 2, :]).then_inc(inverse, 1)
                dve.wait_ge(inverse, n + 1)
                dve.scalar_tensor_tensor(KN[:, j, cols], RJ[:, 4 + j, cols], par(A, KK + 2 * j), R[:, n % 2, :],
                                         ALU.mult, ALU.mult).then_inc(keyed, 1)
            for n in range(6, RW_TILES):
                mix(n)
            dve.wait_ge(tanh_in, 2)
            dve.tensor_scalar(RJ[:, 13, :], RJ[:, 13, :], 0.5, 0.5, ALU.mult, ALU.add)
            for n, (j, h) in enumerate(units):
                cols = slice(h * HALF, (h + 1) * HALF)
                dve.wait_ge(tanh_out, 2 * n + 2)
                dve.tensor_scalar(DEC[:, j, cols], DEC[:, j, cols], -0.5 * DECAY_SCALE, -0.5 * DECAY_SCALE,
                                  ALU.mult, ALU.add)
                dve.tensor_scalar(AA[:, j, cols], AA[:, j, cols], 0.5, 0.5, ALU.mult, ALU.add)

        @block.scalar
        def _(act):
            for n, (j, h) in enumerate(units):
                act.wait_ge(mixed, 3 + j)
                if n >= 2:
                    act.wait_ge(summed, n - 1)
                act.activation(SQ[:, n % 2, :], RJ[:, 4 + j, h * HALF:(h + 1) * HALF], ACT.Square,
                               scale=par(A, KK + 2 * j)).then_inc(squared, 1)
                act.wait_ge(clamped, n + 1)
                act.activation(R[:, n % 2, :], R[:, n % 2, :], ACT.Sqrt).then_inc(root, 1)
            act.wait_ge(mixed, 2)
            act.activation(RJ[0:64, 12, :], RJ[0:64, 12, :], ACT.Tanh).then_inc(tanh_in, 1)
            act.activation(RJ[:, 13, :], RJ[:, 13, :], ACT.Tanh, scale=0.5).then_inc(tanh_in, 1)
            act.wait_ge(half_bias, 1)
            for n, (j, h) in enumerate(units):
                cols = slice(h * HALF, (h + 1) * HALF)
                for x, dst in enumerate((DEC, AA)):
                    act.wait_ge(product, 2 * n + x + 1)
                    act.activation(dst[:, j, cols], PS[:, 2 + 2 * x + n % 2, :], ACT.Tanh, scale=0.5,
                                   bias=HALFB[:, 4 * x + j:4 * x + j + 1]).then_inc(tanh_out, 1)

        @block.tensor
        def _(pe):
            for n in range(len(units)):
                pe.wait_ge(squared, n + 1)
                if n >= 2:
                    pe.wait_ge(clamped, n - 1)
                pe.matmul(PS[:, n % 2, :], cst(A, "blockones"), SQ[:, n % 2, :], start=True, stop=True).then_inc(summed, 1)
            pe.wait_ge(loaded, 16)
            pe.wait_ge(tanh_in, 1)
            for n, (j, h) in enumerate(units):
                for x in range(2):
                    if n >= 2:
                        pe.wait_ge(tanh_out, 2 * n + x - 3)
                    rows = slice(64 * x, 64 * x + 64)
                    pe.matmul(PS[:, 2 + 2 * x + n % 2, :], LORA[rows, j * P:(j + 1) * P],
                              RJ[rows, 12, h * HALF:(h + 1) * HALF], start=True, stop=True).then_inc(product, 1)


def rwkv_chunks(nc, A, NV, WK, PS, RJ, DEC, AA, KN):
    R8, K8, V8, D8, A8, KN8 = (x.rearrange("p a (b n) -> p (a b) n", b=2)
                               for x in (RJ.first[:, 0:4, :], RJ.first[:, 4:8, :], RJ.second[:, 0:4, :], DEC, AA, KN))
    room = [NV.at(4 * 1024 + 512 * x, 8, C) for x in range(8)] + [NV.at(O_VT + 512 * x, 8, C) for x in range(4)]
    room += [WK.at(x, 8, C) for x in range(14 * 1024, WORK - 511, 512)]
    names = iter(room)

    def temp():
        return next(names)

    def flat(x):
        return x.rearrange("p a b -> p (a b)")

    AR = RJ.second[:, 4, :].rearrange("p (x a b) -> p x a b", x=2, b=C)
    AMV = WK.at(12 * 1024, 8, 2, C)
    GH = WK.at(13 * 1024, 8, 2, C)
    LW, E0, E1, E2, KM, Bf, Kf, Kc = (temp() for _ in range(8))
    Bc = LW
    Vt, Bt, Kt = (temp() for _ in range(3))
    V_IN = temp()
    MT, RB, RK = (temp() for _ in range(3))
    N1, L1, L32, L64 = (temp() for _ in range(4))
    L2, N2, L4, N4, L8 = (temp() for _ in range(5))
    Z, TT, X = (temp() for _ in range(3))
    DG = E0

    def bc(ap):
        return ap.unsqueeze(1).to_broadcast([P, 8, C])

    def bank(b):
        return PS[:, b, :].rearrange("p (a n) -> p a n", n=C)

    def wide(b):
        return PS[:, b:b + 2, :].rearrange("p b (a x n) -> p (b a) x n", x=2, n=C)

    def split(b):
        return PS[:, b:b + 2, 0:4 * C].rearrange("p s (m n) -> p s m n", n=C)

    def duo(b):
        return PS[:, b:b + 2, :].rearrange("p s (m x n) -> p s m x n", x=2, n=C)

    def halves(x):
        return x.rearrange("p (m s) n -> p s m n", s=2)

    def bc3(ap):
        return ap.unsqueeze(1).unsqueeze(1).to_broadcast([P, 2, 4, C])

    def dual(b, m):
        return PS[:, b, m * P:(m + 1) * P]

    units = [(m, h, c) for m in range(4) for h in range(2) for c in range(2)]
    rows = lambda x: slice(64 * x, 64 * x + 64)
    W_LAST = E1[:, :, C - 1:C].to_broadcast([P, 8, C])

    with ExitStack() as ctx:
        sem = ctx.enter_context(cleared_semaphores(nc, "r_"))
        block = ctx.enter_context(nc.Block())

        @block.gpsimd
        def _(pool):
            pool.tensor_copy(flat(V_IN), V8[:, 0, :]).then_inc(sem("v_in"), 1)
            with pool.Fori(1, 8) as it:
                pool.wait_ge(sem("t_v"), it)
                pool.tensor_copy(flat(V_IN), V8[:, it, :]).then_inc(sem("v_in"), 1)

        @block.scalar
        def _(act):
            act.sem_inc(sem("y0"), 1)
            act.sem_inc(sem("qq"), 1)
            with act.Fori(0, 8) as it:
                def wait(n):
                    act.wait_ge(sem(n), it + 1)

                def copy(dst, src, done):
                    act.activation(dst, src, ACT.Copy).then_inc(sem(done), 1)

                wait("lw")
                act.activation(E2, LW, ACT.Exp, scale=-1.0).then_inc(sem("e2"), 1)
                act.activation(E1, LW, ACT.Exp).then_inc(sem("e1"), 1)
                wait("lwx")
                act.activation(E0, E0, ACT.Exp).then_inc(sem("e0"), 1)
                wait("t_v")
                copy(flat(Vt), PS[:, 6, :], "v_out")
                wait("t_b")
                copy(flat(Bt), PS[:, 7, :], "b_out")
                wait("t_k")
                copy(flat(Kt), PS[:, 2, :], "k_out")
                wait("t_a")
                copy(AMV[:, :, 0, :], bank(3), "a_out")
                for src, dst, b in (("l2", L2, 6), ("l4", L4, 6), ("l8", L8, 6), ("t4", TT, 7), ("t5", TT, 7)):
                    wait("p_" + src)
                    copy(dst, bank(b), src)
                wait("p_mv")
                copy(AMV[:, :, 1, :], bank(5), "mv")
                wait("p_gh")
                copy(GH, wide(0), "gh")
                wait("p_y0")
                copy(halves(K8[:, it, :].rearrange("p (a b) -> p a b", b=C)), split(4), "y0")
                wait("p_q")
                copy(halves(A8[:, it, :].rearrange("p (a b) -> p a b", b=C)), split(0), "qq")

        @block.vector
        def _(dve):
            dve.sem_inc(sem("r2"), 1)
            dve.sem_inc(sem("pp"), 1)
            with dve.Fori(0, 8) as it:
                def wait(n):
                    dve.wait_ge(sem(n), it + 1)

                def mul(dst, a, b, done):
                    dve.tensor_tensor(dst, a, b, ALU.mult).then_inc(sem(done), 1)

                def add(dst, a, b, done):
                    dve.tensor_tensor(dst, a, b, ALU.add).then_inc(sem(done), 1)

                def eight(x):
                    return x[:, it, :].rearrange("p (a b) -> p a b", b=C)

                dve.tensor_tensor_scan(flat(LW), cst(A, "scan"), D8[:, it, :], 0.0, ALU.mult,
                                       ALU.add).then_inc(sem("lw"), 1)
                wait("lw")
                dve.tensor_tensor(flat(E0), flat(LW), D8[:, it, :], ALU.subtract).then_inc(sem("lwx"), 1)
                dve.tensor_scalar(flat(KM), A8[:, it, :], -1.0, A.at(O_PAR + KA, 8)[:, bass.ds(it, 1)],
                                  ALU.add, ALU.mult).then_inc(sem("kmt"), 1)
                wait("kmt")
                dve.scalar_tensor_tensor(flat(KM), flat(KM), 1.0, K8[:, it, :], ALU.add,
                                         ALU.mult).then_inc(sem("km"), 1)
                wait("e2")
                dve.tensor_tensor(Bf, eight(KN8), eight(A8), ALU.mult).then_inc(sem("bonus"), 1)
                wait("km")
                mul(Kf, KM, E2, "kh")
                dve.wait_ge(sem("bonus"), 2 * it + 1)
                mul(Bf, Bf, E2, "bh")
                wait("e1")
                mul(AR[:, 1], eight(R8), E1, "rh")
                wait("e0")
                dve.scalar_tensor_tensor(AR[:, 0], eight(KN8), -1.0, E0, ALU.mult,
                                         ALU.mult).then_inc(sem("ah"), 1)
                wait("kh")
                wait("bh")
                dve.scalar_tensor_tensor(flat(E2), R8[:, it, :], A.at(O_PAR + RKP, 8)[:, bass.ds(it, 1)], flat(KM),
                                         ALU.mult, ALU.mult).then_inc(sem("rk_in"), 1)
                mul(Bc, Bf, W_LAST, "bc")
                mul(Kc, Kf, W_LAST, "kc")
                wait("ah")
                mul(DG, bc(cst(A, "ident64")), W_LAST, "dg")
                wait("p_nrb")
                dve.tensor_tensor(halves(N1), duo(0)[:, :, :, 0, :], bc3(cst(A, "u_d")), ALU.mult)
                mul(halves(RB), duo(0)[:, :, :, 1, :], bc3(cst(A, "u_le")), "nrb_out")
                wait("p_l")
                for dst, name in ((L1, "l_d"), (L32, "l_32")):
                    dve.tensor_tensor(halves(dst), split(2), bc3(cst(A, name)), ALU.mult)
                mul(halves(L64), split(2), bc3(cst(A, "l_64")), "l_out")
                wait("nrb_out")
                add(Z, N1, bc(cst(A, "ident64")), "z1")
                wait("p_mrk")
                dve.tensor_tensor(halves(MT), duo(4)[:, :, :, 0, :], bc3(cst(A, "u_lt")), ALU.mult)
                mul(halves(RK), duo(4)[:, :, :, 1, :], bc3(cst(A, "u_le")), "mrk_out")
                wait("bonus_sum")
                wait("v_in")
                dve.tensor_tensor(V8[:, it, :], PS[:, 4, :], V8[:, it, :], ALU.mult).then_inc(sem("bonus"), 1)

                def power(name, dst):
                    wait("p_" + name)
                    dve.tensor_copy(dst, bank(0)).then_inc(sem(name), 1)

                def to_z(name):
                    wait("p_" + name)
                    add(Z, Z, bank(1), name)

                power("n2", N2)
                to_z("z2")
                power("n4", N4)
                to_z("z3")
                to_z("z4")
                power("x", X)
                to_z("z5")
                power("x2", X)
                to_z("z6")
                wait("p_r2")
                add(halves(eight(R8)), halves(AR[:, 1]), split(2), "r2")
                wait("p_p")
                add(halves(eight(D8)), halves(DG), split(6), "pp")

        @block.tensor
        def _(pe):
            with pe.Fori(0, 8) as it:
                def wait(n):
                    pe.wait_ge(sem(n), it + 1)

                def before(n):
                    pe.wait_ge(sem(n), it + 1)

                def started():
                    pe.sem_inc(sem("begun"), 1)

                def token(out_bank, lhs, rhs, done):
                    started()
                    for m, h, c in units:
                        last = pe.matmul(bank(out_bank)[rows(c), 2 * m + h, :], lhs[rows(c), 2 * m + h, :],
                                         rhs[rows(c), 2 * m + h, :], start=True, stop=True)
                    last.then_inc(sem(done), 1)

                def turn(out_bank, src, done):
                    for m in range(4):
                        last = pe.transpose(dual(out_bank, m), src[:, 2 * m:2 * m + 2, :], cst(A, "ident"))
                    last.then_inc(sem(done), 1)

                wait("ah")
                wait("bh")
                wait("rh")
                before("qq")
                started()
                for m, h, c in units:
                    last = pe.matmul(duo(0)[rows(c), h, m, :, :], Bf[rows(h), 2 * m + c, :],
                                     AR[rows(h), :, 2 * m + c, :], start=True, stop=True)
                last.then_inc(sem("p_nrb"), 1)
                before("r2")
                started()
                for m, h, c in units:
                    last = pe.matmul(split(2)[rows(c), h, m, :], AR[rows(h), 0, 2 * m + c, :],
                                     Bf[rows(h), 2 * m + c, :], start=True, stop=True)
                last.then_inc(sem("p_l"), 1)
                wait("kh")
                before("y0")
                started()
                for m, h, c in units:
                    last = pe.matmul(duo(4)[rows(c), h, m, :, :], Kf[rows(h), 2 * m + c, :],
                                     AR[rows(h), :, 2 * m + c, :], start=True, stop=True)
                last.then_inc(sem("p_mrk"), 1)
                wait("v_in")
                before("pp")
                for m in range(4):
                    last = pe.transpose(dual(6, m), V_IN[:, 2 * m:2 * m + 2, :], cst(A, "ident"))
                last.then_inc(sem("t_v"), 1)
                wait("bc")
                turn(7, Bc, "t_b")
                wait("kc")
                wait("l_out")
                turn(2, Kc, "t_k")
                for m in range(4):
                    last = pe.transpose(dual(3, m), AR[:, 0, 2 * m:2 * m + 2, :], cst(A, "ident"))
                last.then_inc(sem("t_a"), 1)
                wait("mrk_out")
                wait("rk_in")
                pe.matmul(PS[:, 4, :], cst(A, "blockones"), flat(E2), start=True, stop=True).then_inc(sem("bonus_sum"), 1)
                wait("nrb_out")
                wait("v_out")
                token(6, N1, L1, "p_l2")
                token(0, L1, N1, "p_n2")
                wait("z1")
                wait("l2")
                token(1, L2, Z, "p_z2")
                wait("n2")
                token(6, N2, L2, "p_l4")
                token(0, L2, N2, "p_n4")
                wait("v_out")
                token(5, MT, Vt, "p_mv")
                wait("l4")
                wait("z2")
                token(1, L4, Z, "p_z3")
                wait("n4")
                token(6, N4, L4, "p_l8")
                wait("l8")
                wait("z3")
                token(1, L8, Z, "p_z4")
                wait("z4")
                token(0, L32, Z, "p_x")
                wait("b_out")
                started()
                for m, h, c in units:
                    last = pe.matmul(bank(7)[rows(c), 2 * m + h, :], Z[rows(c), 2 * m + h, :],
                                     cst(A, "ident64")[rows(c), :], start=True, stop=True)
                last.then_inc(sem("p_t4"), 1)
                wait("x")
                wait("t4")
                token(1, TT, X, "p_z5")
                wait("z5")
                token(0, L64, Z, "p_x2")
                started()
                for m, h, c in units:
                    last = pe.matmul(bank(7)[rows(c), 2 * m + h, :], Z[rows(c), 2 * m + h, :],
                                     cst(A, "ident64")[rows(c), :], start=True, stop=True)
                last.then_inc(sem("p_t5"), 1)
                wait("x2")
                wait("t5")
                token(1, TT, X, "p_z6")
                wait("z6")
                wait("mv")
                wait("a_out")
                started()
                for m, h, c in units:
                    last = pe.matmul(wide(0)[rows(c), 2 * m + h, :, :], Z[rows(c), 2 * m + h, :],
                                     AMV[rows(c), 2 * m + h, :, :], start=True, stop=True)
                last.then_inc(sem("p_gh"), 1)
                wait("k_out")
                wait("gh")
                started()
                for m, h, c in units:
                    last = pe.matmul(split(2)[rows(h), c, m, :], GH[rows(c), 2 * m + h, 0, :],
                                     RB[rows(c), 2 * m + h, :], start=True, stop=True)
                last.then_inc(sem("p_r2"), 1)
                pe.wait_ge(sem("bonus"), 2 * it + 2)
                started()
                for m, h, c in units:
                    pe.matmul(split(4)[rows(h), c, m, :], GH[rows(c), 2 * m + h, 1, :],
                              RB[rows(c), 2 * m + h, :], start=True, stop=False)
                    last = pe.matmul(split(4)[rows(h), c, m, :], Vt[rows(c), 2 * m + h, :],
                                     RK[rows(c), 2 * m + h, :], start=False, stop=True)
                last.then_inc(sem("p_y0"), 1)
                started()
                for m, h, c in units:
                    last = pe.matmul(split(6)[rows(h), c, m, :], GH[rows(c), 2 * m + h, 0, :],
                                     Bt[rows(c), 2 * m + h, :], start=True, stop=True)
                last.then_inc(sem("p_p"), 1)
                started()
                for m, h, c in units:
                    pe.matmul(split(0)[rows(h), c, m, :], Bt[rows(c), 2 * m + h, :],
                              GH[rows(c), 2 * m + h, 1, :], start=True, stop=False)
                    last = pe.matmul(split(0)[rows(h), c, m, :], Kt[rows(c), 2 * m + h, :],
                                     Vt[rows(c), 2 * m + h, :], start=False, stop=True)
                last.then_inc(sem("p_q"), 1)


def rwkv_scan(nc, A, NV, PS, RJ, DEC, AA):
    S = NV.at(4 * 1024, 2, PAIRS, C)
    chunk = lambda x, n: x[:, 0:PAIRS, n * C:(n + 1) * C]
    with (nc.semaphore("s_moved") as moved, nc.semaphore("s_state") as state, nc.semaphore("s_read") as read,
          nc.semaphore("s_y") as y_done, nc.Block() as block):
        @block.tensor
        def _(pe):
            for n in range(NCH):
                pe.wait_ge(state, n + 1)
                P_, R_ = chunk(DEC, n), chunk(RJ.first, n)
                if n < NCH - 1:
                    for j in range(PAIRS):
                        for h in range(2):
                            r = slice(64 * h, 64 * h + 64)
                            last = pe.matmul(PS[r, n % 2, j * C:(j + 1) * C], P_[r, j, :], S[r, n % 2, j, :],
                                             start=True, stop=True)
                    last.then_inc(moved, 1)
                if n >= 2:
                    pe.wait_ge(y_done, n - 1)
                for j in range(PAIRS):
                    for h in range(2):
                        r = slice(64 * h, 64 * h + 64)
                        last = pe.matmul(PS[r, 2 + n % 2, j * C:(j + 1) * C], S[r, n % 2, j, :], R_[r, j, :],
                                         start=True, stop=True)
                last.then_inc(read, 1)

        @block.vector
        def _(dve):
            dve.memset(S[:, 0], 0.0).then_inc(state, 1)

            def out(n):
                dve.wait_ge(read, n + 1)
                y0 = chunk(RJ.first[:, 4:8, :], n)
                dve.tensor_tensor(y0, y0, PS[:, 2 + n % 2, 0:PAIRS * C].rearrange("p (a b) -> p a b", b=C),
                                  ALU.add).then_inc(y_done, 1)

            for n in range(NCH):
                if n < NCH - 1:
                    dve.wait_ge(moved, n + 1)
                    if n >= 1:
                        dve.wait_ge(read, n)
                    dve.tensor_tensor(S[:, (n + 1) % 2], PS[:, n % 2, 0:PAIRS * C].rearrange("p (a b) -> p a b", b=C),
                                      chunk(AA, n), ALU.add).then_inc(state, 1)
                out(n)


def rwkv_out(nc, A, NV, PS, RJ, g_in):
    GUP = NV.at(O_VT, HALF)
    W = NV.at(4 * 1024, 8, HALF)
    with ExitStack() as ctx:
        sem = ctx.enter_context(cleared_semaphores(nc, "g_"))
        loaded, mean, centred, squared, var, root, inverse, gate, out, step = (
            sem(x) for x in ("loaded", "mean", "centred", "squared", "var", "root", "inverse", "gate", "out", "step"))
        block = ctx.enter_context(nc.Block())
        units = [(j, slice(h * HALF, (h + 1) * HALF)) for j in range(PAIRS) for h in range(2)]

        @block.sync
        def _(sp):
            sp.dma_start(GUP, g_in).then_inc(loaded, 16)

        @block.tensor
        def _(pe):
            pe.wait_ge(loaded, 16)
            for n in range(len(units) + 1):
                if n < len(units):
                    j, cols = units[n]
                    if n >= 2:
                        pe.wait_ge(centred, n - 1)
                    pe.matmul(PS[:, n % 2, :], cst(A, "blockones"), RJ[:, 4 + j, cols], start=True, stop=True).then_inc(mean, 1)
                if n >= 1:
                    k = n - 1
                    j, cols = units[k]
                    pe.wait_ge(squared, k + 1)
                    if k >= 2:
                        pe.wait_ge(root, k - 1)
                        pe.wait_ge(out, k - 1)
                    pe.matmul(PS[:, 2 + k % 2, :], cst(A, "blockones"), W[:, k % 2, :], start=True, stop=True).then_inc(var, 1)
                    pe.matmul(PS[:, 4 + k % 2, :], GUP[:, j * P:(j + 1) * P], RJ[:, 13, cols], start=True,
                              stop=True).then_inc(gate, 1)

        @block.scalar
        def _(act):
            for n, (j, cols) in enumerate(units):
                act.wait_ge(centred, n + 1)
                if n >= 2:
                    act.wait_ge(var, n - 1)
                act.activation(W[:, n % 2, :], RJ[:, 4 + j, cols], ACT.Square).then_inc(squared, 1)
                act.wait_ge(var, n + 1)
                if n >= 2:
                    act.wait_ge(out, n - 1)
                act.activation(W[:, 2 + n % 2, :], PS[:, 2 + n % 2, :], ACT.Sqrt, scale=1.0 / HD,
                               bias=cst(A, "gneps")).then_inc(root, 1)

        @block.vector
        def _(dve):
            def centre(n):
                j, cols = units[n]
                dve.wait_ge(mean, n + 1)
                dve.scalar_tensor_tensor(RJ[:, 4 + j, cols], PS[:, n % 2, :], -1.0 / HD, RJ[:, 4 + j, cols],
                                         ALU.mult, ALU.add).then_inc(centred, 1)

            centre(0)
            for n, (j, cols) in enumerate(units):
                if n + 1 < len(units):
                    centre(n + 1)
                dve.wait_ge(root, n + 1)
                R = W[:, 2 + n % 2, :]
                Y = RJ[:, 4 + j, cols]
                dve.reciprocal(R, R).then_inc(inverse, 1)
                dve.wait_ge(inverse, n + 1)
                dve.scalar_tensor_tensor(Y, Y, par(A, LNW + j), R, ALU.mult, ALU.mult).then_inc(step, 1)
                dve.wait_ge(step, 2 * n + 1)
                dve.scalar_tensor_tensor(Y, Y, par(A, LNB + j), RJ[:, 8 + j, cols], ALU.add, ALU.add).then_inc(step, 1)
                dve.wait_ge(step, 2 * n + 2)
                dve.wait_ge(gate, n + 1)
                dve.tensor_tensor(Y, Y, PS[:, 4 + n % 2, :], ALU.mult).then_inc(out, 1)


def split_tiles(nc, tag, sources, R):
    with nc.semaphore(tag + "_hi") as hi, nc.Block() as block:
        @block.scalar
        def _(act):
            for c, x in enumerate(sources):
                act.activation(hi_of(R)[:, c, :], x, ACT.Copy).then_inc(hi, 1)

        @block.vector
        def _(dve):
            for c, x in enumerate(sources):
                dve.wait_ge(hi, c + 1)
                dve.tensor_tensor(lo_of(R)[:, c, :], x, hi_of(R)[:, c, :].bitcast(F32), ALU.subtract)


def merge(nc, A, PS, w_in, gates, Y, M, GT, raw, W):
    n_pairs = KC // 2
    with ExitStack() as ctx:
        sem = ctx.enter_context(cleared_semaphores(nc, "e_"))
        loaded, rounded, split, product, begun = slot_semaphores(sem)
        gate = [sem("gate0"), sem("gate1")]
        part = [sem("part0"), sem("part1")]
        merged = [sem("merged0"), sem("merged1")]
        block = ctx.enter_context(nc.Block())

        @block.sync
        def _(sp):
            load_weights(sp, raw, w_in, loaded, split, n_pairs)

        @block.gpsimd
        def _(pool):
            split_weights(pool, raw, W, loaded, rounded, split, product, begun, n_pairs)

        @block.scalar
        def _(act):
            g2 = gates.rearrange("(x n) p t -> n x p t", x=2)

            def load(n, s):
                act.dma_start(GT[:, s], g2[n].rearrange("x p t -> p x t")).then_inc(gate[s], 16)

            for s in range(2):
                load(s, s)
            with act.Fori(1, n_pairs) as i:
                for s in range(2):
                    act.wait_ge(merged[s], 2 * i + 1)
                    load(2 * i + s, s)

        @block.tensor
        def _(pe):
            with pe.Fori(0, n_pairs) as i:
                for s in range(2):
                    pe.wait_ge(split[s], i + 1)
                    pe.wait_ge(merged[s], 2 * i + 1)
                    for h in range(2):
                        for x in range(2):
                            out = PS[:, 4 * s + 2 * h + x, :]
                            for c in range(PAIRS * x, PAIRS * x + PAIRS):
                                pe.matmul(out, W[:, s, 0, c, :], hi_of(Y)[:, c, HALVES[h]], start=c == PAIRS * x, stop=False)
                                pe.matmul(out, W[:, s, 0, c, :], lo_of(Y)[:, c, HALVES[h]], start=False, stop=False)
                                last = pe.matmul(out, W[:, s, 1, c, :], hi_of(Y)[:, c, HALVES[h]], start=False,
                                                 stop=c == PAIRS * x + PAIRS - 1)
                        last.then_inc(product[s], 1)

        @block.vector
        def _(dve):
            for s in range(2):
                dve.sem_inc(merged[s], 1)
            with dve.Fori(0, n_pairs) as i:
                for s in range(2):
                    dve.wait_ge(gate[s], 16 * i + 16)
                    for h in range(2):
                        dve.wait_ge(product[s], 2 * i + h + 1)
                        for x in range(2):
                            dve.scalar_tensor_tensor(GT[:, s, x, HALVES[h]], GT[:, s, x, HALVES[h]], 1.0,
                                                     PS[:, 4 * s + 2 * h + x, :], ALU.add, ALU.mult).then_inc(part[s], 1)
                        dve.wait_ge(part[s], 4 * i + 2 * h + 2)
                        dve.tensor_tensor(M[:, 2 * i + s, HALVES[h]], GT[:, s, 0, HALVES[h]], GT[:, s, 1, HALVES[h]],
                                          ALU.add).then_inc(merged[s], 1)


def project_out(nc, A, PS, x_in, w_in, M, X, raw, W):
    n_pairs = KC // 2
    with ExitStack() as ctx:
        sem = ctx.enter_context(cleared_semaphores(nc, "o_"))
        loaded, rounded, split, product, begun = slot_semaphores(sem)
        added = [sem("added0"), sem("added1")]
        x_loaded = sem("x")
        block = ctx.enter_context(nc.Block())

        @block.sync
        def _(sp):
            load_weights(sp, raw, w_in, loaded, split, n_pairs)

        @block.gpsimd
        def _(pool):
            split_weights(pool, raw, W, loaded, rounded, split, product, begun, n_pairs)

        @block.tensor
        def _(pe):
            with pe.Fori(0, n_pairs) as i:
                for s in range(2):
                    pe.wait_ge(split[s], i + 1)
                    for h in range(2):
                        pe.wait_ge(added[s], 2 * i + 1)
                        three_passes(pe, PS[:, 2 * s + h, :], W, s, M, HALVES[h]).then_inc(product[s], 1)

        @block.scalar
        def _(act):
            act.dma_start(X, x_in.rearrange("(c p) t -> p c t", p=P)).then_inc(x_loaded, 16)

        @block.vector
        def _(dve):
            dve.wait_ge(x_loaded, 16)
            for s in range(2):
                dve.sem_inc(added[s], 1)
            with dve.Fori(0, n_pairs) as i:
                for s in range(2):
                    for h in range(2):
                        dve.wait_ge(product[s], 2 * i + h + 1)
                        dve.scalar_tensor_tensor(X[:, 2 * i + s, HALVES[h]], PS[:, 2 * s + h, :], 0.5,
                                                 X[:, 2 * i + s, HALVES[h]], ALU.mult, ALU.add).then_inc(added[s], 1)


def norm_again(nc, A, PS, X, H, SQ, TMP):
    R = A.at(O_RSTD, 1024)
    with (nc.semaphore("f_sq") as squared, nc.semaphore("f_sum") as summed, nc.semaphore("f_rms") as rms,
          nc.semaphore("f_rs") as rs, nc.semaphore("f_scaled") as scaled, nc.semaphore("f_hi") as hi,
          nc.semaphore("f_lo") as lo, nc.Block() as block):
        @block.scalar
        def _(act):
            for c in range(KC):
                if c >= 2:
                    act.wait_ge(summed, c - 1)
                act.activation(SQ[:, c % 2, :], X[:, c, :], ACT.Square).then_inc(squared, 1)
            act.wait_ge(summed, KC)
            act.activation(R, PS[:, 0:2, :], ACT.Sqrt, scale=1.0 / D, bias=cst(A, "eps")).then_inc(rms, 1)
            for c in range(KC):
                act.wait_ge(scaled, c + 1)
                act.activation(hi_of(H)[:, c, :], TMP[:, c % 2, :], ACT.Copy).then_inc(hi, 1)

        @block.tensor
        def _(pe):
            for c in range(KC):
                pe.wait_ge(squared, c + 1)
                for h in range(2):
                    last = pe.matmul(PS[:, h, :], cst(A, "ones"), SQ[:, c % 2, HALVES[h]],
                                     start=c == 0, stop=c == KC - 1)
                last.then_inc(summed, 1)

        @block.vector
        def _(dve):
            dve.wait_ge(rms, 1)
            dve.reciprocal(R, R).then_inc(rs, 1)
            dve.wait_ge(rs, 1)
            for c in range(KC + 1):
                if c < KC:
                    if c >= 2:
                        dve.wait_ge(lo, c - 1)
                    dve.scalar_tensor_tensor(TMP[:, c % 2, :], X[:, c, :], par(A, FFNN + c), R, ALU.mult,
                                             ALU.mult).then_inc(scaled, 1)
                if c >= 1:
                    dve.wait_ge(hi, c)
                    dve.tensor_tensor(lo_of(H)[:, c - 1, :], TMP[:, (c - 1) % 2, :],
                                      hi_of(H)[:, c - 1, :].bitcast(F32), ALU.subtract).then_inc(lo, 1)


def mlp(nc, A, PS, w_in, H, F, X, R, out, raw, W):
    GROUPS = DFF // 1024
    with ExitStack() as ctx:
        sem = ctx.enter_context(cleared_semaphores(nc, "p_"))
        loaded, rounded, split, product, begun_pool = slot_semaphores(sem)
        relu = [sem("relu0"), sem("relu1")]
        square = [sem("square0"), sem("square1")]
        hi = [sem("hi0"), sem("hi1")]
        inner = [sem("inner0"), sem("inner1")]
        added = [sem("added0"), sem("added1")]
        stored = sem("stored")
        begun = sem("inner_begun")
        block = ctx.enter_context(nc.Block())

        @block.sync
        def _(sp):
            load_weights(sp, raw, w_in, loaded, split, 8 * GROUPS)
            for s in range(2):
                sp.wait_ge(added[s], 8 * GROUPS + 1)
            sp.dma_start(out.rearrange("(c p) t -> p c t", p=P), X).then_inc(stored, 16)
            sp.wait_ge(stored, 16)

        @block.gpsimd
        def _(pool):
            split_weights(pool, raw, W, loaded, rounded, split, product, begun_pool, 8 * GROUPS)

        @block.tensor
        def _(pe):
            def tile(s, src, n, free):
                pe.wait_ge(split[s], n + 1)
                for h in range(2):
                    for sem_, count in free:
                        pe.wait_ge(sem_, count)
                    three_passes(pe, PS[:, 2 * s + h, :], W, s, src, HALVES[h]).then_inc(product[s], 1)

            with pe.Fori(0, GROUPS) as g:
                with pe.Fori(0, 4) as i:
                    for s in range(2):
                        tile(s, H, 8 * g + i, [(inner[s], 8 * g + 2 * i + 1), (added[s], 8 * g + 1)])
                for s in range(2):
                    pe.wait_ge(inner[s], 8 * g + 9)
                pe.sem_inc(begun, 1)
                with pe.Fori(0, 4) as i:
                    for s in range(2):
                        tile(s, F, 8 * g + 4 + i, [(added[s], 8 * g + 2 * i + 1)])

        @block.scalar
        def _(act):
            with act.Fori(0, GROUPS) as g:
                with act.Fori(0, 4) as i:
                    for s in range(2):
                        for h in range(2):
                            act.wait_ge(product[s], 16 * g + 2 * i + h + 1)
                            act.wait_ge(inner[s], 8 * g + 2 * i + 1)
                            act.activation(R[:, 2 * s + h, :], PS[:, 2 * s + h, :], ACT.Relu).then_inc(relu[s], 1)
                        for h in range(2):
                            act.wait_ge(square[s], 8 * g + 2 * i + h + 1)
                            act.activation(hi_of(F)[:, 2 * i + s, HALVES[h]], R[:, 2 * s + h, :],
                                           ACT.Copy).then_inc(hi[s], 1)

        @block.vector
        def _(dve):
            for s in range(2):
                dve.sem_inc(inner[s], 1)
                dve.sem_inc(added[s], 1)
            with dve.Fori(0, GROUPS) as g:
                with dve.Fori(0, 4) as i:
                    for s in range(2):
                        for h in range(2):
                            dve.wait_ge(relu[s], 8 * g + 2 * i + h + 1)
                            dve.tensor_tensor(R[:, 2 * s + h, :], PS[:, 2 * s + h, :], R[:, 2 * s + h, :],
                                              ALU.mult).then_inc(square[s], 1)
                        for h in range(2):
                            dve.wait_ge(hi[s], 8 * g + 2 * i + h + 1)
                            dve.tensor_tensor(lo_of(F)[:, 2 * i + s, HALVES[h]], R[:, 2 * s + h, :],
                                              hi_of(F)[:, 2 * i + s, HALVES[h]].bitcast(F32),
                                              ALU.subtract).then_inc(inner[s], 1)
                with dve.Fori(0, 4) as i:
                    for s in range(2):
                        for h in range(2):
                            dve.wait_ge(product[s], 16 * g + 8 + 2 * i + h + 1)
                            dve.tensor_tensor(X[:, 2 * i + s, HALVES[h]], PS[:, 2 * s + h, :], X[:, 2 * i + s, HALVES[h]],
                                              ALU.add).then_inc(added[s], 1)


class Tiles:

    def __init__(self, first, second):
        self.first, self.second = first, second

    def __getitem__(self, key):
        rows, i, *rest = key
        part, i = (self.first, i) if i < 8 else (self.second, i - 8)
        return part[(rows, i, *rest)]


def layer(nc, x, cst_in, par_in, w_nsa, w_tok, w1, w2, pos, w_rw, lora, g_up, w_gate, w_merge, w_out, w_mlp, out,
          debug=None, stage=None):
    gates = nc.dram_tensor("gates", (2 * KC, P, T), F32, kind="Internal").ap()

    def sb(ctx, name, n, dt=F32):
        return ctx.enter_context(nc.sbuf_tensor(name, [P, n], dt))

    def split_pair(ctx, name, n=8):
        return sb(ctx, name, 2 * n * 1024, F32R)[:, :].rearrange("p (x c n) -> p x c n", x=2, c=n)

    def weight_slots(ctx, tag):
        raw = sb(ctx, tag + "raw", 2048)[:, :].rearrange("p (s c n) -> p s c n", s=2, c=KC)
        W = sb(ctx, tag + "split", 4480, F32R)
        return raw, W, W[:, 0:4096].rearrange("p (s x c n) -> p s x c n", s=2, x=2, c=KC)

    with ExitStack() as whole:
        A = Arena(sb(whole, "base", BASE))
        first = sb(whole, "tiles_rk", 8 * 1024)[:, :].rearrange("p (c n) -> p c n", c=8)
        PS = whole.enter_context(nc.psum_tensor("psum", [P, 8, HALF], F32))
        with ExitStack() as mixing:
            second = sb(mixing, "tiles_v", 6 * 1024)[:, :].rearrange("p (c n) -> p c n", c=6)
            NV = Arena(sb(mixing, "attn_tiles", 8 * 1024 + 8 * TOKC))
            RJ = Tiles(first, second)
            NSA = NV.at(0, 8, 1024)
            VT = NV.at(O_VT, 8, TOKC)
            with ExitStack() as phase:
                U = split_pair(phase, "u")
                raw, W_all, W = weight_slots(phase, "a")
                SQ = raw.rearrange("p s c n -> p s (c n)")
                load_and_norm(nc, A, PS, x, cst_in, par_in, first, SQ, U)
                project(nc, A, PS, w_gate, 2 * KC, NSA[:, 0:2, :], U, raw, W, "gate", gates)
                project(nc, A, PS, w_nsa, NSA_TILES, NSA, U, raw, W, "nsa")
                project_tokens(nc, A, PS, w_tok, VT, U,
                               first[:, 0:3, :].rearrange("p c n -> p (c n)")[:, 0:KC * TOKC].rearrange("p (c n) -> p c n", c=KC),
                               W_all[:, 0:2 * KC * TOKC].rearrange("p (x c n) -> p x c n", x=2, c=KC))
                project(nc, A, PS, w_rw[0:8], 8, first, U, raw, W, "rk")
                project(nc, A, PS, w_rw[8:14], 6, second, U, raw, W, "vg")
            with ExitStack() as phase:
                WK = Arena(sb(phase, "work", WORK))
                KPAD = WK.at(0, 4, 1024)
                KPC = WK.at(22232, 2, NCMP)
                VC = WK.at(22232 + 2 * NCMP, 2, HD)
                compress(nc, A, WK, PS, NSA, KPC, VC, w1, w2, pos)
                norm_heads(nc, A, WK, PS, NSA, KPAD)
                attention(nc, A, WK, PS, NSA, KPAD, KPC, VT, VC)
                DEC = WK.at(0, PAIRS, 1024)
                AA = WK.at(4096, PAIRS, 1024)
                KN = WK.at(8192, PAIRS, 1024)
                mix_and_lora(nc, A, NV, PS, RJ, DEC, AA, KN, lora)
                rwkv_chunks(nc, A, NV, WK, PS, RJ, DEC, AA, KN)
                rwkv_scan(nc, A, NV, PS, RJ, DEC, AA)
                rwkv_out(nc, A, NV, PS, RJ, g_up)
            with ExitStack() as phase:
                Y = split_pair(phase, "ym")
                raw, _, W = weight_slots(phase, "b")
                GT = second[:, 0:4, :].rearrange("p (s x) n -> p s x n", s=2)
                split_tiles(nc, "y", [NSA[:, j, :] for j in range(PAIRS)] + [first[:, 4 + j, :] for j in range(PAIRS)], Y)
                merge(nc, A, PS, w_merge, gates, Y, NSA, GT, raw, W)
                split_tiles(nc, "m", [NSA[:, c, :] for c in range(KC)], Y)
                project_out(nc, A, PS, x, w_out, Y, first, raw, W)
        with ExitStack() as phase:
            H = split_pair(phase, "h")
            F = split_pair(phase, "f")
            raw, _, W = weight_slots(phase, "c")
            SQ = raw.rearrange("p s c n -> p s (c n)")
            R = Arena(sb(phase, "relu", 2048))
            norm_again(nc, A, PS, first, H, SQ, R.at(0, 2, 1024))
            mlp(nc, A, PS, w_mlp, H, F, first, R.at(0, 4, HALF), out, raw, W)


def tiles(w):
    k, n = w.shape
    return np.ascontiguousarray(w.reshape(k // P, P, n // P, P).transpose(2, 1, 0, 3).reshape(n // P, P, -1))


def cols(v):
    return np.asarray(v).reshape(-1, P).T


def host_layout(x, mix_norm, w_in, q_gain, k_gain, cmp_pos, cmp_w1, cmp_w2, w_attn_branch, tok_mix, w0, w_lora_up,
                a0, a_lora_up, g_lora_up, k_k, k_a, r_k, ln_x_w, ln_x_b, w_rwkv_branch, w_out, ffn_norm,
                w_ffn_up, w_ffn_down):
    W = np.asarray(w_in)[0]
    q = [np.concatenate([W[:, HD * j:HD * j + HD], W[:, HD * (j + 4):HD * (j + 4) + HD]], 1) for j in range(PAIRS)]
    kc, vc, ks, vs, kw, vw = (W[:, 512 + P * i:640 + P * i] for i in range(6))
    gates = W[:, 1280:1304]
    wa = np.asarray(w_attn_branch[0]).reshape(2, PAIRS, HD, D).transpose(1, 0, 2, 3).reshape(-1, D)
    two = lambda v: np.concatenate([v, v])
    twice = lambda v: np.repeat(cols(v), 2, axis=1)
    params = np.concatenate([
        cols(mix_norm[0]), cols(ffn_norm[0]), cols(two(q_gain[0])), *(cols(two(k_gain[0, i])) for i in range(3)),
        cols(tok_mix[0]), cols(w0[0]), cols(a0[0]), twice(k_k[0]), twice(k_a[0]), twice(r_k[0].reshape(-1)),
        cols(ln_x_w[0]), cols(ln_x_b[0])], 1)
    wtok = np.concatenate([vs, vw, gates], 1)
    c = np.ascontiguousarray
    return {
        "x": c(x[0].T), "cst": constants(), "par": c(params),
        "w_nsa": tiles(np.concatenate(q + [ks, kw, kc, vc], 1)),
        "w_tok": c(wtok.reshape(KC, P, TOKC).transpose(1, 0, 2).reshape(P, -1)),
        "w1": c(cmp_w1[0].reshape(2, 32, HD, CMP_HID).transpose(2, 0, 1, 3)),
        "w2": c(cmp_w2[0].transpose(1, 0, 2)),
        "pos": c(cmp_pos[0].transpose(2, 0, 1)),
        "w_rw": tiles(W[:, NSA_COLS:NSA_COLS + RW_TILES * P]),
        "lora": c(np.concatenate([w_lora_up[0], a_lora_up[0]], 0)), "g_up": c(g_lora_up[0]),
        "w_gate": tiles(W[:, -2 * D:]),
        "w_merge": np.concatenate([tiles(wa), tiles(w_rwkv_branch[0])], 2),
        "w_out": tiles(w_out[0]), "w_mlp": np.concatenate([x for g in range(4) for x in (
            tiles(w_ffn_up[0][:, 1024 * g:1024 * g + 1024]), tiles(w_ffn_down[0][1024 * g:1024 * g + 1024]))]),
    }


def kernel(**inputs):
    import concourse.bacc as bacc
    from concourse.bass_utils import run_bass_kernel_spmd

    nc = bacc.Bacc("TRN2", target_bir_lowering=False, num_devices=1)
    arrays = host_layout(**{k: np.asarray(v) for k, v in inputs.items()})
    args = [nc.dram_tensor(n, a.shape, mybir.dt.from_np(a.dtype), kind="ExternalInput").ap() for n, a in arrays.items()]
    out = nc.dram_tensor("out", (D, T), F32, kind="ExternalOutput").ap()
    layer(nc, *args, out)
    r = run_bass_kernel_spmd(nc, [arrays], core_ids=[0])
    return np.ascontiguousarray(r.results[0]["out"].T)[None]
```

```python
import numpy as np
import concourse.bass as bass
from concourse import mybir
from contextlib import ExitStack, contextmanager

F32 = mybir.dt.float32
BF16 = mybir.dt.bfloat16
F32R = mybir.dt.float32r
ALU = mybir.AluOpType
ACT = mybir.ActivationFunctionType
AX = mybir.AxisListType

P = 128
T = 1024
D = 1024
KC = D // P
HALF = 512
NH = 8
HD = 64
PAIRS = NH // 2
NQT = T // P
WIN_TILES = 512 // P
NCMP = (T - 32) // 16 + 1
CMP_HID = 128
DFF = 4096
NSA_TILES = 8
RW_TILES = 14
C = 64
NCH = T // C
NSA_COLS = 1304
TOKC = 280
RMS_EPS = 1e-6
GN_EPS = 64e-5
DECAY_SCALE = float(np.exp(np.float64(-0.5)))
NEG = -1e30

MIXN, FFNN, QG, KG, MU, W0, A0, KK, KA, RKP, LNW, LNB, NPAR = 0, 8, 16, 17, 20, 34, 38, 42, 50, 58, 66, 70, 74
_c = {}
_n = 0
for _name, _w in (("ident", 128), ("ones", 128), ("blockones", 128), ("diagneg", 128), ("winneg", 128),
                  ("cmask", 8 * 63), ("flag", 1), ("u_d", 64), ("u_64", 64), ("u_lt", 64),
                  ("u_le", 64), ("l_d", 64), ("l_32", 64), ("ident64", 64), ("scan", 512),
                  ("eps", 1), ("gneps", 1)):
    _c[_name] = (_n, _w)
    _n += _w
NCST = _n


def constants():
    out = np.zeros((P, NCST), np.float32)

    def put(name, a):
        o, w = _c[name]
        out[:, o:o + w] = np.asarray(a).reshape(-1, w)

    p = np.arange(P)[:, None]
    f = np.arange(P)[None, :]
    put("ident", p == f)
    put("ones", np.ones((P, P)))
    put("blockones", p // HD == f // HD)
    put("diagneg", np.where(f > p, NEG, 0.0))
    put("winneg", np.where(f <= p, NEG, 0.0))
    n = np.arange(NCMP)[None, None, :]
    q = np.arange(NQT)[None, :, None] * P + np.arange(P)[:, None, None]
    put("cmask", np.where(16 * n + 31 <= q, 0.0, NEG))
    put("flag", p >= 31)
    s = p % C
    t = np.arange(C)[None, :]
    b16 = s // 16 == t // 16
    b32 = s // 32 == t // 32
    put("u_d", (s < t) & b16)
    put("u_64", (s < t) & ~b32)
    put("u_lt", s < t)
    put("u_le", s <= t)
    put("l_d", (s > t) & b16)
    put("l_32", (s > t) & ~b16 & b32)
    put("ident64", s == t)
    put("scan", np.broadcast_to(np.arange(512) % C != 0, (P, 512)))
    put("eps", np.full((P, 1), RMS_EPS))
    put("gneps", np.full((P, 1), GN_EPS))
    return out


@contextmanager
def cleared_semaphores(nc, prefix):
    made = {}

    def sem(name):
        if name not in made:
            made[name] = nc.alloc_semaphore(prefix + name)
        return made[name]

    yield sem
    nc.clear_and_free_semaphores(list(made.values()))
    nc.all_engine_barrier()


class Arena:

    def __init__(self, tensor):
        self.t = tensor

    def at(self, off, *shape):
        n = int(np.prod(shape))
        ap = self.t[:, off:off + n]
        if len(shape) == 1:
            return ap
        names = "abcd"[:len(shape)]
        kw = {x: s for x, s in zip(names, shape)}
        return ap.rearrange("p (" + " ".join(names) + ") -> p " + " ".join(names), **kw)


O_CST = 0
O_PAR = O_CST + NCST
O_SMALL = O_PAR + NPAR
O_RSTD = O_SMALL + 160
BASE = O_RSTD + 1024
O_VT = 8 * 1024
WORK = 24064


def par(A, i, n=1):
    return A.at(O_PAR + i, n)


def cst(A, name):
    o, w = _c[name]
    return A.at(O_CST + o, w)


def hi_of(x):
    return x[:, 0]


def lo_of(x):
    return x[:, 1]


class Weights:

    def __init__(self, sem, w_in, raw, W):
        self.w_in, self.raw, self.W, self.n_pairs = w_in, raw, W, w_in.shape[0] // 2
        self.loaded, self.rounded, self.split, self.product = (
            [sem(f"{n}{s}") for s in range(2)] for n in ("loaded", "rounded", "split", "product"))
        self.begun = sem("poolbegun")

    def load(self, sp, i, s):
        sp.dma_start(self.raw[:, s], self.w_in[2 * i + s].rearrange("p (c n) -> p c n", n=P)).then_inc(self.loaded[s], 16)

    def load_first(self, sp):
        for s in range(2):
            self.load(sp, 0, s)

    def load_rest(self, sp, first, end):
        with sp.Fori(first + 1, min(end + 1, self.n_pairs)) as i:
            for s in range(2):
                sp.wait_ge(self.split[s], i)
                self.load(sp, i, s)

    def split_tile(self, pool, i, s):
        pool.wait_ge(self.loaded[s], 16 * i + 16)
        if not isinstance(i, int) or i > 0:
            pool.wait_ge(self.product[s], 2 * i)
        pool.sem_inc(self.begun, 1)
        pool.tensor_copy(self.W[:, s, 0], self.raw[:, s]).then_inc(self.rounded[s], 1)
        pool.wait_ge(self.rounded[s], i + 1)
        pool.sem_inc(self.begun, 1)
        pool.tensor_tensor(self.W[:, s, 1], self.raw[:, s], self.W[:, s, 0].bitcast(F32),
                           ALU.subtract).then_inc(self.split[s], 1)

    def split_all(self, pool, first, end):
        if first == 0:
            self.split_tile(pool, 0, 0)
            self.split_tile(pool, 0, 1)
            self.split_tile(pool, 1, 0)
        with pool.Fori(max(first, 1), min(end, self.n_pairs - 1)) as i:
            self.split_tile(pool, i, 1)
            self.split_tile(pool, i + 1, 0)
        if end == self.n_pairs:
            self.split_tile(pool, end - 1, 1)


def three_passes(pe, out, W, s, x, cols, chunks=KC):
    for c in range(chunks):
        pe.matmul(out, W[:, s, 0, c, :], hi_of(x)[:, c, cols], start=c == 0, stop=False)
        pe.matmul(out, W[:, s, 0, c, :], lo_of(x)[:, c, cols], start=False, stop=False)
        last = pe.matmul(out, W[:, s, 1, c, :], hi_of(x)[:, c, cols], start=False, stop=c == chunks - 1)
    return last


HALVES = [slice(h * HALF, (h + 1) * HALF) for h in range(2)]


def norm_and_project(nc, A, PS, x_in, cst_in, par_in, w_in, gates, X, SQ, SUM, U, raw, W, NSA, RJ):
    RSTD = A.at(O_RSTD, 1024)
    GAIN = A.at(O_SMALL, 1)
    HEAD_SQ = RJ.second[:, 0:3, 0:HALF]
    HEAD_R = RJ.second[:, 0:3, HALF:T]
    NORMED = range(KC + NSA_TILES // 2, KC + NSA_TILES // 2 + 4)

    def head_unit(i, k):
        if k < 2:
            return NSA[:, i, HALVES[k]]
        return NSA[:, 4:6, :].rearrange("p a n -> p (a n)")[:, bass.ds(i * HALF, HALF)]

    n_pairs = w_in.shape[0] // 2
    with ExitStack() as ctx:
        sem = ctx.enter_context(cleared_semaphores(nc, "u_"))
        weights = Weights(sem, w_in, raw, W)
        const_in, squared, summed, rms, rs = (sem(n) for n in ("const", "squared", "summed", "rms", "rs"))
        x = [sem("x0"), sem("x1")]
        hi, lo, added = sem("hi"), sem("lo"), sem("added")
        product, free = weights.product, [sem("free0"), sem("free1")]
        scaled = [sem("scaled0"), sem("scaled1")]
        staged = [sem("staged0"), sem("staged1")]
        kept = [sem("kept0"), sem("kept1")]
        nsa_done, head_sq, head_sum, head_root = (sem(n) for n in ("nsadone", "headsq", "headsum", "headroot"))
        head_inv, gain = sem("headinv"), sem("gain")
        head_done = sem("headdone")
        block = ctx.enter_context(nc.Block())

        @block.sync
        def _(sp):
            weights.load_first(sp)
            weights.load_rest(sp, 0, n_pairs)

        @block.gpsimd
        def _(pool):
            weights.split_all(pool, 0, n_pairs)

        @block.scalar
        def _(act):
            act.dma_start(A.at(O_PAR, NPAR), par_in).then_inc(const_in, 16)
            for c in range(2):
                act.dma_start(X[:, c, :], x_in[c * P:(c + 1) * P, :]).then_inc(x[c % 2], 16)
            act.dma_start(A.at(O_CST, NCST), cst_in).then_inc(const_in, 16)
            act.wait_ge(const_in, 32)
            for c in range(KC):
                act.wait_ge(x[c % 2], 16 * (c // 2 + 1))
                if c + 2 < KC:
                    act.dma_start(X[:, c + 2, :], x_in[(c + 2) * P:(c + 3) * P, :]).then_inc(x[c % 2], 16)
                act.activation(hi_of(U)[:, c, :], X[:, c, :], ACT.Copy, scale=par(A, MIXN + c)).then_inc(hi, 1)
                if c == 0:
                    act.activation(SUM, X[:, c, :], ACT.Square).then_inc(squared, 1)
                    continue
                if c >= 3:
                    act.wait_ge(added, c - 2)
                act.activation(SQ[:, c % 2, :], X[:, c, :], ACT.Square).then_inc(squared, 1)
            act.wait_ge(summed, 1)
            act.activation(RSTD, PS[:, 4:6, :], ACT.Sqrt, scale=1.0 / D, bias=cst(A, "eps")).then_inc(rms, 1)
            with act.Fori(0, KC) as i:
                for s in range(2):
                    for h in range(2):
                        act.wait_ge(scaled[s], 2 * i + h + 1)
                        act.activation(NSA[:, s, HALVES[h]], NSA[:, s, HALVES[h]], ACT.Tanh,
                                       scale=0.5).then_inc(staged[s], 1)
                    act.wait_ge(staged[s], 2 * i + 2)
                    act.dma_start(gates[2 * i + s], NSA[:, s, :]).then_inc(kept[s], 16)
            for s in range(2):
                act.wait_ge(kept[s], 16 * KC)
            act.wait_ge(nsa_done, 1)
            with act.Fori(0, 4) as i:
                for k in range(3):
                    act.activation(HEAD_SQ[:, k, :], head_unit(i, k), ACT.Square).then_inc(head_sq, 1)
                for k in range(3):
                    act.wait_ge(head_sum, 3 * i + k + 1)
                    act.wait_ge(head_done, 3 * i + 1)
                    act.activation(HEAD_R[:, k, :], PS[:, 4 + k, :], ACT.Sqrt, scale=1.0 / HD,
                                   bias=cst(A, "eps")).then_inc(head_root, 1)

        @block.tensor
        def _(pe):
            pe.wait_ge(const_in, 32)
            pe.wait_ge(lo, KC)
            pe.wait_ge(added, KC - 1)
            for h in range(2):
                last = pe.matmul(PS[:, 4 + h, :], cst(A, "ones"), SUM[:, HALVES[h]], start=True, stop=True)
            last.then_inc(summed, 1)

            def pair(i):
                for s in range(2):
                    pe.wait_ge(weights.split[s], i + 1)
                    for h in range(2):
                        pe.wait_ge(free[s], 2 * i + 1)
                        three_passes(pe, PS[:, 2 * s + h, :], W, s, U, HALVES[h]).then_inc(product[s], 1)

            with pe.Fori(0, NORMED.start) as i:
                pair(i)
            with pe.Fori(NORMED.start, NORMED.stop) as i:
                for k in range(3):
                    pe.wait_ge(head_sq, 3 * i - 3 * NORMED.start + k + 1)
                    pe.matmul(PS[:, 4 + k, :], cst(A, "blockones"), HEAD_SQ[:, k, :],
                              start=True, stop=True).then_inc(head_sum, 1)
                pair(i)
            with pe.Fori(NORMED.stop, n_pairs) as i:
                pair(i)

        @block.vector
        def _(dve):
            for s in range(2):
                dve.sem_inc(free[s], 1)
            for c in range(KC):
                dve.wait_ge(hi, c + 1)
                dve.scalar_tensor_tensor(lo_of(U)[:, c, :], X[:, c, :], par(A, MIXN + c),
                                         hi_of(U)[:, c, :].bitcast(F32), ALU.mult, ALU.subtract).then_inc(lo, 1)
                if c >= 1:
                    dve.wait_ge(squared, c + 1)
                    if c >= 2:
                        dve.wait_ge(added, c - 1)
                    dve.tensor_tensor(SUM, SUM, SQ[:, c % 2, :], ALU.add).then_inc(added, 1)
            dve.wait_ge(rms, 1)
            dve.reciprocal(RSTD, RSTD).then_inc(rs, 1)
            dve.wait_ge(rs, 1)

            def copy_out(out, i, s, h):
                dve.wait_ge(product[s], 2 * i + h + 1)
                last = dve.tensor_tensor(out, PS[:, 2 * s + h, :], RSTD[:, HALVES[h]], ALU.mult)
                last.then_inc(free[s], 1)

            def gate_pair(i):
                for s in range(2):
                    if not isinstance(i, int):
                        dve.wait_ge(kept[s], 16 * i)
                    for h in range(2):
                        copy_out(NSA[:, s, HALVES[h]], i, s, h)
                        dve.wait_ge(free[s], 2 * i + h + 2)
                        dve.sem_inc(scaled[s], 1)

            gate_pair(0)
            with dve.Fori(1, KC) as i:
                gate_pair(i)
            for s in range(2):
                dve.wait_ge(kept[s], 16 * KC)

            def copy_pairs(out, base, n, after=None):
                with dve.Fori(0, n) as i:
                    for k in range(4):
                        s, h = divmod(k, 2)
                        copy_out(out[:, 2 * i + s, HALVES[h]], base + i, s, h)
                        if after and k < 3:
                            after(i, k)

            def normalise(i, k):
                dve.wait_ge(head_root, 3 * i + k + 1)
                dve.reciprocal(HEAD_R[:, k, :], HEAD_R[:, k, :]).then_inc(head_inv, 1)
                dve.wait_ge(head_inv, 3 * i + k + 1)
                x = head_unit(i, k)
                if k < 2:
                    last = dve.scalar_tensor_tensor(x, x, GAIN, HEAD_R[:, k, :], ALU.mult, ALU.mult)
                else:
                    last = dve.tensor_tensor(x, x, HEAD_R[:, k, :], ALU.mult)
                last.then_inc(head_done, 1)

            dve.tensor_scalar(GAIN, par(A, QG), 0.125, None, ALU.mult).then_inc(gain, 1)
            dve.wait_ge(gain, 1)
            dve.sem_inc(head_done, 1)
            copy_pairs(NSA, KC, NSA_TILES // 2)
            for s in range(2):
                dve.wait_ge(free[s], 2 * NORMED.start + 1)
            dve.sem_inc(nsa_done, 1)
            copy_pairs(RJ.first, NORMED.start, 4, normalise)
            copy_pairs(RJ.second, NORMED.stop, RW_TILES // 2 - 4)


def project_tokens(nc, A, PS, w_in, VT, U, RAW, W):
    RSTD = A.at(O_RSTD, NQT, P)
    RT = A.at(O_SMALL + 16, NQT)
    SPARE = PS[:, :, 3 * P:4 * P]
    with (nc.semaphore("t_loaded") as loaded, nc.semaphore("t_product") as product,
          nc.semaphore("t_out") as out, nc.semaphore("t_tanh") as tanh, nc.semaphore("t_hi") as hi,
          nc.semaphore("t_lo") as lo, nc.semaphore("t_turned") as turned, nc.semaphore("t_rt") as rt,
          nc.Block() as block):
        @block.sync
        def _(sp):
            sp.dma_start(RAW, w_in.rearrange("p (c n) -> p c n", c=KC)).then_inc(loaded, 16)

        @block.tensor
        def _(pe):
            for t in range(NQT):
                last = pe.transpose(SPARE[:, t], RSTD[:, t], cst(A, "ident"))
            last.then_inc(turned, 1)
            pe.wait_ge(rt, 1)
            pe.wait_ge(lo, 1)
            for t in range(NQT):
                cols = slice(t * P, (t + 1) * P)
                for c in range(KC):
                    pe.matmul(PS[:, t, 0:TOKC], hi_of(U)[:, c, cols], W[:, 0, c, :], start=c == 0, stop=False)
                    pe.matmul(PS[:, t, 0:TOKC], hi_of(U)[:, c, cols], W[:, 1, c, :], start=False, stop=False)
                    last = pe.matmul(PS[:, t, 0:TOKC], lo_of(U)[:, c, cols], W[:, 0, c, :], start=False,
                                     stop=c == KC - 1)
                last.then_inc(product, 1)

        @block.vector
        def _(dve):
            dve.wait_ge(turned, 1)
            dve.tensor_copy(RT, SPARE[:, :, 0]).then_inc(rt, 1)
            dve.wait_ge(rt, 1)
            dve.wait_ge(hi, 1)
            dve.tensor_tensor(W[:, 1], RAW, W[:, 0].bitcast(F32), ALU.subtract).then_inc(lo, 1)
            for t in range(NQT):
                dve.wait_ge(product, t + 1)
                dve.tensor_scalar(VT[:, t, :], PS[:, t, 0:TOKC], RT[:, t:t + 1], None, ALU.mult).then_inc(out, 1)
            dve.wait_ge(tanh, 1)
            dve.tensor_scalar(VT[:, :, 256:TOKC], VT[:, :, 256:TOKC], 0.5, 0.5, ALU.mult, ALU.add)

        @block.scalar
        def _(act):
            act.wait_ge(loaded, 16)
            act.activation(W[:, 0], RAW, ACT.Copy).then_inc(hi, 1)
            act.wait_ge(out, NQT)
            act.activation(VT[:, :, 256:TOKC], VT[:, :, 256:TOKC], ACT.Tanh, scale=0.5).then_inc(tanh, 1)


def compress(nc, A, WK, PS, NSA, KPAD, KPC, VC, w1_in, w2_in, pos_in):
    W1 = WK.at(6144, 2, 16, CMP_HID)
    KV = WK.at(10240, 2, 2, 1024)
    MOVE = WK.at(14336, 2, 1024)
    POS = WK.at(16384, 2, 32)
    W2 = WK.at(16448, 2, HD)
    H = WK.at(16576, 4, CMP_HID)
    Q = WK.at(17088, 4, CMP_HID)
    HT = WK.at(17600, 4, NCMP)
    SQC = WK.at(17852, NCMP)
    KR = WK.at(17915, NCMP)
    SHIFTED = 1024 - 16
    with ExitStack() as ctx:
        sem = ctx.enter_context(cleared_semaphores(nc, "c_"))
        loaded, loaded2, to_move, posed = (sem(n) for n in ("loaded", "loaded2", "tomove", "posed"))
        moved = [sem("moved_k"), sem("moved_v")]
        hidden, copied, c_squared, inner, tanh, gelu, turned, turned_out, out2, k_sq, k_sum, k_root, step = (
            sem(x) for x in ("hidden", "copied", "squared", "inner", "tanh", "gelu", "turned",
                             "turnedout", "out2", "ksq", "ksum", "kroot", "step"))
        block = ctx.enter_context(nc.Block())

        @block.gpsimd
        def _(pool):
            for b in range(2):
                pool.memset(KPAD[64:128, 2 * b, :], 0.0)
                pool.memset(KPAD[0:64, 2 * b + 1, :], 0.0)

        @block.sync
        def _(sp):
            for half in range(2):
                sp.dma_start(POS[64 * half:64 * half + 64], pos_in).then_inc(loaded2, 16)
            sp.dma_start(W2, w2_in).then_inc(loaded2, 16)
            sp.dma_start(W1, w1_in).then_inc(loaded, 16)
            for v in range(2):
                sp.wait_ge(to_move, 2 * v + 2)
                sp.dma_start(KV[64:128, v, 0, 0:SHIFTED], MOVE[0:64, v, 0:SHIFTED]).then_inc(moved[v], 16)
                sp.dma_start(KV[0:64, v, 1, :], MOVE[64:128, v, :]).then_inc(moved[v], 16)
            for v in range(2):
                sp.wait_ge(moved[v], 32)

        @block.vector
        def _(dve):
            def with_position(dst, rows, v, second, done_):
                at = 16 * second
                n = 1024 - at
                dve.tensor_tensor(dst[:, 0:n].rearrange("p (n s) -> p n s", s=16),
                                  NSA[rows, 6 + v, at:1024].rearrange("p (n s) -> p n s", s=16),
                                  POS[rows, v, at:at + 16].unsqueeze(1).to_broadcast([64, n // 16, 16]),
                                  ALU.add).then_inc(done_, 1)

            low, high = slice(0, 64), slice(64, 128)
            dve.wait_ge(loaded2, 48)
            for v in range(2):
                with_position(MOVE[low, v, :], low, v, 1, to_move)
                with_position(MOVE[high, v, :], high, v, 0, to_move)
                with_position(KV[low, v, 0, :], low, v, 0, posed)
                with_position(KV[high, v, 1, :], high, v, 1, posed)
            dve.wait_ge(hidden, 4)
            dve.tensor_copy(H[0:NCMP], PS[0:NCMP, 2, :].rearrange("p (a n) -> p a n", a=4)).then_inc(copied, 1)
            dve.wait_ge(c_squared, 1)
            dve.tensor_scalar(Q[0:NCMP], Q[0:NCMP], 0.044715, 1.0, ALU.mult, ALU.add).then_inc(step, 1)
            dve.wait_ge(step, 1)
            dve.tensor_tensor(Q[0:NCMP], Q[0:NCMP], H[0:NCMP], ALU.mult).then_inc(inner, 1)
            dve.wait_ge(tanh, 1)
            dve.scalar_tensor_tensor(H[0:NCMP], Q[0:NCMP], 1.0, H[0:NCMP], ALU.add, ALU.mult).then_inc(gelu, 1)
            dve.wait_ge(turned, 1)
            dve.tensor_scalar(HT, PS[:, 4, 0:4 * NCMP].rearrange("p (a n) -> p a n", a=4), 0.5, None,
                              ALU.mult).then_inc(turned_out, 1)
            dve.wait_ge(out2, 1)
            dve.tensor_copy(VC[0:NCMP], PS[0:NCMP, 6, 0:2 * HD].rearrange("p (g d) -> p g d", g=2))
            dve.memset(KPC, 0.0).then_inc(step, 1)
            dve.wait_ge(k_root, 1)
            dve.reciprocal(KR, KR).then_inc(step, 1)
            dve.wait_ge(step, 3)
            for g in range(2):
                rows = slice(64 * g, 64 * g + 64)
                dve.scalar_tensor_tensor(KPC[rows, g, :], PS[rows, 5, 0:NCMP], par(A, KG)[rows], KR[rows, :],
                                         ALU.mult, ALU.mult)

        @block.tensor
        def _(pe):
            pe.wait_ge(loaded, 16)
            for v in range(2):
                pe.wait_ge(posed, 2 * v + 2)
                pe.wait_ge(moved[v], 32)
                for g in range(2):
                    kv = KV[:, v, g, :].rearrange("p (n s) -> p n s", s=16)
                    at = (2 * v + g) * CMP_HID
                    for p in range(16):
                        last = pe.matmul(PS[0:NCMP, 2, at:at + CMP_HID], kv[:, 0:NCMP, p], W1[:, v, p, :],
                                         start=p == 0, stop=p == 15)
                    last.then_inc(hidden, 1)
            pe.wait_ge(gelu, 1)
            for a in range(4):
                last = pe.transpose(PS[:, 4, a * NCMP:(a + 1) * NCMP], H[0:NCMP, a, :], cst(A, "ident")[0:NCMP, 0:NCMP])
            last.then_inc(turned, 1)
            pe.wait_ge(turned_out, 1)
            for g in range(2):
                pe.matmul(PS[64 * g:64 * g + 64, 5, 0:NCMP], W2[:, 0, :], HT[:, g, :], start=True, stop=True)
            for g in range(2):
                last = pe.matmul(PS[0:NCMP, 6, g * HD:(g + 1) * HD], HT[:, 2 + g, :], W2[:, 1, :], start=True, stop=True)
            last.then_inc(out2, 1)
            pe.wait_ge(k_sq, 1)
            pe.matmul(PS[:, 7, 0:NCMP], cst(A, "blockones"), SQC, start=True, stop=True).then_inc(k_sum, 1)

        @block.scalar
        def _(act):
            for b in range(2):
                for g in range(2):
                    rows = slice(64 * g, 64 * g + 64)
                    act.activation(KPAD[rows, 2 * b + g, :], NSA[rows, 4 + b, :], ACT.Copy,
                                   scale=par(A, KG + 1 + b)[rows])
            act.wait_ge(copied, 1)
            act.activation(Q[0:NCMP], H[0:NCMP], ACT.Square).then_inc(c_squared, 1)
            act.wait_ge(inner, 1)
            act.activation(Q[0:NCMP], Q[0:NCMP], ACT.Tanh, scale=float(np.sqrt(2.0 / np.pi))).then_inc(tanh, 1)
            act.wait_ge(out2, 1)
            act.activation(SQC, PS[:, 5, 0:NCMP], ACT.Square).then_inc(k_sq, 1)
            act.wait_ge(k_sum, 1)
            act.activation(KR, PS[:, 7, 0:NCMP], ACT.Sqrt, scale=1.0 / HD, bias=cst(A, "eps")).then_inc(k_root, 1)


MIX_ORDER = [12, 13] + list(range(4, 8)) + list(range(0, 4)) + list(range(8, 12))


def token_shift(dve, A, RJ, DIFF, n, diff, mixed):
    i, b = MIX_ORDER[n], n % 2
    if n >= 2:
        dve.wait_ge(mixed, n - 1)
    dve.tensor_tensor(DIFF[:, b, 1:T], RJ[:, i, 0:T - 1], RJ[:, i, 1:T], ALU.subtract)
    dve.tensor_scalar(DIFF[:, b, 0:1], RJ[:, i, 0:1], -1.0, None, ALU.mult).then_inc(diff, 1)
    dve.wait_ge(diff, n + 1)
    dve.scalar_tensor_tensor(RJ[:, i, :], DIFF[:, b, :], par(A, MU + i), RJ[:, i, :],
                             ALU.mult, ALU.add).then_inc(mixed, 1)


def attention(nc, A, WK, PS, NSA, KPAD, KPC, VT, VC, RJ):
    DIFF = WK.at(14336, 2, 1024)
    PT = WK.at(4096, 2, 14, P)
    PB = WK.at(8192, 2, 1728)
    QB = WK.at(12288, P)
    at = 12416
    IDENTB = WK.at(at, 64).bitcast(BF16)
    DIAGB = WK.at(at + 64, 64).bitcast(BF16)
    WINB = WK.at(at + 128, 64).bitcast(BF16)
    NM = WK.at(at + 192, 2, 3)
    L = WK.at(at + 198, 2, 3)
    RL = WK.at(at + 204, 2, 3)
    SC = WK.at(at + 210, 2, 3)
    OT = WK.at(at + 216, 2, HD)
    CMP, SLC, WIN = 0, 1, 2
    S_slc = PS[:, 0:2, :].rearrange("p a n -> p (a n)")
    S_win = PS[:, 2:4, :].rearrange("p a n -> p (a n)")
    CMP_AT = 640
    T_BANK = 4
    O = PS[:, 7, 0:6 * HD].rearrange("p (g b d) -> p g b d", g=2, b=3)
    FLIP = PS[:, 7, 6 * HD:6 * HD + P]
    KINDS = {"cmp": CMP, "slc": SLC, "win": WIN}

    def window(qt):
        return max(0, qt - WIN_TILES), qt + 1

    def blocks(qt):
        lo, hi = window(qt)
        return ([("slc", k, k * P) for k in range(qt + 1)]
                + [("win", k, 1024 + (k - lo) * P) for k in range(lo, hi)] + [("cmp", 0, 1664)])

    def chunks(qt):
        b = list(enumerate(blocks(qt)))
        return [b[k:k + 4] for k in range(0, len(b), 4)]

    def evacuated_by(qt):
        return [k % 2 for k in range(len(chunks(qt)))]

    n_chunks = [len(chunks(qt)) for qt in range(NQT)]
    per_engine = [[evacuated_by(qt).count(e) for qt in range(NQT)] for e in range(2)]

    def unit(qt, j, g):
        return 8 * qt + 2 * j + g

    def chunk_count(qt, j, g, k):
        return 8 * sum(n_chunks[:qt]) + (2 * j + g) * n_chunks[qt] + k + 1

    def out_count(e, qt, j, g, k):
        return (8 * sum(per_engine[e][:qt]) + (2 * j + g) * per_engine[e][qt]
                + evacuated_by(qt)[:k + 1].count(e))

    nothing = lambda *unit: None

    def in_order(eng, scores, values, turn, flip, between=nothing):
        scores(0, 0, 0)
        for qt in range(NQT):
            scores(qt, 0, 1)
            if qt > 0:
                values(qt - 1, PAIRS - 1, 1)
            turn(qt, 0, 0)
            if qt > 0:
                flip(qt - 1, PAIRS - 1)
                between(2 * qt - 2)

            def pair(j):
                scores(qt, j + 1, 0)
                values(qt, j, 0)
                turn(qt, j, 1)
                scores(qt, j + 1, 1)
                values(qt, j, 1)
                turn(qt, j + 1, 0)
                flip(qt, j)

            if qt == 0:
                for j in range(PAIRS - 1):
                    pair(j)
            else:
                with eng.Fori(0, PAIRS - 1) as j:
                    pair(j)
            if qt + 1 < NQT:
                scores(qt + 1, 0, 0)
            values(qt, PAIRS - 1, 0)
            turn(qt, PAIRS - 1, 1)
            if qt > 0:
                between(2 * qt - 1)
        values(NQT - 1, PAIRS - 1, 1)
        flip(NQT - 1, PAIRS - 1)

    with ExitStack() as ctx:
        sem = ctx.enter_context(cleared_semaphores(nc, "a_"))
        masks = sem("masks")
        q_copied = sem("qcopied")
        scored_slc = sem("scoredslc")
        scored_win = sem("scoredwin")
        maxed = sem("maxed")
        exp_slc = sem("expslc")
        exp_win = sem("expwin")
        inverse = sem("inverse")
        unseen = sem("unseen")
        factor = sem("factor")
        turned = sem("turned")
        out_by = [sem("outact"), sem("outdve")]
        product = sem("product")
        combined = sem("combined")
        flipped = sem("flipped")
        stored = sem("stored")
        begun = sem("begun")
        diff, mixed = sem("diff"), sem("mixed")
        block = ctx.enter_context(nc.Block())

        @block.gpsimd
        def _(pool):
            for dst, name in ((IDENTB, "ident"), (DIAGB, "diagneg"), (WINB, "winneg")):
                last = pool.tensor_copy(dst, cst(A, name))
            last.then_inc(masks, 1)

            def scores(qt, j, g):
                if g == 0:
                    if not (isinstance(j, int) and unit(qt, j, g) == 0):
                        pool.wait_ge(scored_win, unit(qt, j, g))
                    pool.tensor_copy(QB, NSA[:, j, qt * P:(qt + 1) * P]).then_inc(q_copied, 1)

            in_order(pool, scores, nothing, nothing, nothing)

        @block.tensor
        def _(pe):
            pe.wait_ge(masks, 1)

            def scores(qt, j, g):
                u = unit(qt, j, g)
                first = isinstance(u, int) and u == 0
                lo, hi = window(qt)
                pe.wait_ge(q_copied, 4 * qt + j + 1)
                if not first:
                    pe.wait_ge(exp_slc, u)
                n = (qt + 1) * P
                for b in range(0, n, HALF):
                    w = min(HALF, n - b)
                    diag = b + w == n
                    pe.matmul(S_slc[:, b:b + w], QB, KPAD[:, g, b:b + w], start=True, stop=not diag)
                last = pe.matmul(S_slc[:, n - P:n], IDENTB, DIAGB, start=False, stop=True)
                last.then_inc(scored_slc, 1)
                if not first:
                    pe.wait_ge(exp_win, u)
                n = (hi - lo) * P
                for b in range(0, n, HALF):
                    w = min(HALF, n - b)
                    old = b == 0 and qt >= WIN_TILES
                    diag = b + w == n
                    pe.matmul(S_win[:, b:b + w], QB, KPAD[:, 2 + g, lo * P + b:lo * P + b + w], start=True,
                              stop=not (old or diag))
                    if old:
                        pe.matmul(S_win[:, 0:P], IDENTB, WINB, start=False, stop=not diag)
                    if diag:
                        pe.matmul(S_win[:, n - P:n], IDENTB, DIAGB, start=False, stop=True)
                pe.matmul(S_win[:, CMP_AT:CMP_AT + NCMP], QB, KPC[:, g, :], start=True, stop=False)
                last = pe.matmul(S_win[:, CMP_AT:CMP_AT + NCMP], cst(A, "ident"),
                                 cst(A, "cmask")[:, qt * NCMP:(qt + 1) * NCMP], start=False, stop=True)
                last.then_inc(scored_win, 1)

            def values(qt, j, g):
                u = unit(qt, j, g)
                for e in range(2):
                    if per_engine[e][qt]:
                        pe.wait_ge(out_by[e], out_count(e, qt, j, g, n_chunks[qt] - 1))
                if not (isinstance(u, int) and u == 0):
                    pe.wait_ge(combined, 3 * u)
                if not (isinstance(u, int) and u < 2):
                    pe.wait_ge(stored, 4 * qt + j)
                pe.sem_inc(begun, 1)
                todo = blocks(qt)
                for x, (kind, k, _) in enumerate(todo):
                    rows = NCMP if kind == "cmp" else P
                    v = (VC[0:NCMP, g, :] if kind == "cmp" else
                         VT[:, k, (kind == "win") * P + g * HD:(kind == "win") * P + (g + 1) * HD])
                    same = [y for y, t in enumerate(todo) if t[0] == kind]
                    last = pe.matmul(O[:, g, KINDS[kind], :], PT[0:rows, g, x, :], v,
                                     start=x == same[0], stop=x == same[-1])
                last.then_inc(product, 1)

            def turn(qt, j, g):
                u = unit(qt, j, g)
                pe.wait_ge(exp_slc, u + 1)
                for k, chunk in enumerate(chunks(qt)):
                    kinds = {kind for _, (kind, _, _) in chunk}
                    if kinds & {"win", "cmp"}:
                        pe.wait_ge(exp_win, u + 1)
                    if k >= 3:
                        e = evacuated_by(qt)[k - 3]
                        pe.wait_ge(out_by[e], out_count(e, qt, j, g, k - 3))
                    pe.sem_inc(begun, 1)
                    for x, (_, (kind, _, col)) in enumerate(chunk):
                        if kind == "cmp":
                            last = pe.transpose(PS[0:NCMP, T_BANK + k % 3, x * P:(x + 1) * P],
                                                PB[:, g, col:col + NCMP], cst(A, "ident"))
                        else:
                            last = pe.transpose(PS[:, T_BANK + k % 3, x * P:(x + 1) * P],
                                                PB[:, g, col:col + P], cst(A, "ident"))
                    last.then_inc(turned, 1)

            def flip(qt, j):
                n = 4 * qt + j
                pe.wait_ge(combined, 6 * n + 6)
                pe.sem_inc(begun, 1)
                pe.transpose(FLIP, OT, cst(A, "ident")).then_inc(flipped, 1)

            in_order(pe, scores, values, turn, flip)

        def copy_out(eng, e, copy, qt, j, g):
            for k, chunk in enumerate(chunks(qt)):
                if evacuated_by(qt)[k] != e:
                    continue
                eng.wait_ge(turned, chunk_count(qt, j, g, k))
                x0 = chunk[0][0]
                whole = [c for c in chunk if c[1][0] != "cmp"]
                if whole:
                    last = copy(PT[:, g, x0:x0 + len(whole), :],
                                PS[:, T_BANK + k % 3, 0:len(whole) * P].rearrange("p (a n) -> p a n", n=P))
                if len(whole) < len(chunk):
                    x = len(whole)
                    last = copy(PT[0:NCMP, g, x0 + x, :], PS[0:NCMP, T_BANK + k % 3, x * P:(x + 1) * P])
                last.then_inc(out_by[e], 1)

        @block.vector
        def _(dve):
            def scores(qt, j, g):
                u = unit(qt, j, g)
                lo, hi = window(qt)
                dve.wait_ge(scored_slc, u + 1)
                dve.tensor_reduce(NM[:, g, SLC:SLC + 1], S_slc[:, 0:(qt + 1) * P], axis=AX.X, op=ALU.max,
                                  negate=True).then_inc(maxed, 1)
                dve.wait_ge(scored_win, u + 1)
                dve.tensor_reduce(NM[:, g, WIN:WIN + 1], S_win[:, 0:(hi - lo) * P], axis=AX.X, op=ALU.max,
                                  negate=True).then_inc(maxed, 1)
                dve.tensor_reduce(NM[:, g, CMP:CMP + 1], S_win[:, CMP_AT:CMP_AT + NCMP], axis=AX.X, op=ALU.max,
                                  negate=True).then_inc(maxed, 1)

            def values(qt, j, g):
                u = unit(qt, j, g)
                dve.wait_ge(product, u + 1)
                if not (isinstance(u, int) and u < 2):
                    dve.wait_ge(flipped, 4 * qt + j)
                dve.tensor_scalar(OT[:, g, :], O[:, g, 0, :], SC[:, g, 0:1], None, ALU.mult).then_inc(combined, 1)
                for b in (1, 2):
                    dve.wait_ge(combined, 3 * u + b)
                    dve.scalar_tensor_tensor(OT[:, g, :], O[:, g, b, :], SC[:, g, b:b + 1], OT[:, g, :], ALU.mult,
                                             ALU.add).then_inc(combined, 1)

            def turn(qt, j, g):
                u = unit(qt, j, g)
                copy_out(dve, 1, lambda o, i: dve.tensor_copy(o, i), qt, j, g)
                dve.wait_ge(exp_win, u + 1)
                dve.reciprocal(RL[:, g, :], L[:, g, :]).then_inc(inverse, 1)
                dve.wait_ge(inverse, u + 1)
                if qt == 0:
                    dve.tensor_tensor(RL[:, g, CMP:CMP + 1], RL[:, g, CMP:CMP + 1], cst(A, "flag"),
                                      ALU.mult).then_inc(unseen, 1)
                    dve.wait_ge(unseen, u + 1)
                gate = VT[:, qt, 256:TOKC].rearrange("p (g j c) -> p g j c", g=2, c=3)[:, g, j, :]
                dve.tensor_tensor(SC[:, g, :], RL[:, g, :], gate, ALU.mult).then_inc(factor, 1)
                dve.wait_ge(factor, u + 1)

            in_order(dve, scores, values, turn, nothing,
                     lambda n: token_shift(dve, A, RJ, DIFF, n, diff, mixed))

        @block.scalar
        def _(act):
            def scores(qt, j, g):
                u = unit(qt, j, g)
                lo, hi = window(qt)
                if not (isinstance(u, int) and u < 2):
                    act.wait_ge(turned, free_count(qt, j, g))
                    act.wait_ge(inverse, u - 1)
                act.wait_ge(maxed, 3 * u + 1)
                act.activation(PB[:, g, 0:(qt + 1) * P], S_slc[:, 0:(qt + 1) * P], ACT.Exp,
                               bias=NM[:, g, SLC:SLC + 1], accum_out=L[:, g, SLC:SLC + 1]).then_inc(exp_slc, 1)
                act.wait_ge(maxed, 3 * u + 3)
                act.activation(PB[:, g, 1024:1024 + (hi - lo) * P], S_win[:, 0:(hi - lo) * P], ACT.Exp,
                               bias=NM[:, g, WIN:WIN + 1], accum_out=L[:, g, WIN:WIN + 1])
                act.activation(PB[:, g, 1664:1664 + NCMP], S_win[:, CMP_AT:CMP_AT + NCMP], ACT.Exp,
                               bias=NM[:, g, CMP:CMP + 1], accum_out=L[:, g, CMP:CMP + 1]).then_inc(exp_win, 1)

            def free_count(qt, j, g):
                if isinstance(j, int):
                    q0, r = divmod(unit(qt, j, g) - 2, 8)
                    return chunk_count(q0, r // 2, r % 2, n_chunks[q0] - 1)
                return chunk_count(qt, j - 1, g, n_chunks[qt] - 1)

            def turn(qt, j, g):
                copy_out(act, 0, lambda o, i: act.activation(o, i, ACT.Copy), qt, j, g)

            def flip(qt, j):
                n = 4 * qt + j
                act.wait_ge(flipped, n + 1)
                act.activation(NSA[:, j, qt * P:(qt + 1) * P], FLIP, ACT.Copy).then_inc(stored, 1)

            in_order(act, scores, nothing, turn, flip)


def decay_and_keys(nc, A, NV, WK, PS, RJ, DEC, AA, KN, lora_in):
    R = NV.at(4 * 1024, 8, HALF)
    SQ = WK.at(14336, 2, HALF)
    LORA = NV.at(O_VT, HALF)
    HALFB = A.at(O_SMALL, 8)
    units = [(j, slice(h * HALF, (h + 1) * HALF)) for j in range(PAIRS) for h in range(2)]
    with ExitStack() as ctx:
        sem = ctx.enter_context(cleared_semaphores(nc, "m_"))
        loaded, tanh_in, product, tanh_out = (sem(x) for x in ("loaded", "tanhin", "product", "tanhout"))
        squared, summed, clamped, root, inverse, half_bias = (
            sem(x) for x in ("squared", "summed", "clamped", "root", "inverse", "halfbias"))
        block = ctx.enter_context(nc.Block())

        @block.sync
        def _(sp):
            sp.dma_start(LORA, lora_in).then_inc(loaded, 16)

        @block.vector
        def _(dve):
            dve.tensor_scalar(HALFB, par(A, W0, 8), 0.5, None, ALU.mult).then_inc(half_bias, 1)
            for n in range(len(units)):
                dve.wait_ge(summed, n + 1)
                dve.tensor_scalar(R[:, n, :], PS[:, n % 2, :], 1e-24, None, ALU.max).then_inc(clamped, 1)

            def affine(n):
                j, cols = units[n]
                dve.wait_ge(tanh_out, 2 * n + 2)
                dve.tensor_scalar(DEC[:, j, cols], DEC[:, j, cols], -0.5 * DECAY_SCALE, -0.5 * DECAY_SCALE,
                                  ALU.mult, ALU.add)
                dve.tensor_scalar(AA[:, j, cols], AA[:, j, cols], 0.5, 0.5, ALU.mult, ALU.add)

            for n, (j, cols) in enumerate(units):
                dve.wait_ge(root, n + 1)
                dve.reciprocal(R[:, n, :], R[:, n, :]).then_inc(inverse, 1)
                dve.wait_ge(inverse, n + 1)
                dve.scalar_tensor_tensor(KN[:, j, cols], RJ[:, 4 + j, cols], par(A, KK + 2 * j), R[:, n, :],
                                         ALU.mult, ALU.mult)
                if n >= 2:
                    affine(n - 2)
            affine(len(units) - 2)
            affine(len(units) - 1)
            dve.wait_ge(tanh_in, 2)
            dve.tensor_scalar(RJ[:, 13, :], RJ[:, 13, :], 0.5, 0.5, ALU.mult, ALU.add)

        @block.scalar
        def _(act):
            act.activation(RJ[0:64, 12, :], RJ[0:64, 12, :], ACT.Tanh).then_inc(tanh_in, 1)
            act.activation(RJ[:, 13, :], RJ[:, 13, :], ACT.Tanh, scale=0.5).then_inc(tanh_in, 1)
            for n, (j, cols) in enumerate(units):
                if n >= 2:
                    act.wait_ge(summed, n - 1)
                act.activation(SQ[:, n % 2, :], RJ[:, 4 + j, cols], ACT.Square, scale=par(A, KK + 2 * j)).then_inc(squared, 1)
            for n in range(len(units)):
                act.wait_ge(clamped, n + 1)
                act.activation(R[:, n, :], R[:, n, :], ACT.Sqrt).then_inc(root, 1)
            act.wait_ge(half_bias, 1)
            for n, (j, cols) in enumerate(units):
                for x, dst in enumerate((DEC, AA)):
                    act.wait_ge(product, 2 * n + x + 1)
                    act.activation(dst[:, j, cols], PS[:, 2 + 2 * x + n % 2, :], ACT.Tanh, scale=0.5,
                                   bias=HALFB[:, 4 * x + j:4 * x + j + 1]).then_inc(tanh_out, 1)

        @block.tensor
        def _(pe):
            for n in range(len(units)):
                pe.wait_ge(squared, n + 1)
                if n >= 2:
                    pe.wait_ge(clamped, n - 1)
                pe.matmul(PS[:, n % 2, :], cst(A, "blockones"), SQ[:, n % 2, :], start=True, stop=True).then_inc(summed, 1)
            pe.wait_ge(loaded, 16)
            pe.wait_ge(tanh_in, 1)
            for n, (j, cols) in enumerate(units):
                for x in range(2):
                    if n >= 2:
                        pe.wait_ge(tanh_out, 2 * n + x - 3)
                    rows = slice(64 * x, 64 * x + 64)
                    pe.matmul(PS[:, 2 + 2 * x + n % 2, :], LORA[rows, j * P:(j + 1) * P],
                              RJ[rows, 12, cols], start=True, stop=True).then_inc(product, 1)


def rwkv_chunks(nc, A, NV, WK, PS, RJ, DEC, AA, KN):
    R8, K8, V8, D8, A8, KN8 = (x.rearrange("p a (b n) -> p (a b) n", b=2)
                               for x in (RJ.first[:, 0:4, :], RJ.first[:, 4:8, :], RJ.second[:, 0:4, :], DEC, AA, KN))
    room = [NV.at(4 * 1024 + 512 * x, 8, C) for x in range(8)] + [NV.at(O_VT + 512 * x, 8, C) for x in range(4)]
    room += [WK.at(x, 8, C) for x in range(14 * 1024, WORK - 511, 512)]
    names = iter(room)

    def temp():
        return next(names)

    def flat(x):
        return x.rearrange("p a b -> p (a b)")

    AR = RJ.second[:, 4, :].rearrange("p (x a b) -> p x a b", x=2, b=C)
    AMV = WK.at(12 * 1024, 8, 2, C)
    GH = WK.at(13 * 1024, 8, 2, C)
    LW, E0, E1, E2, KM, Bf, Kf, Kc, DG = (temp() for _ in range(9))
    Bc = LW
    Vt, Bt, Kt = (temp() for _ in range(3))
    V_IN = temp()
    RB, RK = (temp() for _ in range(2))
    N1, L1, N2, L2, L32, N64, MT, Z = ([temp().rearrange("p a n -> p (a n)").rearrange("p (a n) -> p a n", n=P)
                                        for _ in range(2)] for _ in range(8))
    N4, L4 = N1, L1
    L8, TT, X = L2, N2, L1
    G2 = [x.rearrange("p a (x n) -> p a x n", x=2) for x in L2]

    def bc(ap):
        return ap.unsqueeze(1).to_broadcast([P, 8, C])

    def bank(b):
        return PS[:, b, :].rearrange("p (a n) -> p a n", n=C)

    def part(x, f):
        return x[:, 4 * f:4 * f + 4, :]

    def squares(b):
        return PS[:, b, :].rearrange("p (a n) -> p a n", n=P)

    def wide(b):
        return PS[:, b:b + 2, :].rearrange("p b (a x n) -> p (b a) x n", x=2, n=C)

    def split(b):
        return PS[:, b:b + 2, 0:4 * C].rearrange("p s (m n) -> p s m n", n=C)

    def duo(b):
        return PS[:, b:b + 2, :].rearrange("p s (m x n) -> p s m x n", x=2, n=C)

    def halves(x):
        return x.rearrange("p (m s) n -> p s m n", s=2)

    def bc3(ap):
        return ap.unsqueeze(1).unsqueeze(1).to_broadcast([P, 2, 4, C])

    def dual(b, m):
        return PS[:, b, m * P:(m + 1) * P]

    units = [(m, h, c) for m in range(4) for h in range(2) for c in range(2)]
    rows = lambda x: slice(64 * x, 64 * x + 64)
    W_LAST = E1[:, :, C - 1:C].to_broadcast([P, 8, C])

    with ExitStack() as ctx:
        sem = ctx.enter_context(cleared_semaphores(nc, "r_"))
        block = ctx.enter_context(nc.Block())

        @block.gpsimd
        def _(pool):
            pool.tensor_copy(flat(V_IN), V8[:, 0, :]).then_inc(sem("v_in"), 1)
            with pool.Fori(1, 8) as it:
                pool.wait_ge(sem("t_v"), it)
                pool.tensor_copy(flat(V_IN), V8[:, it, :]).then_inc(sem("v_in"), 1)

        @block.scalar
        def _(act):
            act.sem_inc(sem("y0"), 1)
            act.sem_inc(sem("qq"), 1)

            def decays(it):
                act.wait_ge(sem("lw"), it + 1)
                act.activation(E2, LW, ACT.Exp, scale=-1.0).then_inc(sem("e2"), 1)
                act.activation(E1, LW, ACT.Exp).then_inc(sem("e1"), 1)
                act.wait_ge(sem("lwx"), it + 1)
                act.activation(E0, E0, ACT.Exp).then_inc(sem("e0"), 1)

            def turn(it, last):
                def wait(n):
                    act.wait_ge(sem(n), it + 1)

                def copy(dst, src, done):
                    act.activation(dst, src, ACT.Copy).then_inc(sem(done), 1)

                wait("t_v")
                copy(flat(Vt), PS[:, 6, :], "v_out")
                wait("t_b")
                copy(flat(Bt), PS[:, 7, :], "b_out")
                wait("t_k")
                copy(flat(Kt), PS[:, 2, :], "k_out")
                wait("t_a")
                copy(AMV[:, :, 0, :], bank(3), "a_out")
                for f in range(2):
                    wait(f"p_l2{f}")
                    copy(L2[f], squares(f), f"l2{f}")
                wait("p_mv")
                copy(AMV[:, :, 1, :], bank(5), "mv")
                for f in range(2):
                    wait(f"p_l4{f}")
                    copy(L4[f], squares(f), f"l4{f}")
                for f in range(2):
                    wait(f"p_l8{f}")
                    copy(L8[f], squares(f), f"l8{f}")
                for f in range(2):
                    wait(f"p_xt{f}")
                    copy(X[f], squares(f), f"x{f}")
                    copy(TT[f], squares(2 + f), f"tt{f}")
                for f in range(2):
                    wait(f"p_g1{f}")
                    copy(part(GH, f), part(wide(0), f), f"g1{f}")
                for f in range(2):
                    wait(f"p_g2{f}")
                    copy(G2[f], part(wide(0), f), f"g2{f}")
                if not last:
                    decays(it + 1)
                wait("p_y0")
                copy(halves(K8[:, it, :].rearrange("p (a b) -> p a b", b=C)), split(4), "y0")
                wait("p_q")
                copy(halves(A8[:, it, :].rearrange("p (a b) -> p a b", b=C)), split(0), "qq")

            decays(0)
            with act.Fori(0, 7) as it:
                turn(it, False)
            turn(7, True)

        @block.vector
        def _(dve):
            dve.sem_inc(sem("r2"), 1)
            dve.sem_inc(sem("pp"), 1)

            def tools(it):
                def wait(n):
                    dve.wait_ge(sem(n), it + 1)

                def mul(dst, a, b, done):
                    dve.tensor_tensor(dst, a, b, ALU.mult).then_inc(sem(done), 1)

                def add(dst, a, b, done):
                    dve.tensor_tensor(dst, a, b, ALU.add).then_inc(sem(done), 1)

                def eight(x):
                    return x[:, it, :].rearrange("p (a b) -> p a b", b=C)

                def column(i):
                    return A.at(O_PAR + i, 8)[:, bass.ds(it, 1)]

                return wait, mul, add, eight, column

            def decayed(it):
                wait, mul, add, eight, column = tools(it)
                dve.tensor_tensor_scan(flat(LW), cst(A, "scan"), D8[:, it, :], 0.0, ALU.mult,
                                       ALU.add).then_inc(sem("lw"), 1)
                wait("lw")
                dve.tensor_tensor(flat(E0), flat(LW), D8[:, it, :], ALU.subtract).then_inc(sem("lwx"), 1)
                dve.tensor_scalar(flat(KM), A8[:, it, :], -1.0, column(KA), ALU.add, ALU.mult).then_inc(sem("kmt"), 1)
                dve.tensor_tensor(Bf, eight(KN8), eight(A8), ALU.mult).then_inc(sem("bh_in"), 1)
                wait("kmt")
                dve.scalar_tensor_tensor(flat(KM), flat(KM), 1.0, K8[:, it, :], ALU.add,
                                         ALU.mult).then_inc(sem("km"), 1)
                wait("bh_in")
                wait("e2")
                mul(Bf, Bf, E2, "bh")
                wait("km")
                mul(Kf, KM, E2, "kh")
                wait("e1")
                mul(AR[:, 1], eight(R8), E1, "rh")
                wait("e0")
                dve.scalar_tensor_tensor(AR[:, 0], eight(KN8), -1.0, E0, ALU.mult,
                                         ALU.mult).then_inc(sem("ah"), 1)

            def turn(it, last):
                wait, mul, add, eight, column = tools(it)
                wait("kh")
                wait("bh")
                dve.scalar_tensor_tensor(flat(E2), R8[:, it, :], column(RKP), flat(KM),
                                         ALU.mult, ALU.mult).then_inc(sem("rk_in"), 1)
                mul(Bc, Bf, W_LAST, "bc")
                mul(Kc, Kf, W_LAST, "kc")

                def masked(dst, src, name):
                    for f in range(2):
                        for c in range(2):
                            out = dst[f][rows(c), :, c * C:(c + 1) * C].rearrange("p (m s) n -> p s m n", s=2)
                            last = dve.tensor_tensor(out, src[rows(c), :, 2 * f:2 * f + 2],
                                                     cst(A, name)[rows(c)].unsqueeze(1).unsqueeze(1).to_broadcast([C, 2, 2, C]),
                                                     ALU.mult)
                    return last

                wait("p_nrb")
                masked(N1, duo(0)[:, :, :, 0, :], "u_d").then_inc(sem("n_out"), 1)
                masked(N64, duo(0)[:, :, :, 0, :], "u_64")
                mul(halves(RB), duo(0)[:, :, :, 1, :], bc3(cst(A, "u_le")), "nrb_out")
                wait("p_l")
                masked(L1, split(2), "l_d").then_inc(sem("l_out"), 1)
                masked(L32, split(2), "l_32").then_inc(sem("l32_out"), 1)
                wait("n_out")
                for f in range(2):
                    add(Z[f], N1[f], cst(A, "ident").unsqueeze(1).to_broadcast([P, 4, P]), f"z1{f}")
                wait("bonus_sum")
                wait("v_in")
                dve.tensor_tensor(V8[:, it, :], PS[:, 6, :], V8[:, it, :], ALU.mult).then_inc(sem("bonus"), 1)
                wait("p_mrk")
                masked(MT, duo(4)[:, :, :, 0, :], "u_lt")
                mul(halves(RK), duo(4)[:, :, :, 1, :], bc3(cst(A, "u_le")), "mrk_out")
                for power in ("2", "4"):
                    for f in range(2):
                        wait(f"p_n{power}{f}")
                        dve.tensor_copy({"2": N2, "4": N4}[power][f], squares(2 + f)).then_inc(sem(f"n{power}{f}"), 1)
                        wait(f"p_z{power}{f}")
                        add(Z[f], Z[f], squares(6 + f), f"z{power}{f}")
                for step in ("8", "16"):
                    for f in range(2):
                        wait(f"p_z{step}{f}")
                        add(Z[f], Z[f], squares(6 + f), f"z{step}{f}")
                for f in range(2):
                    wait(f"p_gh{f}")
                    add(part(GH, f), part(GH, f), part(wide(6), f), f"gh{f}")
                mul(DG, bc(cst(A, "ident64")), W_LAST, "dg")
                wait("p_r2")
                add(halves(eight(R8)), halves(AR[:, 1]), split(2), "r2")
                if not last:
                    decayed(it + 1)
                wait("dg")
                wait("p_p")
                add(halves(eight(D8)), halves(DG), split(6), "pp")

            decayed(0)
            for x in (N1, L1, L32, N64, MT):
                for f in range(2):
                    for c in range(2):
                        dve.memset(x[f][rows(c), :, (1 - c) * C:(2 - c) * C], 0.0)
            with dve.Fori(0, 7) as it:
                turn(it, False)
            turn(7, True)

        @block.tensor
        def _(pe):
            with pe.Fori(0, 8) as it:
                def wait(n):
                    pe.wait_ge(sem(n), it + 1)

                def before(n):
                    pe.wait_ge(sem(n), it + 1)

                def started():
                    pe.sem_inc(sem("begun"), 1)

                def product(out, lhs, rhs):
                    for i in range(4):
                        last = pe.matmul(out[:, i], lhs[:, i], rhs[:, i], start=True, stop=True)
                    return last

                def turn(out_bank, src, done):
                    for m in range(4):
                        last = pe.transpose(dual(out_bank, m), src[:, 2 * m:2 * m + 2, :], cst(A, "ident"))
                    last.then_inc(sem(done), 1)

                before("pp")
                wait("v_in")
                for m in range(4):
                    last = pe.transpose(dual(6, m), V_IN[:, 2 * m:2 * m + 2, :], cst(A, "ident"))
                last.then_inc(sem("t_v"), 1)
                wait("bc")
                turn(7, Bc, "t_b")
                wait("kc")
                before("r2")
                turn(2, Kc, "t_k")
                wait("ah")
                for m in range(4):
                    last = pe.transpose(dual(3, m), AR[:, 0, 2 * m:2 * m + 2, :], cst(A, "ident"))
                last.then_inc(sem("t_a"), 1)
                wait("bh")
                wait("rh")
                before("qq")
                started()
                for m, h, c in units:
                    last = pe.matmul(duo(0)[rows(c), h, m, :, :], Bf[rows(h), 2 * m + c, :],
                                     AR[rows(h), :, 2 * m + c, :], start=True, stop=True)
                last.then_inc(sem("p_nrb"), 1)
                wait("k_out")
                wait("a_out")
                started()
                for m, h, c in units:
                    last = pe.matmul(split(2)[rows(c), h, m, :], AR[rows(h), 0, 2 * m + c, :],
                                     Bf[rows(h), 2 * m + c, :], start=True, stop=True)
                last.then_inc(sem("p_l"), 1)
                wait("kh")
                before("y0")
                started()
                for m, h, c in units:
                    last = pe.matmul(duo(4)[rows(c), h, m, :, :], Kf[rows(h), 2 * m + c, :],
                                     AR[rows(h), :, 2 * m + c, :], start=True, stop=True)
                last.then_inc(sem("p_mrk"), 1)
                wait("v_out")
                wait("rk_in")
                pe.matmul(PS[:, 6, :], cst(A, "blockones"), flat(E2), start=True, stop=True).then_inc(sem("bonus_sum"), 1)
                wait("nrb_out")
                wait("l32_out")
                for f in range(2):
                    product(squares(f), N1[f], L1[f]).then_inc(sem(f"p_l2{f}"), 1)
                    product(squares(2 + f), L1[f], N1[f]).then_inc(sem(f"p_n2{f}"), 1)
                wait("mrk_out")
                for f in range(2):
                    last = product(part(bank(5), f), MT[f], part(Vt, f))
                last.then_inc(sem("p_mv"), 1)
                wait("b_out")
                wait("bonus")
                for f in range(2):
                    wait(f"z1{f}")
                    wait(f"l2{f}")
                    product(squares(6 + f), L2[f], Z[f]).then_inc(sem(f"p_z2{f}"), 1)
                    wait(f"n2{f}")
                    product(squares(f), N2[f], L2[f]).then_inc(sem(f"p_l4{f}"), 1)
                    product(squares(2 + f), L2[f], N2[f]).then_inc(sem(f"p_n4{f}"), 1)
                for f in range(2):
                    wait(f"z2{f}")
                    wait(f"l4{f}")
                    product(squares(6 + f), L4[f], Z[f]).then_inc(sem(f"p_z4{f}"), 1)
                    wait(f"n4{f}")
                    product(squares(f), N4[f], L4[f]).then_inc(sem(f"p_l8{f}"), 1)
                for f in range(2):
                    wait(f"z4{f}")
                    wait(f"l8{f}")
                    product(squares(6 + f), L8[f], Z[f]).then_inc(sem(f"p_z8{f}"), 1)
                for f in range(2):
                    wait(f"z8{f}")
                    started()
                    product(squares(f), L32[f], Z[f])
                    for i in range(4):
                        last = pe.transpose(squares(2 + f)[:, i], Z[f][:, i], cst(A, "ident"))
                    last.then_inc(sem(f"p_xt{f}"), 1)
                for f in range(2):
                    wait(f"x{f}")
                    wait(f"tt{f}")
                    product(squares(6 + f), TT[f], X[f]).then_inc(sem(f"p_z16{f}"), 1)
                wait("mv")
                for f in range(2):
                    wait(f"z16{f}")
                    product(part(wide(0), f), Z[f], part(AMV, f)).then_inc(sem(f"p_g1{f}"), 1)
                for f in range(2):
                    wait(f"g1{f}")
                    product(part(wide(0), f), N64[f], part(GH, f)).then_inc(sem(f"p_g2{f}"), 1)
                for f in range(2):
                    wait(f"g2{f}")
                    product(part(wide(6), f), Z[f], G2[f]).then_inc(sem(f"p_gh{f}"), 1)
                for f in range(2):
                    wait(f"gh{f}")
                    started()
                    for m, h, c in units[8 * f:8 * f + 8]:
                        last = pe.matmul(split(2)[rows(h), c, m, :], GH[rows(c), 2 * m + h, 0, :],
                                         RB[rows(c), 2 * m + h, :], start=True, stop=True)
                last.then_inc(sem("p_r2"), 1)
                started()
                for m, h, c in units:
                    pe.matmul(split(4)[rows(h), c, m, :], GH[rows(c), 2 * m + h, 1, :],
                              RB[rows(c), 2 * m + h, :], start=True, stop=False)
                    last = pe.matmul(split(4)[rows(h), c, m, :], Vt[rows(c), 2 * m + h, :],
                                     RK[rows(c), 2 * m + h, :], start=False, stop=True)
                last.then_inc(sem("p_y0"), 1)
                started()
                for m, h, c in units:
                    last = pe.matmul(split(6)[rows(h), c, m, :], GH[rows(c), 2 * m + h, 0, :],
                                     Bt[rows(c), 2 * m + h, :], start=True, stop=True)
                last.then_inc(sem("p_p"), 1)
                started()
                for m, h, c in units:
                    pe.matmul(split(0)[rows(h), c, m, :], Bt[rows(c), 2 * m + h, :],
                              GH[rows(c), 2 * m + h, 1, :], start=True, stop=False)
                    last = pe.matmul(split(0)[rows(h), c, m, :], Kt[rows(c), 2 * m + h, :],
                                     Vt[rows(c), 2 * m + h, :], start=False, stop=True)
                last.then_inc(sem("p_q"), 1)


def rwkv_scan(nc, A, NV, PS, RJ, DEC, AA):
    S = NV.at(4 * 1024, 2, PAIRS, C)
    chunk = lambda x, n: x[:, 0:PAIRS, n * C:(n + 1) * C]
    with (nc.semaphore("s_moved") as moved, nc.semaphore("s_state") as state, nc.semaphore("s_read") as read,
          nc.semaphore("s_y") as y_done, nc.Block() as block):
        @block.tensor
        def _(pe):
            for n in range(NCH):
                pe.wait_ge(state, n + 1)
                P_, R_ = chunk(DEC, n), chunk(RJ.first, n)
                if n < NCH - 1:
                    for j in range(PAIRS):
                        for h in range(2):
                            r = slice(64 * h, 64 * h + 64)
                            last = pe.matmul(PS[r, n % 2, j * C:(j + 1) * C], P_[r, j, :], S[r, n % 2, j, :],
                                             start=True, stop=True)
                    last.then_inc(moved, 1)
                if n >= 2:
                    pe.wait_ge(y_done, n - 1)
                for j in range(PAIRS):
                    for h in range(2):
                        r = slice(64 * h, 64 * h + 64)
                        last = pe.matmul(PS[r, 2 + n % 2, j * C:(j + 1) * C], S[r, n % 2, j, :], R_[r, j, :],
                                         start=True, stop=True)
                last.then_inc(read, 1)

        @block.vector
        def _(dve):
            dve.memset(S[:, 0], 0.0).then_inc(state, 1)

            def out(n):
                dve.wait_ge(read, n + 1)
                y0 = chunk(RJ.first[:, 4:8, :], n)
                dve.tensor_tensor(y0, y0, PS[:, 2 + n % 2, 0:PAIRS * C].rearrange("p (a b) -> p a b", b=C),
                                  ALU.add).then_inc(y_done, 1)

            for n in range(NCH):
                if n < NCH - 1:
                    dve.wait_ge(moved, n + 1)
                    if n >= 1:
                        dve.wait_ge(read, n)
                    dve.tensor_tensor(S[:, (n + 1) % 2], PS[:, n % 2, 0:PAIRS * C].rearrange("p (a b) -> p a b", b=C),
                                      chunk(AA, n), ALU.add).then_inc(state, 1)
                out(n)


def rwkv_out(nc, A, NV, PS, RJ, g_in):
    GUP = NV.at(O_VT, HALF)
    W = NV.at(4 * 1024, 8, HALF)
    with ExitStack() as ctx:
        sem = ctx.enter_context(cleared_semaphores(nc, "g_"))
        loaded, mean, centred, squared, var, root, inverse, gate, out, step = (
            sem(x) for x in ("loaded", "mean", "centred", "squared", "var", "root", "inverse", "gate", "out", "step"))
        block = ctx.enter_context(nc.Block())
        units = [(j, slice(h * HALF, (h + 1) * HALF)) for j in range(PAIRS) for h in range(2)]

        @block.sync
        def _(sp):
            sp.dma_start(GUP, g_in).then_inc(loaded, 16)

        @block.tensor
        def _(pe):
            pe.wait_ge(loaded, 16)
            for n in range(len(units) + 1):
                if n < len(units):
                    j, cols = units[n]
                    if n >= 2:
                        pe.wait_ge(centred, n - 1)
                    pe.matmul(PS[:, n % 2, :], cst(A, "blockones"), RJ[:, 4 + j, cols], start=True, stop=True).then_inc(mean, 1)
                if n >= 1:
                    k = n - 1
                    j, cols = units[k]
                    pe.wait_ge(squared, k + 1)
                    if k >= 2:
                        pe.wait_ge(root, k - 1)
                        pe.wait_ge(out, k - 1)
                    pe.matmul(PS[:, 2 + k % 2, :], cst(A, "blockones"), W[:, k % 2, :], start=True, stop=True).then_inc(var, 1)
                    pe.matmul(PS[:, 4 + k % 2, :], GUP[:, j * P:(j + 1) * P], RJ[:, 13, cols], start=True,
                              stop=True).then_inc(gate, 1)

        @block.scalar
        def _(act):
            for n, (j, cols) in enumerate(units):
                act.wait_ge(centred, n + 1)
                if n >= 2:
                    act.wait_ge(var, n - 1)
                act.activation(W[:, n % 2, :], RJ[:, 4 + j, cols], ACT.Square).then_inc(squared, 1)
                act.wait_ge(var, n + 1)
                if n >= 2:
                    act.wait_ge(out, n - 1)
                act.activation(W[:, 2 + n % 2, :], PS[:, 2 + n % 2, :], ACT.Sqrt, scale=1.0 / HD,
                               bias=cst(A, "gneps")).then_inc(root, 1)

        @block.vector
        def _(dve):
            def centre(n):
                j, cols = units[n]
                dve.wait_ge(mean, n + 1)
                dve.scalar_tensor_tensor(RJ[:, 4 + j, cols], PS[:, n % 2, :], -1.0 / HD, RJ[:, 4 + j, cols],
                                         ALU.mult, ALU.add).then_inc(centred, 1)

            centre(0)
            for n, (j, cols) in enumerate(units):
                if n + 1 < len(units):
                    centre(n + 1)
                dve.wait_ge(root, n + 1)
                R = W[:, 2 + n % 2, :]
                Y = RJ[:, 4 + j, cols]
                dve.reciprocal(R, R).then_inc(inverse, 1)
                dve.wait_ge(inverse, n + 1)
                dve.scalar_tensor_tensor(Y, Y, par(A, LNW + j), R, ALU.mult, ALU.mult).then_inc(step, 1)
                dve.wait_ge(step, 2 * n + 1)
                dve.scalar_tensor_tensor(Y, Y, par(A, LNB + j), RJ[:, 8 + j, cols], ALU.add, ALU.add).then_inc(step, 1)
                dve.wait_ge(step, 2 * n + 2)
                dve.wait_ge(gate, n + 1)
                dve.tensor_tensor(Y, Y, PS[:, 4 + n % 2, :], ALU.mult).then_inc(out, 1)


def merge(nc, A, PS, weights, pairs, gates, Y, M, GT, TMP):
    first, end = pairs
    n_pairs = end - first
    with ExitStack() as ctx:
        sem = ctx.enter_context(cleared_semaphores(nc, "e_"))
        split, product = weights.split, weights.product
        gate = [sem("gate0"), sem("gate1")]
        part = [sem("part0"), sem("part1")]
        merged = [sem("merged0"), sem("merged1")]
        hi = [sem("hi0"), sem("hi1")]
        free = [sem("free0"), sem("free1")]
        block = ctx.enter_context(nc.Block())

        @block.sync
        def _(sp):
            weights.load_rest(sp, first, end)

        @block.gpsimd
        def _(pool):
            weights.split_all(pool, first, end)

        @block.scalar
        def _(act):
            g2 = gates.rearrange("(x n) p t -> n x p t", x=2)

            def load(n, s):
                act.dma_start(GT[:, s], g2[n].rearrange("x p t -> p x t")).then_inc(gate[s], 16)

            def round_m(i):
                for s in range(2):
                    for h in range(2):
                        act.wait_ge(merged[s], 2 * i + h + 1)
                        act.activation(hi_of(M)[:, 2 * i + s, HALVES[h]], TMP[:, s, HALVES[h]], ACT.Copy).then_inc(hi[s], 1)

            for s in range(2):
                load(s, s)
            with act.Fori(1, n_pairs) as i:
                round_m(i - 1)
                for s in range(2):
                    act.wait_ge(free[s], 2 * i + 1)
                    load(2 * i + s, s)
            round_m(n_pairs - 1)

        @block.tensor
        def _(pe):
            with pe.Fori(0, n_pairs) as i:
                for s in range(2):
                    pe.wait_ge(split[s], first + i + 1)
                    pe.wait_ge(free[s], 2 * i + 1)
                    for h in range(2):
                        for x in range(2):
                            out = PS[:, 4 * s + 2 * h + x, :]
                            W = weights.W
                            for c in range(PAIRS * x, PAIRS * x + PAIRS):
                                pe.matmul(out, W[:, s, 0, c, :], hi_of(Y)[:, c, HALVES[h]], start=c == PAIRS * x, stop=False)
                                pe.matmul(out, W[:, s, 0, c, :], lo_of(Y)[:, c, HALVES[h]], start=False, stop=False)
                                last = pe.matmul(out, W[:, s, 1, c, :], hi_of(Y)[:, c, HALVES[h]], start=False,
                                                 stop=c == PAIRS * x + PAIRS - 1)
                        last.then_inc(product[s], 1)

        @block.vector
        def _(dve):
            for s in range(2):
                dve.sem_inc(free[s], 1)
            with dve.Fori(0, n_pairs) as i:
                for s in range(2):
                    dve.wait_ge(gate[s], 16 * i + 16)
                    for h in range(2):
                        dve.wait_ge(product[s], 2 * (first + i) + h + 1)
                        for x in range(2):
                            dve.scalar_tensor_tensor(GT[:, s, x, HALVES[h]], GT[:, s, x, HALVES[h]], 1.0,
                                                     PS[:, 4 * s + 2 * h + x, :], ALU.add, ALU.mult).then_inc(part[s], 1)
                        dve.wait_ge(part[s], 4 * i + 2 * h + 2)
                        dve.tensor_tensor(TMP[:, s, HALVES[h]], GT[:, s, 0, HALVES[h]], GT[:, s, 1, HALVES[h]],
                                          ALU.add).then_inc(merged[s], 1)
                        dve.wait_ge(merged[s], 2 * i + h + 1)
                        dve.wait_ge(hi[s], 2 * i + h + 1)
                        dve.tensor_tensor(lo_of(M)[:, 2 * i + s, HALVES[h]], TMP[:, s, HALVES[h]],
                                          hi_of(M)[:, 2 * i + s, HALVES[h]].bitcast(F32), ALU.subtract).then_inc(free[s], 1)


def split_branches(nc, sources, Y, weights):
    with nc.semaphore("y_hi") as hi, nc.Block() as block:
        @block.sync
        def _(sp):
            weights.load_first(sp)

        @block.scalar
        def _(act):
            for c, x in enumerate(sources):
                act.activation(hi_of(Y)[:, c, :], x, ACT.Copy).then_inc(hi, 1)

        @block.vector
        def _(dve):
            for c, x in enumerate(sources):
                dve.wait_ge(hi, c + 1)
                dve.tensor_tensor(lo_of(Y)[:, c, :], x, hi_of(Y)[:, c, :].bitcast(F32), ALU.subtract)


def project_out(nc, A, PS, weights, pairs, x_in, M, X, H, SQ, SUM):
    first, end = pairs
    n_pairs = end - first
    with ExitStack() as ctx:
        sem = ctx.enter_context(cleared_semaphores(nc, "o_"))
        split, product = weights.split, weights.product
        added = [sem("added0"), sem("added1")]
        x_loaded, hi, squared, lo = sem("x"), sem("hi"), sem("squared"), sem("lo")
        block = ctx.enter_context(nc.Block())

        @block.sync
        def _(sp):
            weights.load_rest(sp, first, end)

        @block.gpsimd
        def _(pool):
            weights.split_all(pool, first, end)

        @block.tensor
        def _(pe):
            with pe.Fori(0, n_pairs) as i:
                for s in range(2):
                    pe.wait_ge(split[s], first + i + 1)
                    for h in range(2):
                        pe.wait_ge(added[s], 2 * i + 1)
                        three_passes(pe, PS[:, 2 * s + h, :], weights.W, s, M, HALVES[h]).then_inc(product[s], 1)

        @block.scalar
        def _(act):
            act.dma_start(X, x_in.rearrange("(c p) t -> p c t", p=P)).then_inc(x_loaded, 16)
            with act.Fori(0, n_pairs) as i:
                for s in range(2):
                    act.wait_ge(added[s], 2 * i + 3)
                    act.activation(hi_of(H)[:, 2 * i + s, :], X[:, 2 * i + s, :], ACT.Copy,
                                   scale=A.at(O_PAR + FFNN, KC)[:, bass.ds(2 * i + s, 1)]).then_inc(hi, 1)
                    act.activation(SQ, X[:, 2 * i + s, :], ACT.Square).then_inc(squared, 1)

        @block.vector
        def _(dve):
            dve.memset(SUM, 0.0).then_inc(lo, 1)
            dve.wait_ge(x_loaded, 16)
            for s in range(2):
                dve.sem_inc(added[s], 1)
            with dve.Fori(0, n_pairs) as i:
                for s in range(2):
                    for h in range(2):
                        dve.wait_ge(product[s], 2 * (first + i) + h + 1)
                        dve.scalar_tensor_tensor(X[:, 2 * i + s, HALVES[h]], PS[:, 2 * s + h, :], 0.5,
                                                 X[:, 2 * i + s, HALVES[h]], ALU.mult, ALU.add).then_inc(added[s], 1)
                    dve.wait_ge(hi, 2 * i + s + 1)
                    dve.scalar_tensor_tensor(lo_of(H)[:, 2 * i + s, :], X[:, 2 * i + s, :],
                                             A.at(O_PAR + FFNN, KC)[:, bass.ds(2 * i + s, 1)],
                                             hi_of(H)[:, 2 * i + s, :].bitcast(F32), ALU.mult, ALU.subtract)
                    dve.wait_ge(squared, 2 * i + s + 1)
                    dve.wait_ge(lo, 2 * i + s + 1)
                    dve.tensor_tensor(SUM, SUM, SQ, ALU.add).then_inc(lo, 1)


def mlp(nc, A, PS, weights, pairs, H, F, X, TMP, R, SUM, out):
    GROUPS = DFF // 1024
    first, end = pairs
    RSTD = A.at(O_RSTD, 1024)
    with ExitStack() as ctx:
        sem = ctx.enter_context(cleared_semaphores(nc, "p_"))
        split, product = weights.split, weights.product
        summed, rms, rs = sem("summed"), sem("rms"), sem("rs")
        scaled = [sem("scaled0"), sem("scaled1")]
        square = [sem("square0"), sem("square1")]
        hi = [sem("hi0"), sem("hi1")]
        inner = [sem("inner0"), sem("inner1")]
        added = [sem("added0"), sem("added1")]
        stored = [sem("stored0"), sem("stored1")]
        begun = sem("begun")
        block = ctx.enter_context(nc.Block())

        @block.sync
        def _(sp):
            weights.load_rest(sp, first, end)
            for n in range(KC):
                sp.wait_ge(added[n % 2], 8 * (GROUPS - 1) + 2 * (n // 2) + 3)
                sp.dma_start(out[n * P:(n + 1) * P, :], X[:, n, :]).then_inc(stored[n % 2], 16)
            for s in range(2):
                sp.wait_ge(stored[s], 16 * KC // 2)

        @block.gpsimd
        def _(pool):
            weights.split_all(pool, first, end)

        @block.tensor
        def _(pe):
            for h in range(2):
                last = pe.matmul(PS[:, 4 + h, :], cst(A, "ones"), SUM[:, HALVES[h]], start=True, stop=True)
            last.then_inc(summed, 1)

            def tile(s, src, n, free):
                pe.wait_ge(split[s], first + n + 1)
                for h in range(2):
                    for sem_, count in free:
                        pe.wait_ge(sem_, count)
                    three_passes(pe, PS[:, 2 * s + h, :], weights.W, s, src, HALVES[h]).then_inc(product[s], 1)

            with pe.Fori(0, GROUPS) as g:
                with pe.Fori(0, 4) as i:
                    for s in range(2):
                        tile(s, H, 8 * g + i, [(inner[s], 8 * g + 2 * i + 1), (added[s], 8 * g + 1)])
                for s in range(2):
                    pe.wait_ge(inner[s], 8 * g + 9)
                pe.sem_inc(begun, 1)
                with pe.Fori(0, 4) as i:
                    for s in range(2):
                        tile(s, F, 8 * g + 4 + i, [(added[s], 8 * g + 2 * i + 1)])

        @block.scalar
        def _(act):
            act.wait_ge(summed, 1)
            act.activation(RSTD, PS[:, 4:6, :], ACT.Sqrt, scale=1.0 / D, bias=cst(A, "eps")).then_inc(rms, 1)
            with act.Fori(0, GROUPS) as g:
                with act.Fori(0, 4) as i:
                    for s in range(2):
                        for h in range(2):
                            act.wait_ge(square[s], 8 * g + 2 * i + h + 1)
                            act.activation(hi_of(F)[:, 2 * i + s, HALVES[h]], R[:, h, :], ACT.Copy).then_inc(hi[s], 1)

        @block.vector
        def _(dve):
            for s in range(2):
                dve.sem_inc(inner[s], 1)
                dve.sem_inc(added[s], 1)
            dve.wait_ge(rms, 1)
            dve.reciprocal(RSTD, RSTD).then_inc(rs, 1)
            dve.wait_ge(rs, 1)
            with dve.Fori(0, GROUPS) as g:
                with dve.Fori(0, 4) as i:
                    for s in range(2):
                        for h in range(2):
                            dve.wait_ge(product[s], 2 * first + 16 * g + 2 * i + h + 1)
                            dve.tensor_tensor(TMP[:, h, :], PS[:, 2 * s + h, :], RSTD[:, HALVES[h]],
                                              ALU.mult).then_inc(scaled[s], 1)
                            dve.wait_ge(scaled[s], 8 * g + 2 * i + h + 1)
                            dve.scalar_tensor_tensor(R[:, h, :], TMP[:, h, :], 0.0, TMP[:, h, :], ALU.max,
                                                     ALU.mult).then_inc(square[s], 1)
                            dve.wait_ge(hi[s], 8 * g + 2 * i + h + 1)
                            dve.tensor_tensor(lo_of(F)[:, 2 * i + s, HALVES[h]], R[:, h, :],
                                              hi_of(F)[:, 2 * i + s, HALVES[h]].bitcast(F32),
                                              ALU.subtract).then_inc(inner[s], 1)
                with dve.Fori(0, 4) as i:
                    for s in range(2):
                        for h in range(2):
                            dve.wait_ge(product[s], 2 * first + 16 * g + 8 + 2 * i + h + 1)
                            dve.tensor_tensor(X[:, 2 * i + s, HALVES[h]], PS[:, 2 * s + h, :], X[:, 2 * i + s, HALVES[h]],
                                              ALU.add).then_inc(added[s], 1)


class Tiles:

    def __init__(self, first, second):
        self.first, self.second = first, second

    def __getitem__(self, key):
        rows, i, *rest = key
        part, i = (self.first, i) if i < 8 else (self.second, i - 8)
        return part[(rows, i, *rest)]


def layer(nc, x, cst_in, par_in, w_first, w_tok, w1, w2, pos, lora, g_up, w_last, out):
    gates = nc.dram_tensor("gates", (2 * KC, P, T), F32, kind="Internal").ap()

    def sb(ctx, name, n, dt=F32, side="left"):
        return ctx.enter_context(nc.sbuf_tensor(name, [P, n], dt, side=side))

    def split_pair(ctx, name, side="left"):
        n = 8
        return sb(ctx, name, 2 * n * 1024, F32R, side)[:, :].rearrange("p (x c n) -> p x c n", x=2, c=n)

    def weight_slots(ctx, tag, n, side="left"):
        raw_all = sb(ctx, tag + "raw", n // 2, F32, side)
        raw = raw_all[:, 0:2048].rearrange("p (s c n) -> p s c n", s=2, c=KC)
        W = sb(ctx, tag + "split", n, F32R, side)
        return raw_all, raw, W, W[:, 0:4096].rearrange("p (s x c n) -> p s x c n", s=2, x=2, c=KC)

    with ExitStack() as whole:
        A = Arena(sb(whole, "base", BASE))
        first = sb(whole, "tiles_rk", 8 * 1024)[:, :].rearrange("p (c n) -> p c n", c=8)
        PS = whole.enter_context(nc.psum_tensor("psum", [P, 8, HALF], F32))
        mixing, y_space, last = ExitStack(), ExitStack(), ExitStack()
        second = sb(mixing, "tiles_v", 6 * 1024)[:, :].rearrange("p (c n) -> p c n", c=6)
        NV = Arena(sb(mixing, "attn_tiles", 8 * 1024 + 8 * TOKC))
        RJ = Tiles(first, second)
        NSA = NV.at(0, 8, 1024)
        VT = NV.at(O_VT, 8, TOKC)
        with ExitStack() as phase:
            U = split_pair(phase, "u")
            raw_all, raw, W_all, W = weight_slots(phase, "a", 2 * KC * TOKC)
            SQ = NSA[:, 0:2, :]
            SUM = NSA[:, 2, :]
            norm_and_project(nc, A, PS, x, cst_in, par_in, w_first, gates, first, SQ, SUM, U, raw, W, NSA, RJ)
            project_tokens(nc, A, PS, w_tok, VT, U, raw_all[:, :].rearrange("p (c n) -> p c n", c=KC),
                           W_all[:, :].rearrange("p (x c n) -> p x c n", x=2, c=KC))
        with ExitStack() as phase:
            WK = Arena(sb(phase, "work", WORK))
            KPAD = WK.at(0, 4, 1024)
            KPC = WK.at(22232, 2, NCMP)
            VC = WK.at(22232 + 2 * NCMP, 2, HD)
            compress(nc, A, WK, PS, NSA, KPAD, KPC, VC, w1, w2, pos)
            attention(nc, A, WK, PS, NSA, KPAD, KPC, VT, VC, RJ)
            DEC = WK.at(0, PAIRS, 1024)
            AA = WK.at(4096, PAIRS, 1024)
            KN = WK.at(8192, PAIRS, 1024)
            decay_and_keys(nc, A, NV, WK, PS, RJ, DEC, AA, KN, lora)
            rwkv_chunks(nc, A, NV, WK, PS, RJ, DEC, AA, KN)
            rwkv_scan(nc, A, NV, PS, RJ, DEC, AA)
            rwkv_out(nc, A, NV, PS, RJ, g_up)
        _, raw, _, W = weight_slots(last, "b", 4096, "right")
        sem = whole.enter_context(cleared_semaphores(nc, "w_"))
        weights = Weights(sem, w_last, raw, W)
        Y = split_pair(y_space, "ysplit", "right")
        split_branches(nc, [NSA[:, j, :] for j in range(PAIRS)] + [first[:, 4 + j, :] for j in range(PAIRS)], Y, weights)
        mixing.close()
        with ExitStack() as out_space:
            M = split_pair(out_space, "msplit")
            merge(nc, A, PS, weights, (0, 4), gates, Y, M, first[:, 0:4, :].rearrange("p (s x) n -> p s x n", s=2),
                  first[:, 4:6, :])
            y_space.close()
            H = split_pair(last, "h", "right")
            SQ = sb(out_space, "squares", 1024)[:, :]
            SUM = A.at(O_RSTD, 1024)
            project_out(nc, A, PS, weights, (4, 8), x, M, first, H, SQ, SUM)
        f_space = whole.enter_context(ExitStack())
        F = split_pair(f_space, "f")
        R = Arena(sb(f_space, "relu", 2048))
        mlp(nc, A, PS, weights, (8, 40), H, F, first, R.at(0, 2, HALF), R.at(1024, 2, HALF), SUM, out)
        last.close()


def tiles(w):
    k, n = w.shape
    return np.ascontiguousarray(w.reshape(k // P, P, n // P, P).transpose(2, 1, 0, 3).reshape(n // P, P, -1))


def cols(v):
    return np.asarray(v).reshape(-1, P).T


def host_layout(x, mix_norm, w_in, q_gain, k_gain, cmp_pos, cmp_w1, cmp_w2, w_attn_branch, tok_mix, w0, w_lora_up,
                a0, a_lora_up, g_lora_up, k_k, k_a, r_k, ln_x_w, ln_x_b, w_rwkv_branch, w_out, ffn_norm,
                w_ffn_up, w_ffn_down):
    W = np.asarray(w_in)[0]
    q = [np.concatenate([W[:, HD * j:HD * j + HD], W[:, HD * (j + 4):HD * (j + 4) + HD]], 1) for j in range(PAIRS)]
    kc, vc, ks, vs, kw, vw = (W[:, 512 + P * i:640 + P * i] for i in range(6))
    gates = W[:, 1280:1304]
    wa = np.asarray(w_attn_branch[0]).reshape(2, PAIRS, HD, D).transpose(1, 0, 2, 3).reshape(-1, D)
    two = lambda v: np.concatenate([v, v])
    twice = lambda v: np.repeat(cols(v), 2, axis=1)
    params = np.concatenate([
        cols(mix_norm[0]), cols(ffn_norm[0]), cols(two(q_gain[0])), *(cols(two(k_gain[0, i])) for i in range(3)),
        cols(tok_mix[0]), cols(w0[0]), cols(a0[0]), twice(k_k[0]), twice(k_a[0]), twice(r_k[0].reshape(-1)),
        cols(ln_x_w[0]), cols(ln_x_b[0])], 1)
    wtok = np.concatenate([vs, vw, gates], 1)
    c = np.ascontiguousarray
    return {
        "x": c(x[0].T), "cst": constants(), "par": c(params),
        "w_first": tiles(np.concatenate([W[:, -2 * D:]] + q + [ks, kw, kc, vc] + [
            W[:, NSA_COLS:NSA_COLS + RW_TILES * P]], 1)),
        "w_tok": c(wtok.reshape(KC, P, TOKC).transpose(1, 0, 2).reshape(P, -1)),
        "w1": c(cmp_w1[0].reshape(2, 2, 16, HD, CMP_HID).transpose(1, 3, 0, 2, 4).reshape(P, 2, 16, CMP_HID)),
        "w2": c(cmp_w2[0].transpose(1, 0, 2)),
        "pos": c(cmp_pos[0].transpose(2, 0, 1)),
        "lora": c(np.concatenate([w_lora_up[0], a_lora_up[0]], 0)), "g_up": c(g_lora_up[0]),
        "w_last": np.concatenate([np.concatenate([tiles(wa), tiles(w_rwkv_branch[0])], 2), tiles(w_out[0])] + [
            x for g in range(4) for x in (tiles(w_ffn_up[0][:, 1024 * g:1024 * g + 1024]),
                                          tiles(w_ffn_down[0][1024 * g:1024 * g + 1024]))]),
    }


def kernel(**inputs):
    import concourse.bacc as bacc
    from concourse.bass_utils import run_bass_kernel_spmd

    nc = bacc.Bacc("TRN2", target_bir_lowering=False, num_devices=1)
    arrays = host_layout(**{k: np.asarray(v) for k, v in inputs.items()})
    args = [nc.dram_tensor(n, a.shape, mybir.dt.from_np(a.dtype), kind="ExternalInput").ap() for n, a in arrays.items()]
    out = nc.dram_tensor("out", (D, T), F32, kind="ExternalOutput").ap()
    layer(nc, *args, out)
    r = run_bass_kernel_spmd(nc, [arrays], core_ids=[0])
    return np.ascontiguousarray(r.results[0]["out"].T)[None]
```
